# Optimizing a Trainium2 kernel written in Bass

```python
import math
import jax, jax.numpy as jnp
from jax import lax
import numpy as np

D_MODEL = 1024
BATCH = 1
SEQ = 512
DEPTH = 1
DEC_BATCH = 8
DEC_SEQ = 4
PAST_LEN = 2048
PAGE_SIZE = 128

HEAD_DIM = 64
POOL_WINDOWS = (2, 4, 8, 16)
POOL_GROUP = D_MODEL // 16
POOL_WIDTH = POOL_GROUP * len(POOL_WINDOWS)
POOL_BUF = max(POOL_WINDOWS) - 1
NSA_HEADS = D_MODEL // 128
NSA_KV_HEADS = 2
NSA_HPG = NSA_HEADS // NSA_KV_HEADS
NSA_WIDTH = NSA_HEADS * HEAD_DIM
KV_WIDTH = 2 * NSA_KV_HEADS * HEAD_DIM
CMP_BLOCK = 32
CMP_STRIDE = 16
SLC_BLOCK = 64
SLC_TOPK = 16
WINDOW = 512
SEL_Q_BLOCK = 32
WIN_Q_BLOCK = 128
MEM_TOKENS = 256
MEM_HEADS = 4
MEM_WIDTH = MEM_HEADS * HEAD_DIM
NUM_BUCKETS = 32
MAX_DISTANCE = 128
N_EXPERTS = 32
TOP_K = 4
D_FF = D_MODEL
SWIGLU_ALPHA = 1.702
SWIGLU_LIMIT = 7.0
MOE_BLOCK = 64
N_BRANCH = 3
EPS = 1e-6
IN_SPLITS = (POOL_WIDTH, NSA_WIDTH, MEM_WIDTH, KV_WIDTH, KV_WIDTH, KV_WIDTH, 3 * NSA_HEADS, N_BRANCH * D_MODEL)
D_IN = sum(IN_SPLITS)
SCALE = HEAD_DIM ** -0.5

kernel_name = "hybrid_pool_nsa_memxattn_moe_step"

def rmsnorm(x, g):
    xf = x.astype(jnp.float32)
    r = lax.rsqrt(jnp.mean(xf * xf, axis=-1, keepdims=True) + EPS)
    return (xf * r).astype(x.dtype) * g

def masked_softmax(s, mask, axes=-1):
    s = jnp.where(mask, s.astype(jnp.float32), -jnp.inf)
    m = jnp.max(s, axis=axes, keepdims=True)
    m = jnp.where(jnp.isfinite(m), m, 0.0)
    e = jnp.where(mask, jnp.exp(s - m), 0.0)
    return e / jnp.maximum(jnp.sum(e, axis=axes, keepdims=True), 1e-30)

def rel_bucket(dist):
    n = jnp.maximum(dist, 0)
    max_exact = NUM_BUCKETS // 2
    nf = jnp.maximum(n, 1).astype(jnp.float32)
    large = max_exact + (jnp.log(nf / max_exact) / math.log(MAX_DISTANCE / max_exact)
                         * (NUM_BUCKETS - max_exact)).astype(jnp.int32)
    large = jnp.minimum(large, NUM_BUCKETS - 1)
    return jnp.where(n < max_exact, n, large)

def split_cols(z):
    outs, o = [], 0
    for n in IN_SPLITS:
        outs.append(z[..., o:o + n])
        o += n
    return outs

def norm_keys(kv, g):
    return jnp.stack([rmsnorm(kv[:, :, 0], g), kv[:, :, 1]], axis=2)

def project_in(x, p):
    b, t = x.shape[:2]
    u, q, qm, kvc, kvs, kvw, gn, gb = split_cols(rmsnorm(x, p["norm1_g"]) @ p["w_in"])
    q = rmsnorm(q.reshape(b, t, NSA_KV_HEADS, NSA_HPG, HEAD_DIM), p["nsa_qk_norm"][0])
    qm = rmsnorm(qm.reshape(b, t, MEM_HEADS, HEAD_DIM), p["mem_qk_norm"][0])
    kvc = kvc.reshape(b, t, 2, NSA_KV_HEADS, HEAD_DIM)
    kvs = norm_keys(kvs.reshape(b, t, 2, NSA_KV_HEADS, HEAD_DIM), p["nsa_qk_norm"][2])
    kvw = norm_keys(kvw.reshape(b, t, 2, NSA_KV_HEADS, HEAD_DIM), p["nsa_qk_norm"][3])
    gn = jax.nn.sigmoid(gn.astype(jnp.float32)).astype(x.dtype).reshape(b, t, 3, NSA_KV_HEADS, NSA_HPG)
    gb = jax.nn.sigmoid(gb.astype(jnp.float32)).astype(x.dtype).reshape(b, t, N_BRANCH, D_MODEL)
    return u, q, qm, kvc, kvs, kvw, gn, gb

def pool_mix(u, buf, pos0, p):
    b, t = u.shape[:2]
    z = jnp.concatenate([buf, u], axis=1).astype(jnp.float32)
    cs = jnp.concatenate([jnp.zeros((b, 1, POOL_WIDTH), jnp.float32), lax.cumsum(z, axis=1)], axis=1)
    pos = pos0 + jnp.arange(t)
    outs = []
    for gi, w in enumerate(POOL_WINDOWS):
        ch = slice(gi * POOL_GROUP, (gi + 1) * POOL_GROUP)
        hi = cs[:, POOL_BUF + 1:POOL_BUF + 1 + t, ch]
        lo = cs[:, POOL_BUF + 1 - w:POOL_BUF + 1 - w + t, ch]
        cnt = jnp.minimum(pos + 1, w).astype(jnp.float32)[None, :, None]
        d = ((hi - lo) / cnt).astype(u.dtype) - u[:, :, ch]
        outs.append(d @ p["pool_w"][gi])
    return jnp.concatenate(outs, axis=-1) * p["pool_scale"]

def compress_blocks(kv, cmp_w, cmp_pe):
    b, T = kv.shape[:2]
    n_cmp = (T - CMP_BLOCK) // CMP_STRIDE + 1
    r_sub = CMP_BLOCK // CMP_STRIDE
    n_sub = n_cmp + r_sub - 1
    sub = kv[:, :n_sub * CMP_STRIDE].reshape(b, n_sub, CMP_STRIDE, 2, NSA_KV_HEADS, HEAD_DIM)
    out = None
    for r in range(r_sub):
        sl = slice(r * CMP_STRIDE, (r + 1) * CMP_STRIDE)
        pe_r = jnp.transpose(cmp_pe[:, sl], (1, 0, 2))[:, :, None, :]
        part = jnp.einsum("bnjcgd,cjde->bncge", sub + pe_r, cmp_w[:, sl])[:, r:r + n_cmp]
        out = part if out is None else out + part
    end_pos = jnp.arange(n_cmp) * CMP_STRIDE + (CMP_BLOCK - 1)
    return out, end_pos

def cmp_attention(q, qpos, kc, vc, end_pos, rel_bias):
    t, n = q.shape[1], kc.shape[1]
    s = jnp.einsum("btgpd,bngd->btgpn", q, kc).astype(jnp.float32) * SCALE
    bias = rel_bias[rel_bucket(qpos[:, None] - end_pos[None, :])]
    bias = bias.reshape(t, n, NSA_KV_HEADS, NSA_HPG).transpose(0, 2, 3, 1)
    mask = (end_pos[None, :] <= qpos[:, None])[:, None, None, :]
    pr = masked_softmax(s + bias, mask)
    o = jnp.einsum("btgpn,bngd->btgpd", pr.astype(vc.dtype), vc)
    return o, pr

def select_blocks(p_cmp, qpos, end_pos, n_slc):
    start = end_pos - CMP_BLOCK + 1
    js = jnp.arange(n_slc) * SLC_BLOCK
    covers = (start[:, None] < js[None, :] + SLC_BLOCK) & (end_pos[:, None] >= js[None, :])
    imp = jnp.einsum("btgpn,nj->btgj", p_cmp, covers.astype(jnp.float32))
    qblk = qpos // SLC_BLOCK
    jj = jnp.arange(n_slc)[None, :]
    causal = jj <= qblk[:, None]
    forced = (jj == 0) | (jj == qblk[:, None]) | (jj == qblk[:, None] - 1)
    score = jnp.where(forced[None, :, None, :], jnp.inf, imp)
    score = jnp.where(causal[None, :, None, :], score, -jnp.inf)
    top, idx = lax.top_k(score, min(SLC_TOPK, n_slc))
    return idx, top > -jnp.inf

def slc_attention(q, qpos, kv_blocks, idx, valid, rel_bias):
    b = q.shape[0]
    bi = jnp.arange(b)[:, None, None, None]
    gi = jnp.arange(NSA_KV_HEADS)[None, None, :, None]
    kv = kv_blocks[bi, gi, idx]
    s = jnp.einsum("bcgpd,bcgkld->bcgpkl", q, kv[..., 0, :]).astype(jnp.float32) * SCALE
    kpos = idx[..., None] * SLC_BLOCK + jnp.arange(SLC_BLOCK)
    dist = qpos[None, :, None, None, None] - kpos
    rel_g = rel_bias.reshape(NUM_BUCKETS, NSA_KV_HEADS, NSA_HPG)
    bias = rel_g[rel_bucket(dist), gi[..., None]]
    bias = jnp.moveaxis(bias, -1, 3)
    mask = (valid[..., None] & (dist >= 0))[:, :, :, None]
    pr = masked_softmax(s + bias, mask, axes=(-2, -1))
    return jnp.einsum("bcgpkl,bcgkld->bcgpd", pr.astype(kv.dtype), kv[..., 1, :])

def nsa_global(q, qpos, kv_cmp, kv_slc, p, rel_bias):
    b, t = q.shape[:2]
    blk, end_pos = compress_blocks(kv_cmp, p["cmp_w"], p["cmp_pe"])
    kc = rmsnorm(blk[:, :, 0], p["nsa_qk_norm"][1])
    o_cmp, p_cmp = cmp_attention(q, qpos, kc, blk[:, :, 1], end_pos, rel_bias)
    T = kv_slc.shape[1]
    n_slc = -(-T // SLC_BLOCK)
    idx, valid = select_blocks(p_cmp, qpos, end_pos, n_slc)
    kvs = jnp.pad(kv_slc, ((0, 0), (0, n_slc * SLC_BLOCK - T), (0, 0), (0, 0), (0, 0)))
    kvs = kvs.reshape(b, n_slc, SLC_BLOCK, 2, NSA_KV_HEADS, HEAD_DIM).transpose(0, 4, 1, 2, 3, 5)
    c = math.gcd(SEL_Q_BLOCK, t)
    nc = t // c

    def chunks(a):
        return jnp.moveaxis(a.reshape((b, nc, c) + a.shape[2:]), 1, 0)

    xs = (chunks(q), qpos.reshape(nc, c), chunks(idx), chunks(valid))
    o = lax.map(lambda a: slc_attention(a[0], a[1], kvs, a[2], a[3], rel_bias), xs)
    o_slc = jnp.moveaxis(o, 0, 1).reshape(q.shape)
    return o_cmp, o_slc

def win_attention(q, qpos, kv, kpos, rel_bias):
    nb, c = qpos.shape
    k = kpos.shape[1]
    s = jnp.einsum("bncgpd,bnkgd->bngpck", q, kv[:, :, :, 0]).astype(jnp.float32) * SCALE
    dist = qpos[:, :, None] - kpos[:, None, :]
    mask = (dist >= 0) & (dist < WINDOW) & (kpos[:, None, :] >= 0)
    bias = rel_bias[rel_bucket(dist)].reshape(nb, c, k, NSA_KV_HEADS, NSA_HPG).transpose(0, 3, 4, 1, 2)
    pr = masked_softmax(s + bias[None], mask[None, :, None, None])
    return jnp.einsum("bngpck,bnkgd->bncgpd", pr.astype(kv.dtype), kv[:, :, :, 1])

def nsa_combine(gn, o_cmp, o_slc, o_win):
    return (gn[:, :, 0, :, :, None] * o_cmp + gn[:, :, 1, :, :, None] * o_slc
            + gn[:, :, 2, :, :, None] * o_win)

def mem_kv_proj(mem, p):
    b, m = mem.shape[:2]
    kv = (rmsnorm(mem, p["mem_norm_g"]) @ p["w_mem_kv"]).reshape(b, m, 2, MEM_HEADS, HEAD_DIM)
    return norm_keys(kv, p["mem_qk_norm"][1])

def mem_attention(qm, mem_kv):
    s = jnp.einsum("bthd,bmhd->bhtm", qm, mem_kv[:, :, 0]).astype(jnp.float32) * SCALE
    pr = jax.nn.softmax(s, axis=-1)
    return jnp.einsum("bhtm,bmhd->bthd", pr.astype(mem_kv.dtype), mem_kv[:, :, 1])

def moe(h, p):
    b, t, d = h.shape
    hf = h.reshape(-1, d)
    n = hf.shape[0]
    logits = (hf @ p["router_w"] + p["router_b"]).astype(jnp.float32)
    top, eidx = lax.top_k(logits, TOP_K)
    gates = jax.nn.softmax(top, axis=-1)
    a = n * TOP_K
    flat_e = eidx.reshape(-1)
    order = jnp.argsort(flat_e)
    sorted_e = flat_e[order]
    counts = jnp.bincount(flat_e, length=N_EXPERTS)
    starts = jnp.cumsum(counts) - counts
    padded = (counts + MOE_BLOCK - 1) // MOE_BLOCK * MOE_BLOCK
    pad_ends = jnp.cumsum(padded)
    pad_starts = pad_ends - padded
    dest = pad_starts[sorted_e] + jnp.arange(a) - starts[sorted_e]
    n_blocks = -(-a // MOE_BLOCK) + N_EXPERTS
    rows = jnp.zeros((n_blocks * MOE_BLOCK, d), h.dtype).at[dest].set(hf[order // TOP_K])
    blk_e = jnp.minimum(jnp.searchsorted(pad_ends, jnp.arange(n_blocks) * MOE_BLOCK, side="right"),
                        N_EXPERTS - 1)

    def expert_block(args):
        xb, e = args
        gu = xb @ p["w_gu"][e] + p["b_gu"][e]
        gate = jnp.minimum(gu[:, :D_FF], SWIGLU_LIMIT)
        up = jnp.clip(gu[:, D_FF:], -SWIGLU_LIMIT, SWIGLU_LIMIT)
        act = gate * jax.nn.sigmoid(SWIGLU_ALPHA * gate) * (up + 1)
        return act @ p["w_down"][e] + p["b_down"][e]

    out_rows = lax.map(expert_block, (rows.reshape(n_blocks, MOE_BLOCK, d), blk_e)).reshape(-1, d)
    y = jnp.zeros((a, d), h.dtype).at[order].set(out_rows[dest]).reshape(n, TOP_K, d)
    return jnp.einsum("nk,nkd->nd", gates.astype(h.dtype), y).reshape(b, t, d)

def layer_tail(x, gb, o_pool, o_nsa, o_mem, p):
    b, t = x.shape[:2]
    mixed = (gb[:, :, 0] * (o_pool @ p["w_up_pool"])
             + gb[:, :, 1] * (o_nsa.reshape(b, t, NSA_WIDTH) @ p["w_up_nsa"])
             + gb[:, :, 2] * (o_mem.reshape(b, t, MEM_WIDTH) @ p["w_up_mem"]))
    x = x + mixed @ p["w_out"]
    return x + moe(rmsnorm(x, p["norm2_g"]), p)

def last_rows(a, n):
    t = a.shape[1]
    if t < n:
        a = jnp.pad(a, [(0, 0), (n - t, 0)] + [(0, 0)] * (a.ndim - 2))
    return a[:, a.shape[1] - n:]

def prompt_layer(x, mem, p, rel_bias):
    b, s = x.shape[:2]
    u, q, qm, kvc, kvs, kvw, gn, gb = project_in(x, p)
    pos = jnp.arange(s)
    o_pool = pool_mix(u, jnp.zeros((b, POOL_BUF, POOL_WIDTH), u.dtype), 0, p)
    o_cmp, o_slc = nsa_global(q, pos, kvc, kvs, p, rel_bias)
    nb = s // WIN_Q_BLOCK
    n_prev = -(-(WINDOW - 1) // WIN_Q_BLOCK)
    padded = jnp.pad(kvw, ((0, 0), (n_prev * WIN_Q_BLOCK, 0), (0, 0), (0, 0), (0, 0)))
    padded = padded.reshape((b, nb + n_prev, WIN_Q_BLOCK) + kvw.shape[2:])
    span = jnp.concatenate([padded[:, i:i + nb] for i in range(n_prev + 1)], axis=2)
    kpos = (jnp.arange(nb)[:, None] - n_prev) * WIN_Q_BLOCK + jnp.arange((n_prev + 1) * WIN_Q_BLOCK)[None, :]
    qb = q.reshape((b, nb, WIN_Q_BLOCK) + q.shape[2:])
    o_win = win_attention(qb, pos.reshape(nb, WIN_Q_BLOCK), span, kpos, rel_bias).reshape(q.shape)
    o_nsa = nsa_combine(gn, o_cmp, o_slc, o_win)
    mem_kv = mem_kv_proj(mem, p)
    o_mem = mem_attention(qm, mem_kv)
    y = layer_tail(x, gb, o_pool, o_nsa, o_mem, p)
    win_buf = min(WINDOW, PAST_LEN)
    return y, (kvc, kvs, last_rows(kvw, win_buf), mem_kv, last_rows(u, POOL_BUF))

def sample_layer(x, cache_cmp, cache_slc, cache_win, cache_mem, pool_buf, page_table, p, rel_bias):
    b, t = x.shape[:2]
    past = page_table.shape[1] * cache_cmp.shape[1]
    u, q, qm, kvc, kvs, kvw, gn, gb = project_in(x, p)
    pos = past + jnp.arange(t)

    def gather(pool):
        return pool[page_table].reshape((b, past) + pool.shape[2:])

    full_c = jnp.concatenate([gather(cache_cmp), kvc], axis=1)
    full_s = jnp.concatenate([gather(cache_slc), kvs], axis=1)
    o_pool = pool_mix(u, pool_buf, past, p)
    o_cmp, o_slc = nsa_global(q, pos, full_c, full_s, p, rel_bias)
    wb = cache_win.shape[1]
    win_kv = jnp.concatenate([cache_win, kvw], axis=1)
    kpos = (past - wb + jnp.arange(wb + t))[None, :]
    o_win = win_attention(q[:, None], pos[None, :], win_kv[:, None], kpos, rel_bias)[:, 0]
    o_nsa = nsa_combine(gn, o_cmp, o_slc, o_win)
    o_mem = mem_attention(qm, cache_mem)
    y = layer_tail(x, gb, o_pool, o_nsa, o_mem, p)
    new_pool = jnp.concatenate([pool_buf, u], axis=1)[:, t:]
    return y, (kvc, kvs, win_kv[:, t:], new_pool)

def setup_inputs(seed: int = 0) -> dict:
    key = jax.random.key(seed)
    ks = iter(jax.random.split(key, 40))

    def nrm(shape, scale):
        return jax.random.normal(next(ks), shape, jnp.float32) * scale

    n_pages = PAST_LEN // PAGE_SIZE
    n_used = DEC_BATCH * n_pages
    n_phys = n_used + max(1, n_used // 4)
    page_table = jax.random.permutation(next(ks), n_phys)[:n_used].astype(jnp.int32).reshape(DEC_BATCH, n_pages)
    win_buf = min(WINDOW, PAST_LEN)
    kv_tail = (2, NSA_KV_HEADS, HEAD_DIM)
    L = DEPTH
    return {
        "x_prompt": nrm((BATCH, SEQ, D_MODEL), 1.0),
        "x_sample": nrm((DEC_BATCH, DEC_SEQ, D_MODEL), 1.0),
        "cache_cmp_kv": nrm((L, n_phys, PAGE_SIZE) + kv_tail, 1.0),
        "cache_slc_kv": nrm((L, n_phys, PAGE_SIZE) + kv_tail, 1.0),
        "cache_win_kv": nrm((L, DEC_BATCH, win_buf) + kv_tail, 1.0),
        "cache_mem_kv": nrm((L, DEC_BATCH, MEM_TOKENS, 2, MEM_HEADS, HEAD_DIM), 1.0),
        "state_pool": nrm((L, DEC_BATCH, POOL_BUF, POOL_WIDTH), 1.0),
        "page_table": page_table,
        "mem_prompt": nrm((BATCH, MEM_TOKENS, D_MODEL), 1.0),
        "rel_bias": nrm((NUM_BUCKETS, NSA_HEADS), 0.5),
        "norm1_g": 1.0 + nrm((L, D_MODEL), 0.02),
        "w_in": nrm((L, D_MODEL, D_IN), D_MODEL ** -0.5),
        "nsa_qk_norm": 1.0 + nrm((L, 4, HEAD_DIM), 0.02),
        "mem_qk_norm": 1.0 + nrm((L, 2, HEAD_DIM), 0.02),
        "cmp_w": nrm((L, 2, CMP_BLOCK, HEAD_DIM, HEAD_DIM), (CMP_BLOCK * HEAD_DIM) ** -0.5),
        "cmp_pe": nrm((L, 2, CMP_BLOCK, HEAD_DIM), 0.1),
        "pool_w": nrm((L, len(POOL_WINDOWS), POOL_GROUP, POOL_GROUP), POOL_GROUP ** -0.5),
        "pool_scale": 1.0 + nrm((L, POOL_WIDTH), 0.1),
        "mem_norm_g": 1.0 + nrm((L, D_MODEL), 0.02),
        "w_mem_kv": nrm((L, D_MODEL, 2 * MEM_WIDTH), D_MODEL ** -0.5),
        "w_up_pool": nrm((L, POOL_WIDTH, D_MODEL), POOL_WIDTH ** -0.5),
        "w_up_nsa": nrm((L, NSA_WIDTH, D_MODEL), NSA_WIDTH ** -0.5),
        "w_up_mem": nrm((L, MEM_WIDTH, D_MODEL), MEM_WIDTH ** -0.5),
        "w_out": nrm((L, D_MODEL, D_MODEL), D_MODEL ** -0.5),
        "norm2_g": 1.0 + nrm((L, D_MODEL), 0.02),
        "router_w": nrm((L, D_MODEL, N_EXPERTS), D_MODEL ** -0.5),
        "router_b": nrm((L, N_EXPERTS), 0.01),
        "w_gu": nrm((L, N_EXPERTS, D_MODEL, 2 * D_FF), D_MODEL ** -0.5),
        "b_gu": nrm((L, N_EXPERTS, 2 * D_FF), 0.01),
        "w_down": nrm((L, N_EXPERTS, D_FF, D_MODEL), D_FF ** -0.5),
        "b_down": nrm((L, N_EXPERTS, D_MODEL), 0.01),
    }

def reference(x_prompt, x_sample, cache_cmp_kv, cache_slc_kv, cache_win_kv, cache_mem_kv, state_pool,
              page_table, mem_prompt, rel_bias, norm1_g, w_in, nsa_qk_norm, mem_qk_norm, cmp_w, cmp_pe,
              pool_w, pool_scale, mem_norm_g, w_mem_kv, w_up_pool, w_up_nsa, w_up_mem, w_out, norm2_g,
              router_w, router_b, w_gu, b_gu, w_down, b_down):
    yp, ys = x_prompt, x_sample
    outs_p = [[] for _ in range(5)]
    outs_s = [[] for _ in range(4)]
    for l in range(DEPTH):
        p = {"norm1_g": norm1_g[l], "w_in": w_in[l], "nsa_qk_norm": nsa_qk_norm[l],
             "mem_qk_norm": mem_qk_norm[l], "cmp_w": cmp_w[l], "cmp_pe": cmp_pe[l],
             "pool_w": pool_w[l], "pool_scale": pool_scale[l], "mem_norm_g": mem_norm_g[l],
             "w_mem_kv": w_mem_kv[l], "w_up_pool": w_up_pool[l], "w_up_nsa": w_up_nsa[l],
             "w_up_mem": w_up_mem[l], "w_out": w_out[l], "norm2_g": norm2_g[l],
             "router_w": router_w[l], "router_b": router_b[l], "w_gu": w_gu[l], "b_gu": b_gu[l],
             "w_down": w_down[l], "b_down": b_down[l]}
        yp, st_p = prompt_layer(yp, mem_prompt, p, rel_bias)
        ys, st_s = sample_layer(ys, cache_cmp_kv[l], cache_slc_kv[l], cache_win_kv[l], cache_mem_kv[l],
                                state_pool[l], page_table, p, rel_bias)
        for lst, a in zip(outs_p, st_p):
            lst.append(a)
        for lst, a in zip(outs_s, st_s):
            lst.append(a)
    new_cmp_p, new_slc_p, new_win_p, new_mem_p, new_pool_p = [jnp.stack(a) for a in outs_p]
    new_cmp_s, new_slc_s, new_win_s, new_pool_s = [jnp.stack(a) for a in outs_s]
    return (yp, ys, new_cmp_p, new_slc_p, new_win_p, new_mem_p, new_pool_p,
            new_cmp_s, new_slc_s, new_win_s, new_pool_s)


_drawn_inputs = setup_inputs


def setup_inputs(seed=0):
    import zlib

    import numpy as np

    out = dict(_drawn_inputs(seed))
    spreads = {}
    factors = {'nsa_qk_norm': 4.077,
     'mem_qk_norm': 3.658,
     'mem_norm_g': 2.882,
     'b_gu': 8.0,
     'b_down': 8.0}
    for name, (base, spread) in spreads.items():
        noise = np.random.default_rng([zlib.crc32(name.encode()), seed]).standard_normal(out[name].shape)
        drawn = base * np.exp(spread * noise) if base else spread * noise
        out[name] = __import__('jax').numpy.asarray(drawn.astype(out[name].dtype))
    for name, factor in factors.items():
        out[name] = (out[name] * factor).astype(out[name].dtype)
    return out
```

```python
import math
from contextlib import ExitStack

import numpy as np

import concourse.bass as bass
from concourse import mybir

F32 = mybir.dt.float32
BF16 = mybir.dt.bfloat16
I32 = mybir.dt.int32
U32 = mybir.dt.uint32
ALU = mybir.AluOpType
ACT = mybir.ActivationFunctionType
AX = mybir.AxisListType.X

D = 1024
NP_TOK = 512
NS = 8
TS = 4
NTOK = NP_TOK + NS * TS
NT = 5
ROWS = [128, 128, 128, 128, 32]
KD = D // 128
HD = 64
NH = 8
MH = 4
MEM = 256
EPS = 1e-6
NEG = -1e30
PAST = 2048
PAGE = 128
SUB = 16
NSUB = PAST // SUB
NCMP_S = NSUB - 1
NCMP_P = NP_TOK // SUB - 1
ROWF = SUB * 256
WTOK = 1560
NE = 32
BIASL = 640
CMPL = 1024
QSCALE = HD ** -0.5
HALF = NTOK // 2
TOPK = 4
NBLK = (NTOK * TOPK - NE) // 128 + NE
ALPHA = 1.702
LIMIT = 7.0


def shape_constants():
    def bucket(dist):
        n = np.maximum(dist, 0)
        nf = np.maximum(n, 1).astype(np.float32)
        large = 16 + (np.log(nf / np.float32(16)) / np.float32(math.log(8.0)) * np.float32(16)).astype(np.int32)
        return np.where(n < 16, n, np.minimum(large, 31))

    def onehot(dist, rows):
        out = np.zeros((rows,) + dist.shape, np.float32)
        b = bucket(dist)
        for r in range(32):
            out[r] = (b == r)
        if rows > 32:
            out[:32] *= (dist >= 0)
            out[32] = (dist < 0)
        return out

    c = {}
    c["c_ident"] = np.eye(128, dtype=np.float32)
    c["c_before"] = np.triu(np.ones((128, 128), np.float32), 1)
    c["c_dist_desc"] = onehot(511 - np.arange(BIASL), 33)
    c["c_dist_asc"] = onehot(np.arange(CMPL) - 511, 33)
    t = np.arange(TS)[:, None]
    col = np.arange(PAST)
    slc_key = (col % 128) * SUB + col // 128
    win_key = (np.arange(512) % 128) * 4 + np.arange(512) // 128
    tables = {
        "c_oh_slc": PAST + t - slc_key[None],
        "c_oh_win": 512 + t - win_key[None],
        "c_oh_cmp": PAST + t - (np.arange(NCMP_S)[None] * 16 + 31),
    }
    for name, dist in tables.items():
        o = onehot(dist, 32)
        c[name] = np.ascontiguousarray(o.transpose(1, 0, 2).reshape(128, -1))
    c["c_mask_win"] = np.ascontiguousarray(np.tile(
        np.where(512 + t - win_key[None] < 512, 0.0, NEG).astype(np.float32), (32, 1)))
    new = np.zeros((TS, 32, 32), np.float32)
    cols_t = np.arange(32) % TS
    for tt in range(TS):
        new[tt] = onehot(np.maximum(tt - cols_t, 0), 32)
    c["c_oh_new"] = new.reshape(128, 32)
    mask = np.zeros((128, 2, 32), np.float32)
    for row in range(128):
        for r in range(2):
            for cc in range(32):
                ok = cc // TS == 4 * r + row // 32 and cc % TS <= row % TS
                mask[row, r, cc] = 0.0 if ok else NEG
    c["c_mask_new"] = mask.reshape(128, 64)
    covers = np.zeros((NCMP_S, 33), np.float32)
    for n in range(NCMP_S):
        for j in range(33):
            covers[n, j] = (n * 16 < j * 64 + 64) and (n * 16 + 31 >= j * 64)
    c["c_covers"] = covers
    force = np.zeros((128, 33), np.float32)
    force[:, [0, 31, 32]] = 1e30
    c["c_force"] = force
    inv = np.zeros((128, 2, NP_TOK), np.float32)
    for ch in range(256):
        w = (2, 4, 8, 16)[ch // 64]
        inv[ch % 128, ch // 128] = 1.0 / np.minimum(np.arange(NP_TOK) + 1, w)
    c["c_inv_count"] = inv.reshape(128, -1)
    p = np.arange(128)
    c["c_cols"] = np.stack([p, p % 8, p % 32, 1.0 * (p >= 64), 1.0 * (p < 64)], 1).astype(np.float32)
    c["c_iota32"] = np.tile(np.arange(32, dtype=np.float32), (128, 1))
    tile, choice = np.divmod(np.arange(NT * TOPK), TOPK)
    c["c_row_id"] = (TOPK * (np.arange(128)[:, None] + 128 * tile) + choice + 1).astype(np.float32)
    c["c_spare_row"] = (NTOK * TOPK + 1.0 + np.arange(128, dtype=np.float32))[:, None].astype(np.float32)
    c["c_iota128"] = np.tile(np.arange(128, dtype=np.float32), (128, 1))
    return c


def lay_out(a):
    f = {}
    f["x_all"] = np.concatenate([a["x_prompt"][0], a["x_sample"].reshape(NS * TS, D)], 0)
    f["mem"] = a["mem_prompt"][0]
    w = a["w_in"][0]
    q0, qm0, c0, s0, w0, gn0, gb0 = 256, 768, 1024, 1280, 1536, 1792, 1816
    q = w[:, q0:qm0].reshape(D, 2, 4, HD).transpose(0, 2, 1, 3).reshape(D, 512)
    gn = w[:, gn0:gb0].reshape(D, 3, 2, 4).transpose(0, 3, 2, 1).reshape(D, 24)
    f["w_tok"] = np.concatenate([q, w[:, qm0:c0], w[:, s0:s0 + 128], w[:, w0:w0 + 128], w[:, c0:s0],
                                 w[:, s0 + 128:s0 + 256], w[:, w0 + 128:w0 + 256], gn], 1)
    f["w_u"] = w[:, :256]
    gb = w[:, gb0:].reshape(KD, 128, 3, KD, 128)
    f["w_gb"] = gb.transpose(3, 2, 1, 0, 4).reshape(KD, 3, 128, KD * 128)
    f["w_mem"] = a["w_mem_kv"][0]
    col = lambda v: v.reshape(KD, 128).T
    f["gain_cols"] = np.concatenate([col(a["norm1_g"][0]), col(a["mem_norm_g"][0]), col(a["norm2_g"][0]),
                                     a["pool_scale"][0].reshape(2, 128).T], 1)
    qk, mq = a["nsa_qk_norm"][0], a["mem_qk_norm"][0]
    f["gain_rows"] = np.concatenate([np.tile(qk[0], 8), np.tile(mq[0], 4), np.tile(qk[2], 2), np.tile(qk[3], 2),
                                     np.tile(mq[1], 4), np.tile(qk[1], 2)])[None]
    rb = a["rel_bias"].reshape(32, 2, 4).transpose(0, 2, 1).reshape(32, 8)
    f["rel_bias"] = rb
    cw = a["cmp_w"][0].reshape(2, 2, 8, 2, HD, HD)
    f["w_cmp"] = cw.transpose(3, 4, 0, 2, 1, 5).reshape(128, 2 * 8 * 128)
    pe = a["cmp_pe"][0].reshape(2, 2, 8, 2, HD)
    f["pe_cmp"] = pe.transpose(3, 4, 0, 2, 1).reshape(128, 32)
    pw = np.zeros((2, 128, 128), np.float32)
    for i in range(4):
        h = 64 * (i % 2)
        pw[i // 2, h:h + 64, h:h + 64] = a["pool_w"][0, i]
    f["w_pool"] = pw
    nsa = a["w_up_nsa"][0].reshape(2, 4, HD, D).transpose(1, 0, 2, 3).reshape(512, D)
    f["w_up"] = np.concatenate([a["w_up_pool"][0], nsa, a["w_up_mem"][0]], 0)
    f["w_out"] = a["w_out"][0]
    f["router_w"] = a["router_w"][0]
    f["router_b"] = a["router_b"]
    f["w_gu"] = a["w_gu"][0]
    f["b_gu"] = a["b_gu"][0]
    f["w_down"] = a["w_down"][0]
    f["b_down"] = a["b_down"][0]
    f["cache_cmp"] = a["cache_cmp_kv"][0].reshape(-1, ROWF)
    f["cache_slc"] = a["cache_slc_kv"][0].reshape(-1, ROWF)
    f["cache_win"] = a["cache_win_kv"][0].reshape(NS, 512, 256)
    f["cache_mem"] = a["cache_mem_kv"][0].reshape(NS, 256, 512)
    f["state_pool"] = a["state_pool"][0]
    f["pages"] = np.repeat(np.asarray(a["page_table"]).T, PAGE // SUB, axis=0)
    return {k: np.ascontiguousarray(v) for k, v in f.items()}


OUTPUTS = {
    "y_prompt": (1, 512, 1024), "y_sample": (8, 4, 1024), "new_cmp_p": (1, 1, 512, 2, 2, 64),
    "new_slc_p": (1, 1, 512, 2, 2, 64), "new_win_p": (1, 1, 512, 2, 2, 64), "new_mem_p": (1, 1, 256, 2, 4, 64),
    "new_pool_p": (1, 1, 15, 256), "new_cmp_s": (1, 8, 4, 2, 2, 64), "new_slc_s": (1, 8, 4, 2, 2, 64),
    "new_win_s": (1, 8, 512, 2, 2, 64), "new_pool_s": (1, 8, 15, 256),
}


def build_program(nc, i, o, stop_after=99):
    ctx = ExitStack()
    with ctx:
        of_phase = []

        def sem(name):
            of_phase.append(nc.alloc_semaphore(name=name))
            return of_phase[-1]

        def phase_over():
            nc.clear_and_free_semaphores(list(of_phase))
            nc.all_engine_barrier()
            of_phase.clear()

        def scratch(name, shape, dt=F32):
            return nc.dram_tensor(name, shape, dt, kind="Internal").ap()

        arena = ctx.enter_context(nc.sbuf_tensor("arena", [128, 53000], F32))
        psum = ctx.enter_context(nc.psum_tensor("psum", [128, 8, 512], F32))
        cursor = [0]

        def take(*dims, dt=F32):
            n = int(np.prod(dims))
            words = n if dt in (F32, I32, U32) else -(-n // 2)
            at = arena[:, cursor[0]:cursor[0] + words]
            cursor[0] += words + words % 2
            assert cursor[0] <= 53000, cursor[0]
            if dt != F32:
                at = at.bitcast(dt)
            if len(dims) == 1:
                return at
            names = "abcd"[:len(dims)]
            return at.rearrange(f"p ({' '.join(names)}) -> p {' '.join(names)}",
                                **{n_: d_ for n_, d_ in zip(names, dims)})

        def bank(b, n=1):
            return psum[:, b] if n == 1 else psum[:, b:b + n]

        ident = take(128)
        ones = take(128)
        x = take(NT, D)
        gain_cols = take(26)
        g1c, gmc, g2c, psc = (gain_cols[:, 8 * n:min(8 * n + 8, 26)] for n in range(4))
        cols = take(6)
        iota32 = take(32)
        sumsq, root, rinv = take(8), take(8), take(8)
        eps = take(1)
        moe_base = cursor[0]
        hT = take(KD, NTOK)
        gates = take(NT, 24)
        oT_at = cursor[0]
        oT_nsa = take(4, NTOK)
        oT_mem = take(2, NTOK)
        oT_pool = take(2, NTOK)
        tail_base = cursor[0]
        qT = take(4, NTOK)
        qmT = take(2, NTOK)
        ksT = take(NTOK)
        kwT = take(NTOK)
        kmT = take(2, MEM)
        v_slc = take(NT, 128)
        v_win = take(NT, 128)
        zm = take(2, 512)
        kcT = take(NS + 1, 128)
        v_cmp = take(NS + 1, 128)
        phase_base = cursor[0]
        mT = take(KD, MEM)
        w_tok = take(KD, WTOK)
        w_mem = take(KD, 512)
        w_u = take(KD, 256)
        mem = take(2, D)
        xn = take(2, D)
        zt = arena[:, oT_at:oT_at + 2 * WTOK].rearrange("p (b n) -> p b n", b=2)
        zsq = take(D)
        gain_rows = take(1408)
        ss16, rt16, ri16 = take(16), take(16), take(16)
        cursor[0] = phase_base
        pool_base = cursor[0]
        u_prompt = take(2, 16 + NP_TOK)
        u_sample = take(2, NS, 16 + TS)
        sum_a = take(2, 16 + NP_TOK)
        sum_b = take(2, 16 + NP_TOK)
        ssum_a = take(2, NS, 16 + TS)
        ssum_b = take(2, NS, 16 + TS)
        dT = take(2, NTOK)
        inv_count = take(2, NP_TOK)
        w_pool = take(2, 128)
        hist = take(256)
        u_rows = take(2, 256)
        u_new = take(2, NS * TS)

        s_const = sem("s_const")
        s_ones = sem("s_ones")
        s_x = [sem(f"s_x{n}") for n in range(7)]
        s_wtok = sem("s_wtok")
        s_wmem = sem("s_wmem")
        s_act = sem("s_act")
        s_dve = sem("s_dve")
        s_pool = sem("s_pool")
        s_root = sem("s_root")
        s_xn = sem("s_xn")
        s_tp = sem("s_tp")
        s_hT = sem("s_hT")
        s_zp = sem("s_zp")
        s_ze = sem("s_ze")
        s_sq = sem("s_sq")
        s_ss = sem("s_ss")
        s_rt = sem("s_rt")
        s_zn = sem("s_zn")
        s_vc = sem("s_vc")
        s_gn = sem("s_gn")
        s_zo = [sem(f"s_zo{n}") for n in range(2)]
        s_mo = sem("s_mo")
        s_tq = sem("s_tq")
        s_te = sem("s_te")
        s_cp = sem("s_cp")
        s_up = sem("s_up")
        s_ue = sem("s_ue")
        s_pl = sem("s_pl")
        s_uz = sem("s_uz")
        s_ht = sem("s_ht")
        s_he = sem("s_he")
        s_uo = sem("s_uo")
        s_dT = sem("s_dT")
        s_pp = sem("s_pp")
        s_po = sem("s_po")

        rows_of = lambda n: ROWS[n] if n < NT else 128
        src = lambda n: x[0:rows_of(n), n, :] if n < NT else mem[:, n - NT, :]
        dstT = lambda n: hT[:, :, 128 * n:128 * n + rows_of(n)] if n < NT else mT[:, :, 128 * (n - NT):128 * (n - NT) + 128]
        CH = [(0, 512), (512, 1024), (1024, 1536), (1536, WTOK)]
        tok_rows = lambda ap, n: ap[128 * n:128 * n + ROWS[n]]

        def linked(eng, s, at):
            def link(ins):
                at[0] += 1
                ins.then_inc(s, 1)
                eng.wait_ge(s, at[0])
            return link

        out_cp = o["new_cmp_p"].rearrange("a b t c g d -> (a b t) (c g d)")
        out_sp = o["new_slc_p"].rearrange("a b t c g d -> (a b t) (c g d)")
        out_wp = o["new_win_p"].rearrange("a b t c g d -> (a b t) (c g d)")
        out_cs = o["new_cmp_s"].rearrange("a s t c g d -> (a s t) (c g d)")
        out_ss = o["new_slc_s"].rearrange("a s t c g d -> (a s t) (c g d)")
        out_ws = o["new_win_s"].rearrange("a s t c g d -> (a s) t (c g d)")
        out_mp = o["new_mem_p"].rearrange("a b t c h d -> (a b t) (c h d)")
        out_pp = o["new_pool_p"].rearrange("a b t c -> (a b t) c")
        out_ps = o["new_pool_s"].rearrange("a s t c -> (a s) t c")

        with nc.Block() as block:

            @block.sync
            def _(sp):
                for dst, name in ((ident, "c_ident"), (gain_cols, "gain_cols"), (cols[:, 0:5], "c_cols"),
                                  (iota32, "c_iota32")):
                    sp.dma_start(dst, i[name]).then_inc(s_const, 16)
                sp.dma_start(gain_rows, i["gain_rows"].partition_broadcast(128).rearrange("p a n -> p (a n)")
                             ).then_inc(s_const, 16)
                for n in range(7):
                    r = rows_of(n)
                    from_ = i["x_all"][128 * n:128 * n + r] if n < NT else i["mem"][128 * (n - NT):128 * (n - NT) + 128]
                    sp.dma_start(src(n), from_).then_inc(s_x[n], 16)
                    if n == 0:
                        w = i["w_tok"].rearrange("(k p) n -> p k n", p=128)
                        for k in range(0, KD, 2):
                            sp.dma_start(w_tok[:, k:k + 2], w[:, k:k + 2]).then_inc(s_wtok, 16)
                sp.dma_start(w_mem, i["w_mem"].rearrange("(k p) n -> p k n", p=128)).then_inc(s_wmem, 16)
                sp.dma_start(w_u, i["w_u"].rearrange("(k p) n -> p k n", p=128)).then_inc(s_wmem, 16)
                sp.dma_start(out_ws[:, 0:508], i["cache_win"][:, 4:512]).then_inc(s_cp, 16)
                sp.dma_start(out_ps[:, 0:11], i["state_pool"][:, 4:15]).then_inc(s_cp, 16)
                for n in range(NT):
                    r = ROWS[n]
                    z = zt[0:r, n % 2]
                    sp.wait_ge(s_zn, n + 1)
                    sp.wait_ge(s_ze, 4 * n + 4)
                    if n < 4:
                        oc, os_, ow = tok_rows(out_cp, n), tok_rows(out_sp, n), tok_rows(out_wp, n)
                        sp.dma_start(ow[:, 0:128], z[:, 896:1024]).then_inc(s_zo[n % 2], 16)
                        sp.dma_start(ow[:, 128:256], z[:, 1408:1536]).then_inc(s_zo[n % 2], 16)
                    else:
                        oc, os_ = out_cs, out_ss
                        sp.dma_start(out_ws[:, 508:512, 0:128], z[:, 896:1024]).then_inc(s_zo[n % 2], 16)
                        sp.dma_start(out_ws[:, 508:512, 128:256], z[:, 1408:1536]).then_inc(s_zo[n % 2], 16)
                    sp.dma_start(oc, z[:, 1024:1280]).then_inc(s_zo[n % 2], 16)
                    sp.dma_start(os_[:, 0:128], z[:, 768:896]).then_inc(s_zo[n % 2], 16)
                    sp.dma_start(os_[:, 128:256], z[:, 1280:1408]).then_inc(s_zo[n % 2], 16)
                sp.wait_ge(s_zn, NT + 2)
                sp.wait_ge(s_ze, 22)
                sp.dma_start(out_mp.rearrange("(m p) c -> p m c", p=128), zm).then_inc(s_mo, 16)
                sp.wait_ge(s_zp, 22)
                sp.dma_start(inv_count, i["c_inv_count"].rearrange("p (k t) -> p k t", k=2)).then_inc(s_pl, 16)
                sp.dma_start(w_pool, i["w_pool"].rearrange("k p n -> p k n")).then_inc(s_pl, 16)
                sp.dma_start(hist[0:120], i["state_pool"].rearrange("s t c -> (s t) c")).then_inc(s_pl, 16)
                sp.wait_ge(s_he, 4)
                sp.dma_start(out_pp, u_rows[0:15, 0]).then_inc(s_uo, 16)
                sp.dma_start(out_ps[:, 11:15], u_rows[0:32, 1]).then_inc(s_uo, 16)
                sp.wait_ge(s_zo[0], 16 * 15)
                sp.wait_ge(s_zo[1], 16 * 10)
                sp.wait_ge(s_mo, 16)
                sp.wait_ge(s_cp, 32)
                sp.wait_ge(s_uo, 32)

            @block.scalar
            def _(act):
                link = linked(act, s_act, [0])
                act.wait_ge(s_ones, 2)
                act.wait_ge(s_const, 80)
                for n in range(7):
                    r = rows_of(n)
                    act.wait_ge(s_x[n], 16)
                    link(act.activation(zsq[0:r], src(n), ACT.Square, accum_out=sumsq[0:r, n:n + 1]))
                    act.activation(root[0:r, n:n + 1], sumsq[0:r, n:n + 1], ACT.Sqrt, bias=eps[0:r],
                                   scale=1.0 / D).then_inc(s_root, 1)

                def evacuate(n):
                    r = ROWS[n]
                    if n >= 2:
                        act.wait_ge(s_zo[n % 2], 80 * (n // 2))
                        act.wait_ge(s_tq, 2 * n - 2)
                        act.wait_ge(s_vc, n - 1)
                    for c, (a, b) in enumerate(CH):
                        act.wait_ge(s_zp, 4 * n + c + 1)
                        act.activation(zt[0:r, n % 2, a:b], bank(2 + c)[0:r, 0:b - a], ACT.Copy).then_inc(s_ze, 1)

                def evacuate_mem(m):
                    act.wait_ge(s_zp, 21 + m)
                    act.activation(zm[:, m], bank(2 + m), ACT.Copy).then_inc(s_ze, 1)

                def roots(n):
                    r = rows_of(n)
                    act.wait_ge(s_ss, n + 1)
                    act.activation(rt16[0:r], ss16[0:r], ACT.Sqrt, bias=eps[0:r], scale=1.0 / HD).then_inc(s_rt, 1)

                def heads_out(n):
                    r = ROWS[n]
                    t = slice(128 * n, 128 * n + r)
                    act.wait_ge(s_tq, 2 * n + 1)
                    act.activation(qT[:, :, t], bank(6)[:, 0:4 * r].rearrange("p (a b) -> p a b", a=4), ACT.Copy,
                                   scale=QSCALE).then_inc(s_te, 1)
                    act.wait_ge(s_tq, 2 * n + 2)
                    b7 = bank(7)[:, 0:4 * r].rearrange("p (a b) -> p a b", a=4)
                    act.activation(qmT[:, :, t], b7[:, 0:2], ACT.Copy, scale=QSCALE).then_inc(s_te, 1)
                    act.activation(ksT[:, t], b7[:, 2], ACT.Copy).then_inc(s_te, 1)
                    act.activation(kwT[:, t], b7[:, 3], ACT.Copy).then_inc(s_te, 1)

                def keys_out(m):
                    act.wait_ge(s_tq, 11 + m)
                    act.activation(kmT[:, :, 128 * m:128 * m + 128],
                                   bank(7)[:, 0:256].rearrange("p (a b) -> p a b", a=2), ACT.Copy).then_inc(s_te, 1)

                for n in range(NT):
                    evacuate(n)
                    roots(n)
                    act.wait_ge(s_ze, 4 * n + 4)
                    act.activation(gates[0:ROWS[n], n], zt[0:ROWS[n], n % 2, 1536:WTOK], ACT.Sigmoid).then_inc(s_gn, 1)
                    if n >= 2:
                        heads_out(n - 2)
                for m in range(2):
                    evacuate_mem(m)
                    roots(NT + m)
                    heads_out(NT - 2 + m)
                for m in range(2):
                    keys_out(m)
                act.wait_ge(s_uz, 1)
                for k in range(2):
                    act.wait_ge(s_up, 2 * k + 1)
                    act.activation(u_prompt[:, k, 16:16 + HALF], bank(2 + 2 * k)[:, 0:HALF], ACT.Copy).then_inc(s_ue, 1)
                    act.wait_ge(s_up, 2 * k + 2)
                    b = bank(3 + 2 * k)
                    act.activation(u_prompt[:, k, 16 + HALF:], b[:, 0:NP_TOK - HALF], ACT.Copy).then_inc(s_ue, 1)
                    act.activation(u_sample[:, k, :, 16:], b[:, NP_TOK - HALF:HALF].rearrange("p (s t) -> p s t", t=TS),
                                   ACT.Copy).then_inc(s_ue, 1)
                    act.activation(u_new[:, k], b[:, NP_TOK - HALF:HALF], ACT.Copy).then_inc(s_ue, 1)
                for k in range(2):
                    act.wait_ge(s_ht, k + 1)
                    act.activation(u_sample[:, k, :, 1:16], bank(6 + k)[:, 0:120].rearrange("p (s t) -> p s t", t=15),
                                   ACT.Copy).then_inc(s_he, 1)
                act.wait_ge(s_ht, 3)
                act.activation(u_rows[0:15, 0], bank(0)[0:15, 0:256], ACT.Copy).then_inc(s_he, 1)
                act.wait_ge(s_ht, 4)
                act.activation(u_rows[0:32, 1], bank(1)[0:32, 0:256], ACT.Copy).then_inc(s_he, 1)
                for k in range(2):
                    for h in range(2):
                        act.wait_ge(s_pp, 2 * k + h + 1)
                        act.activation(oT_pool[:, k, h * HALF:(h + 1) * HALF], bank(2 + 2 * k + h)[:, 0:HALF], ACT.Copy,
                                       scale=psc[:, k:k + 1]).then_inc(s_po, 1)

            @block.vector
            def _(dve):
                link = linked(dve, s_dve, [0])
                dve.memset(ones, 1.0).then_inc(s_ones, 1)
                dve.memset(eps, EPS).then_inc(s_ones, 1)
                dve.wait_ge(s_const, 80)

                def norm(n):
                    r = rows_of(n)
                    dve.wait_ge(s_root, n + 1)
                    link(dve.reciprocal(rinv[0:r, n:n + 1], root[0:r, n:n + 1]))
                    if n >= 2:
                        dve.wait_ge(s_tp, 2 * n - 2)
                    dve.tensor_scalar(xn[0:r, n % 2], src(n), rinv[0:r, n:n + 1], None, ALU.mult).then_inc(s_xn, 1)

                def to_hT(n):
                    r = rows_of(n)
                    g = g1c if n < NT else gmc
                    for h in range(2):
                        dve.wait_ge(s_tp, 2 * n + h + 1)
                        dve.tensor_tensor(dstT(n)[:, 4 * h:4 * h + 4], bank(h)[:, 0:4 * r].rearrange("p (a b) -> p a b", a=4),
                                          g[:, 4 * h:4 * h + 4].unsqueeze(2).to_broadcast([128, 4, r]),
                                          ALU.mult).then_inc(s_hT, 1)

                def head_norm(n):
                    r = rows_of(n)
                    heads = 16 if n < NT else 4
                    z = zt[0:r, n % 2, 0:D] if n < NT else zm[:, n - NT, 0:256]
                    g = gain_rows[0:r, 0:D] if n < NT else gain_rows[0:r, D:D + 256]
                    zh = z.rearrange("p (h d) -> p h d", d=HD)
                    dve.wait_ge(s_sq, n + 1)
                    dve.tensor_reduce(ss16[0:r, 0:heads], zsq[0:r, 0:heads * HD].rearrange("p (h d) -> p h d", d=HD),
                                      AX, ALU.add).then_inc(s_ss, 1)
                    dve.wait_ge(s_rt, n + 1)
                    link(dve.reciprocal(ri16[0:r, 0:heads], rt16[0:r, 0:heads]))
                    link(dve.tensor_tensor(zh, zh, ri16[0:r, 0:heads].unsqueeze(2).to_broadcast([r, heads, HD]), ALU.mult))
                    dve.tensor_tensor(z, z, g, ALU.mult).then_inc(s_zn, 1)

                norm(0)
                for n in range(1, 7):
                    norm(n)
                    to_hT(n - 1)
                    if n >= 3:
                        head_norm(n - 3)
                to_hT(6)
                for n in range(4, 7):
                    head_norm(n)
                dve.wait_ge(s_zp, 22)
                dve.memset(u_prompt[:, :, 0:16], 0.0).then_inc(s_uz, 1)
                dve.wait_ge(s_ue, 8)
                dve.wait_ge(s_he, 2)
                dve.wait_ge(s_pl, 48)
                dve.wait_ge(s_uz, 1)
                u, a, b = u_prompt, sum_a, sum_b
                us, sa, sb_ = u_sample, ssum_a, ssum_b
                W = 16 + NP_TOK
                WS = 16 + TS
                link(dve.tensor_tensor(a[:, :, 1:W], u[:, :, 1:W], u[:, :, 0:W - 1], ALU.add))
                link(dve.tensor_tensor(b[:, :, 3:W], a[:, :, 3:W], a[:, :, 1:W - 2], ALU.add))
                link(dve.tensor_copy(a[64:128, 0, 16:W], b[64:128, 0, 16:W]))
                link(dve.tensor_tensor(a[:, 1, 7:W], b[:, 1, 7:W], b[:, 1, 3:W - 4], ALU.add))
                link(dve.tensor_tensor(b[:, 1, 15:W], a[:, 1, 15:W], a[:, 1, 7:W - 8], ALU.add))
                link(dve.tensor_copy(a[64:128, 1, 16:W], b[64:128, 1, 16:W]))
                link(dve.tensor_tensor(a[:, :, 16:W], a[:, :, 16:W], inv_count, ALU.mult))
                dve.tensor_tensor(dT[:, :, 0:NP_TOK], a[:, :, 16:W], u[:, :, 16:W], ALU.subtract).then_inc(s_dT, 1)
                for k in range(2):
                    x_, y_, z_ = us[:, k], sa[:, k], sb_[:, k]
                    link(dve.tensor_tensor(y_[:, :, 2:WS], x_[:, :, 2:WS], x_[:, :, 1:WS - 1], ALU.add))
                    link(dve.tensor_tensor(z_[:, :, 4:WS], y_[:, :, 4:WS], y_[:, :, 2:WS - 2], ALU.add))
                    if k == 0:
                        link(dve.tensor_copy(y_[64:128, :, 16:WS], z_[64:128, :, 16:WS]))
                    else:
                        link(dve.tensor_tensor(y_[:, :, 8:WS], z_[:, :, 8:WS], z_[:, :, 4:WS - 4], ALU.add))
                        link(dve.tensor_tensor(z_[64:128, :, 16:WS], y_[64:128, :, 16:WS], y_[64:128, :, 8:WS - 8], ALU.add))
                        link(dve.tensor_copy(y_[64:128, :, 16:WS], z_[64:128, :, 16:WS]))
                    for h in range(2):
                        q = slice(64 * h, 64 * h + 64)
                        link(dve.tensor_scalar(z_[q, :, 16:WS], y_[q, :, 16:WS], 1.0 / (2, 4, 8, 16)[2 * k + h], None, ALU.mult))
                    dve.tensor_tensor(dT[:, k, NP_TOK:].rearrange("p (s t) -> p s t", t=TS), z_[:, :, 16:WS],
                                      x_[:, :, 16:WS], ALU.subtract).then_inc(s_dT, 1)

            @block.gpsimd
            def _(pool):
                for n in range(NT + 2):
                    r = rows_of(n)
                    if n:
                        pool.wait_ge(s_ss, n)
                    if n == 0:
                        pool.wait_ge(s_root, 7)
                    if n < NT:
                        pool.wait_ge(s_ze, 4 * n + 2)
                        z = zt[0:r, n % 2, 0:D]
                        pool.tensor_tensor(zsq[0:r], z, z, ALU.mult).then_inc(s_sq, 1)
                        pool.wait_ge(s_ze, 4 * n + 3)
                        pool.tensor_copy(v_slc[0:r, n], zt[0:r, n % 2, 1280:1408])
                        pool.tensor_copy(v_win[0:r, n], zt[0:r, n % 2, 1408:1536]).then_inc(s_vc, 1)
                    else:
                        pool.wait_ge(s_ze, 16 + n)
                        z = zm[:, n - NT, 0:256]
                        pool.tensor_tensor(zsq[:, 0:256], z, z, ALU.mult).then_inc(s_sq, 1)

            @block.tensor
            def _(pe):
                pe.wait_ge(s_const, 80)

                def transposes(n):
                    r = rows_of(n)
                    pe.wait_ge(s_xn, n + 1)
                    for h in range(2):
                        if n:
                            pe.wait_ge(s_hT, 2 * n - 1 + h)
                        for k in range(4):
                            mm = pe.transpose(bank(h)[:, k * r:(k + 1) * r],
                                              xn[0:r, n % 2, (4 * h + k) * 128:(4 * h + k + 1) * 128], ident[0:r, 0:r])
                        mm.then_inc(s_tp, 1)

                def project(n):
                    r = rows_of(n)
                    pe.wait_ge(s_hT, 2 * n + 2)
                    if n < NT:
                        if n == 0:
                            pe.wait_ge(s_wtok, 64)
                        for c, (a, b) in enumerate(CH):
                            if n:
                                pe.wait_ge(s_ze, 4 * n - 3 + c)
                            for k in range(KD):
                                mm = pe.matmul(bank(2 + c)[0:r, 0:b - a], dstT(n)[:, k], w_tok[:, k, a:b],
                                               start=(k == 0), stop=(k == KD - 1))
                            mm.then_inc(s_zp, 1)
                    else:
                        if n == NT:
                            pe.wait_ge(s_wmem, 32)
                        pe.wait_ge(s_ze, 17 + n - NT)
                        for k in range(KD):
                            mm = pe.matmul(bank(2 + n - NT), dstT(n)[:, k], w_mem[:, k], start=(k == 0), stop=(k == KD - 1))
                        mm.then_inc(s_zp, 1)

                def heads(n):
                    pe.wait_ge(s_zn, n + 1)
                    if n < NT:
                        r = ROWS[n]
                        z = zt[0:r, n % 2]
                        if n:
                            pe.wait_ge(s_te, 4 * n - 3)
                        for p in range(4):
                            mm = pe.transpose(bank(6)[:, p * r:(p + 1) * r], z[:, p * 128:p * 128 + 128], ident[0:r, 0:r])
                        mm.then_inc(s_tq, 1)
                        if n:
                            pe.wait_ge(s_te, 4 * n)
                        for p in range(4):
                            mm = pe.transpose(bank(7)[:, p * r:(p + 1) * r], z[:, 512 + p * 128:640 + p * 128],
                                              ident[0:r, 0:r])
                        mm.then_inc(s_tq, 1)
                    else:
                        pe.wait_ge(s_te, 20 + n - NT)
                        for p in range(2):
                            mm = pe.transpose(bank(7)[:, p * 128:(p + 1) * 128], zm[:, n - NT, p * 128:p * 128 + 128], ident)
                        mm.then_inc(s_tq, 1)

                transposes(0)
                for n in range(1, 7):
                    transposes(n)
                    project(n - 1)
                    if n >= 3:
                        heads(n - 3)
                project(6)
                for n in range(4, 7):
                    heads(n)
                pe.wait_ge(s_ze, 22)
                for k in range(2):
                    for h in range(2):
                        for kk in range(KD):
                            mm = pe.matmul(bank(2 + 2 * k + h)[:, 0:HALF], w_u[:, kk, k * 128:k * 128 + 128],
                                           hT[:, kk, h * HALF:(h + 1) * HALF], start=(kk == 0), stop=(kk == KD - 1))
                        mm.then_inc(s_up, 1)
                pe.wait_ge(s_te, 22)
                pe.wait_ge(s_pl, 48)
                for k in range(2):
                    pe.transpose(bank(6 + k)[:, 0:120], hist[0:120, k * 128:k * 128 + 128], ident[0:120, 0:120]
                                 ).then_inc(s_ht, 1)
                pe.wait_ge(s_ue, 8)
                for k in range(2):
                    mm = pe.transpose(bank(0)[0:15, k * 128:k * 128 + 128], u_prompt[:, k, 16 + NP_TOK - 15:], ident)
                mm.then_inc(s_ht, 1)
                for k in range(2):
                    mm = pe.transpose(bank(1)[0:32, k * 128:k * 128 + 128], u_new[:, k], ident)
                mm.then_inc(s_ht, 1)
                pe.wait_ge(s_dT, 3)
                for k in range(2):
                    for h in range(2):
                        pe.matmul(bank(2 + 2 * k + h)[:, 0:HALF], w_pool[:, k], dT[:, k, h * HALF:(h + 1) * HALF],
                                  start=True, stop=True).then_inc(s_pp, 1)

        phase_over()
        cursor[0] = phase_base
        pages = take(NS, dt=I32)
        row_index = take(NS, dt=U32)
        gain_kc = take(128)
        w_cmp = take(2, 8, 128)
        pe_cmp = take(2, 8, 2)
        pe_bias = take(2)
        sub_rows = take(2, ROWF)
        kvT = take(2, 8, 2, 128)
        parts = take(2, 2, 128)
        kc_sq = take(128)
        kn = take(128)
        kc_ss, kc_rt, kc_ri = take(2), take(2), take(2)

        s_cw = sem("s_cw")
        s_subp = sem("s_subp")
        s_ix = sem("s_ix")
        s_sub = [sem(f"s_sub{n}") for n in range(2)]
        s_ct = sem("s_ct")
        s_kv = sem("s_kv")
        s_cw_mm = sem("s_cw_mm")
        s_pa = sem("s_pa")
        s_bl = sem("s_bl")
        s_kq = sem("s_kq")
        s_ksum = sem("s_ksum")
        s_kr = sem("s_kr")
        s_kn = sem("s_kn")
        s_vcm = sem("s_vcm")
        s_kt = sem("s_kt")
        s_kc = sem("s_kc")
        s_pb = sem("s_pb")
        s_pbe = sem("s_pbe")
        s_d2 = sem("s_d2")

        subs = lambda s: NSUB if s < NS else NP_TOK // SUB

        with nc.Block() as block:
            @block.sync
            def _(sp):
                sp.dma_start(pages, i["pages"]).then_inc(s_cw, 16)
                sp.dma_start(gain_kc, i["gain_rows"][:, 1280:1408].partition_broadcast(128)
                             .rearrange("p a n -> p (a n)")).then_inc(s_cw, 16)
                sp.dma_start(w_cmp, i["w_cmp"].rearrange("p (c j m) -> p c j m", c=2, j=8)).then_inc(s_cw, 16)
                sp.dma_start(pe_cmp, i["pe_cmp"].rearrange("p (c j r) -> p c j r", c=2, j=8)).then_inc(s_cw, 16)
                sp.wait_ge(s_ct, 8 * 7)
                sp.dma_start(sub_rows[0:32, 0], out_cp.rearrange("(n t) c -> n (t c)", t=SUB)).then_inc(s_subp, 16)

            @block.gpsimd
            def _(pool):
                pool.wait_ge(s_ix, 1)
                for s in range(NS):
                    if s >= 2:
                        pool.wait_ge(s_ct, 8 * (s - 1))
                    pool.indirect_dma_start(sub_rows[:, s % 2], None, i["cache_cmp"],
                                            bass.IndirectOffsetOnAxis(row_index[:, s:s + 1], 0)
                                            ).then_inc(s_sub[s % 2], 16)

            def copy_group(eng, copy, s, c, q):
                n = subs(s)
                eng.wait_ge(s_ct, 8 * s + 4 * c + q + 1)
                if s:
                    eng.wait_ge(s_cw_mm, 2 * s - 1 + c)
                b = bank(q)[:, 0:4 * n].rearrange("p (j a n) -> p j a n", j=2, a=2)
                for g in range(2):
                    for a in range(2):
                        copy(kvT[64 * a:64 * a + 64, c, 2 * q:2 * q + 2, g, 0:n],
                             b[64 * g:64 * g + 64, :, a]).then_inc(s_kv, 1)

            @block.scalar
            def _(act):
                act.wait_ge(s_pb, 1)
                for r in range(2):
                    q = slice(64 * r, 64 * r + 64)
                    act.activation(pe_bias[q, :], bank(7)[q, 0:4].rearrange("p (c r) -> p r c", r=2)[:, r],
                                   ACT.Copy).then_inc(s_pbe, 1)
                act.wait_ge(s_pbe, 2)
                cp = lambda a, b: act.activation(a, b, ACT.Copy)

                def after(s):
                    n = subs(s) - 1
                    act.wait_ge(s_bl, s + 1)
                    if s:
                        act.wait_ge(s_ksum, s)
                    act.activation(kc_sq[0:n], bank(6)[0:n, 0:128], ACT.Square).then_inc(s_kq, 1)
                    act.activation(v_cmp[0:n, s], bank(6)[0:n, 128:256], ACT.Copy).then_inc(s_vcm, 1)
                    act.wait_ge(s_ksum, s + 1)
                    act.activation(kc_rt[0:n], kc_ss[0:n], ACT.Sqrt, bias=eps[0:n], scale=1.0 / HD).then_inc(s_kr, 1)
                    act.wait_ge(s_kt, s + 1)
                    act.activation(kcT[:, s, 0:n], bank(7)[:, 0:n], ACT.Copy).then_inc(s_kc, 1)

                for s in range(NS + 1):
                    for c in range(2):
                        for q in (0, 2):
                            copy_group(act, cp, s, c, q)
                        if c == 0 and s:
                            after(s - 1)
                    for c in range(2):
                        act.wait_ge(s_cw_mm, 2 * s + c + 1)
                        if s:
                            act.wait_ge(s_bl, s)
                        act.activation(parts[:, c, :, 0:subs(s)],
                                       bank(4 + c)[:, 0:2 * subs(s)].rearrange("p (g n) -> p g n", g=2),
                                       ACT.Identity, bias=pe_bias[:, c:c + 1]).then_inc(s_pa, 1)
                after(NS)

            @block.vector
            def _(dve):
                link = linked(dve, s_d2, [0])
                dve.wait_ge(s_cw, 64)
                dve.tensor_scalar(row_index, pages, float(PAGE // SUB), cols[:, 1:2], ALU.mult,
                                  ALU.add).then_inc(s_ix, 1)
                cp = dve.tensor_copy

                def after(s):
                    n = subs(s) - 1
                    heads = lambda ap: ap.rearrange("p (g d) -> p g d", g=2)
                    dve.wait_ge(s_kq, s + 1)
                    dve.tensor_reduce(kc_ss[0:n], heads(kc_sq[0:n]), AX, ALU.add).then_inc(s_ksum, 1)
                    dve.wait_ge(s_kr, s + 1)
                    link(dve.reciprocal(kc_ri[0:n], kc_rt[0:n]))
                    if s:
                        dve.wait_ge(s_kt, s)
                    link(dve.tensor_tensor(heads(kn[0:n]), heads(bank(6)[0:n, 0:128]),
                                           kc_ri[0:n].unsqueeze(2).to_broadcast([n, 2, HD]), ALU.mult))
                    dve.tensor_tensor(kn[0:n], kn[0:n], gain_kc[0:n], ALU.mult).then_inc(s_kn, 1)

                for s in range(NS + 1):
                    for c in range(2):
                        for q in (1, 3):
                            copy_group(dve, cp, s, c, q)
                        if c == 0 and s:
                            after(s - 1)
                after(NS)

            @block.tensor
            def _(pe):
                pe.wait_ge(s_cw, 64)
                for c in range(2):
                    for j in range(8):
                        mm = pe.matmul(bank(7)[:, 2 * c:2 * c + 2], w_cmp[:, c, j], pe_cmp[:, c, j],
                                       start=(j == 0), stop=(j == 7))
                mm.then_inc(s_pb, 1)

                def tokens(s, c):
                    n = subs(s)
                    if c == 0:
                        pe.wait_ge(*((s_sub[s % 2], 16 * (s // 2 + 1)) if s < NS else (s_subp, 16)))
                    rows = sub_rows[0:n, s % 2].rearrange("p (t c f) -> p t c f", t=SUB, c=2)
                    for q in range(4):
                        group = 8 * s + 4 * c + q
                        if group >= 4:
                            pe.wait_ge(s_kv, 16 * (group // 4))
                        for t in range(4):
                            mm = pe.transpose(bank(q)[:, t * n:(t + 1) * n], rows[:, 4 * q + t, c], ident[0:n, 0:n])
                        mm.then_inc(s_ct, 1)

                def products(s, c):
                    n = subs(s)
                    pe.wait_ge(s_kv, 16 * (2 * s + c + 1))
                    if s:
                        pe.wait_ge(s_pa, 2 * s - 1 + c)
                    for j in range(8):
                        mm = pe.matmul(bank(4 + c)[:, 0:2 * n].rearrange("p (g n) -> p g n", g=2), w_cmp[:, c, j],
                                       kvT[:, c, j, :, 0:n], start=(j == 0), stop=(j == 7))
                    mm.then_inc(s_cw_mm, 1)

                def blocks(s):
                    n = subs(s) - 1
                    pe.wait_ge(s_pa, 2 * s + 2)
                    if s:
                        pe.wait_ge(s_kn, s)
                        pe.wait_ge(s_vcm, s)
                    for c in range(2):
                        for g in range(2):
                            out = bank(6)[0:n, 128 * c + 64 * g:128 * c + 64 * g + 64]
                            pe.matmul(out, parts[:, c, g, 0:n], ident[:, 0:64], start=True, stop=False)
                            mm = pe.matmul(out, parts[:, c, g, 1:n + 1], ident[:, 64:128], start=False, stop=True)
                    mm.then_inc(s_bl, 1)

                def keys(s):
                    n = subs(s) - 1
                    pe.wait_ge(s_kn, s + 1)
                    if s:
                        pe.wait_ge(s_kc, s)
                    else:
                        pe.wait_ge(s_pbe, 2)
                    pe.transpose(bank(7)[:, 0:n], kn[0:n], ident[0:n, 0:n]).then_inc(s_kt, 1)

                for s in range(NS + 1):
                    tokens(s, 0)
                    if s:
                        blocks(s - 1)
                    tokens(s, 1)
                    if s:
                        keys(s - 1)
                    for c in range(2):
                        products(s, c)
                blocks(NS)
                keys(NS)

        phase_over()
        cursor[0] = phase_base + 16
        rel_rows = take(128)
        rel4 = take(8)
        oh_cmp = take(NCMP_S)
        oh_new = take(32)
        mask_new = take(2, 32)
        covers = take(33)
        force = take(33)
        bias_cmp = take(128)
        bias_new = take(2, 32)
        bias_win = take(512)
        bias_slc = take(PAST)
        q_rows = take(NS, 32)
        qm_rows = take(2, NS, 32)
        gate_rows = take(2, 3)
        cache = take(4, ROWF)
        keysT = take(PAST)
        scores = take(PAST + 32)
        probT = take(17, 128)
        o_rows = take(128)
        p_cmp = take(128)
        p_sum = take(32)
        p_exp = take(128)
        pick = take(4, 33)
        top8 = take(8)
        top8b = take(8)
        stats = take(16)
        oh_slc = scores[:, 0:PAST]
        oh_win = keysT[:, 0:512]

        gate_scratch = scratch("gate_scratch", [NS * NH * TS, 3])

        s_sc = sem("s_sc")
        s_gs = sem("s_gs")
        s_gl = sem("s_gl")
        s_rr = sem("s_rr")
        s_bp = sem("s_bp")
        s_be = sem("s_be")
        s_qr = sem("s_qr")
        s_cs = [sem(f"s_cs{n}") for n in range(4)]
        s_wl = sem("s_wl")
        s_tk = sem("s_tk")
        s_ke = sem("s_ke")
        s_sp = sem("s_sp")
        s_sr = sem("s_sr")
        s_mx = sem("s_mx")
        s_ex = sem("s_ex")
        s_pt = sem("s_pt")
        s_pe_ = sem("s_pe")
        s_op = sem("s_op")
        s_or = sem("s_or")
        s_im = sem("s_im")
        s_px = sem("s_px")
        s_ot = sem("s_ot")
        s_oe = sem("s_oe")
        s_d3 = sem("s_d3")
        s_pcn = sem("s_pcn")

        C, S, W_, M = range(4)

        with nc.Block() as block:
            @block.sync
            def _(sp):
                for s in range(NS):
                    sp.dma_start(gate_scratch[32 * s:32 * s + 32].rearrange("(h t) n -> t h n", h=NH),
                                 gates[4 * s:4 * s + 4, 4].rearrange("t (h n) -> t h n", n=3)
                                 ).then_inc(s_gs, 16)
                for t in range(TS):
                    sp.dma_start(rel4[32 * t:32 * t + 32], i["rel_bias"]).then_inc(s_sc, 16)
                for dst, name in ((oh_cmp, "c_oh_cmp"), (oh_new, "c_oh_new"), (covers[0:NCMP_S], "c_covers"),
                                  (force, "c_force"), (oh_slc, "c_oh_slc"), (oh_win, "c_oh_win"),
                                  (bias_win, "c_mask_win")):
                    sp.dma_start(dst, i[name]).then_inc(s_sc, 16)
                sp.dma_start(mask_new, i["c_mask_new"].rearrange("p (r c) -> p r c", r=2)).then_inc(s_sc, 16)
                sp.wait_ge(s_gs, 16 * NS)
                sp.dma_start(gate_rows, gate_scratch.rearrange("(r p) n -> p r n", r=2)).then_inc(s_gl, 16)
                for r in range(2):
                    sp.wait_ge(s_op, 4 * r + 2)
                    for s in range(4):
                        sp.dma_start(cache[:, s, 0:1024], i["cache_win"][4 * r + s].rearrange("(p a) c -> p (a c)", p=128)
                                     ).then_inc(s_wl, 16)
                        sp.dma_start(cache[:, s, 1024:2048],
                                     i["cache_mem"][4 * r + s].rearrange("(p a) c -> p (a c)", p=128)).then_inc(s_wl, 16)

            @block.gpsimd
            def _(pool):
                for r in range(2):
                    if r:
                        pool.wait_ge(s_op, 4)
                    for s in range(4):
                        pool.indirect_dma_start(cache[:, s], None, i["cache_slc"],
                                                bass.IndirectOffsetOnAxis(row_index[:, 4 * r + s:4 * r + s + 1], 0)
                                                ).then_inc(s_cs[s], 16)

            def groups():
                for r in range(2):
                    for b, per in ((S, 4), (W_, 1), (M, 1)):
                        for s in range(4):
                            for q in range(per):
                                yield r, b, s, q
            GROUPS = list(groups())

            def copies_keys(eng, copy, mine):
                def run(r, b):
                    for n, (r_, b_, s, q) in enumerate(GROUPS):
                        if (r_, b_) != (r, b):
                            continue
                        if n % 2 == mine:
                            eng.wait_ge(s_tk, n + 1)
                            if n >= 1:
                                eng.wait_ge(s_sp, score_count(n))
                            dst = keysT[:, 512 * q:512 * q + 512] if b == S else keysT[:, 512 * (s % 4):512 * (s % 4) + 512]
                            copy(dst, bank(5 + n % 2)).then_inc(s_ke_of[mine], 1)
                return run
            s_ke_of = [sem("s_ke_act"), sem("s_ke_dve")]

            def score_count(n):
                r, b, s, q = GROUPS[n]
                if b == S:
                    base = SP0 * r + 1
                    if s == 0:
                        return SP0 * r if r else 1
                    return base + 4 * (s - 1) + q + 1
                if b == W_:
                    return SP0 * r + 1 + 16 + 1
                return SP0 * r + 1 + 16 + 1 + s + 1
            SP0 = 27

            @block.scalar
            def _(act):
                copy = lambda a, b: act.activation(a, b, ACT.Copy)
                keys = copies_keys(act, copy, 0)

                def exponentials(k, cols, r):
                    act.wait_ge(s_mx, k + 1)
                    act.activation(scores[:, 0:cols], scores[:, 0:cols], ACT.Exp, bias=stats[:, 4 * (k % 4):4 * (k % 4) + 1],
                                   accum_out=stats[:, 4 * (k % 4) + 1:4 * (k % 4) + 2]).then_inc(s_ex, 1)

                for r in range(2):
                    k = 4 * r
                    act.wait_ge(s_mx, k + 1)
                    act.activation(p_cmp[:, 0:NCMP_S], p_cmp[:, 0:NCMP_S], ACT.Exp, bias=stats[:, 0:1],
                                   accum_out=stats[:, 1:2]).then_inc(s_ex, 1)
                    keys(r, S)
                    exponentials(k + 1, PAST + 32, r)
                    keys(r, W_)
                    exponentials(k + 2, 512 + 32, r)
                    keys(r, M)
                    exponentials(k + 3, MEM, r)
                    act.wait_ge(s_ot, 2 * r + 1)
                    for g in range(2):
                        q = slice(64 * g, 64 * g + 64)
                        rows = bank(7)[q, 0:128].rearrange("d (s p g t) -> d g p s t", s=4, p=4, g=2)[:, g]
                        for p in range(4):
                            act.activation(oT_nsa[q, p, NP_TOK + 16 * r:NP_TOK + 16 * r + 16].rearrange("d (s t) -> d s t", s=4),
                                           rows[:, p], ACT.Copy).then_inc(s_oe, 1)
                    act.wait_ge(s_ot, 2 * r + 2)
                    for mp in range(2):
                        for m2 in range(2):
                            q = slice(64 * m2, 64 * m2 + 64)
                            rows = bank(7)[q, 128 + 128 * mp:256 + 128 * mp].rearrange("d (s m t) -> d m s t", s=4, t=4)
                            act.activation(oT_mem[q, mp, NP_TOK + 16 * r:NP_TOK + 16 * r + 16].rearrange("d (s t) -> d s t", s=4),
                                           rows[:, 2 * mp + m2], ACT.Copy).then_inc(s_oe, 1)

            @block.vector
            def _(dve):
                link = linked(dve, s_d3, [0])
                copy = dve.tensor_copy
                keys = copies_keys(dve, copy, 1)
                dve.wait_ge(s_sc, 16 * 12)
                link(dve.memset(rel_rows, 0.0))
                for t in range(TS):
                    q = slice(32 * t, 32 * t + 32)
                    dst = rel_rows[q].rearrange("b (s h t) -> b t s h", s=4, t=TS)[:, t]
                    dve.tensor_copy(dst, rel4[q].unsqueeze(1).to_broadcast([32, 4, 8])).then_inc(s_rr, 1)
                link(dve.memset(q_rows, 0.0))
                link(dve.memset(qm_rows, 0.0))
                for g in range(2):
                    q = slice(64 * g, 64 * g + 64)
                    for s in range(NS):
                        src = qT[q, :, NP_TOK + 4 * s:NP_TOK + 4 * s + 4]
                        dst = q_rows[q, s].rearrange("d (p g t) -> d g p t", p=4, g=2)[:, g]
                        dve.tensor_copy(dst, src).then_inc(s_qr, 1)
                for mp in range(2):
                    for m2 in range(2):
                        q = slice(64 * m2, 64 * m2 + 64)
                        m = 2 * mp + m2
                        dve.tensor_copy(qm_rows[q, mp, :, 4 * m:4 * m + 4],
                                        qmT[q, mp, NP_TOK:].rearrange("d (s t) -> d s t", t=4)).then_inc(s_qr, 1)
                dve.wait_ge(s_bp, 1)
                dve.tensor_copy(bias_slc.rearrange("p (b n) -> p b n", b=4), bank(0, 4)).then_inc(s_be, 1)
                dve.tensor_tensor(bias_win, bias_win, bank(4), ALU.add).then_inc(s_be, 1)
                dve.tensor_copy(bias_cmp[:, 0:NCMP_S], bank(5)[:, 0:NCMP_S]).then_inc(s_be, 1)
                dve.tensor_tensor(bias_new, mask_new, bank(6)[:, 0:32].unsqueeze(1).to_broadcast([128, 2, 32]),
                                  ALU.add).then_inc(s_be, 1)
                dve.wait_ge(s_be, 4)
                dve.wait_ge(s_gl, 16)

                def maximum(k, ap):
                    at = stats[:, 4 * (k % 4):4 * (k % 4) + 1]
                    dve.tensor_reduce(at, ap, AX, ALU.max, negate=True).then_inc(s_mx, 1)

                def reciprocal(k):
                    at = 4 * (k % 4)
                    dve.wait_ge(s_ex, k + 1)
                    link(dve.reciprocal(stats[:, at + 2:at + 3], stats[:, at + 1:at + 2]))

                def copy_probs(base, banks):
                    for n, (b, dst, width) in enumerate(banks):
                        dve.wait_ge(s_pt, base + n + 1)
                        dve.tensor_copy(dst, width(bank(b))).then_inc(s_pe_, 1)

                PT0 = 8
                four = lambda b: b.rearrange("p (a n) -> p a n", a=4)
                for r in range(2):
                    k = 4 * r
                    base = PT0 * r
                    dve.wait_ge(s_sp, SP0 * r + 1)
                    link(dve.tensor_tensor(p_cmp[:, 0:NCMP_S], bank(4)[:, 0:NCMP_S], bias_cmp[:, 0:NCMP_S], ALU.add))
                    maximum(k, p_cmp[:, 0:NCMP_S])
                    reciprocal(k)
                    dve.tensor_scalar(p_cmp[:, 0:NCMP_S], p_cmp[:, 0:NCMP_S], stats[:, 2:3], None, ALU.mult).then_inc(s_pcn, 1)
                    dve.wait_ge(s_pt, base + 1)
                    dve.tensor_copy(probT[0:NCMP_S, 0], bank(7)[0:NCMP_S, 0:128]).then_inc(s_pe_, 1)
                    dve.wait_ge(s_pe_, 9 * r + 1)
                    rows = probT[0:NCMP_S, 0].rearrange("n (s p q) -> n s q p", s=4, p=4)
                    link(dve.tensor_reduce(p_sum[0:NCMP_S].rearrange("n (s q) -> n s q", s=4), rows, AX, ALU.add))
                    for p in range(4):
                        ins = dve.tensor_copy(p_exp[0:NCMP_S].rearrange("n (s p q) -> n p s q", s=4, p=4)[:, p],
                                              p_sum[0:NCMP_S].rearrange("n (s q) -> n s q", s=4))
                        ins.then_inc(s_px, 1)
                    dve.wait_ge(s_im, r + 1)
                    link(dve.tensor_tensor(pick[:, 0], bank(7)[:, 128:161], force, ALU.add))
                    link(dve.max(top8, pick[:, 0]))
                    link(dve.match_replace(pick[:, 1], top8, pick[:, 0], -1.0))
                    link(dve.max(top8b, pick[:, 1]))
                    link(dve.match_replace(pick[:, 2], top8b, pick[:, 1], -1.0))
                    link(dve.tensor_tensor(pick[:, 3], pick[:, 0], pick[:, 2], ALU.is_equal))
                    link(dve.tensor_scalar(pick[:, 3], pick[:, 3], NEG, None, ALU.mult))
                    if r == 0:
                        dve.wait_ge(s_bp, 1)
                    else:
                        dve.wait_ge(s_ot, 2 * r)
                    blocks_of = lambda ap: ap.rearrange("p (a j k) -> p a j k", a=SUB, k=4)
                    link(dve.tensor_tensor(blocks_of(scores[:, 0:PAST]), blocks_of(bias_slc),
                                           pick[:, 3, 0:32].unsqueeze(1).unsqueeze(3).to_broadcast([128, SUB, 32, 4]),
                                           ALU.add))
                    dve.wait_ge(s_op, 4 * r + 1)
                    dve.tensor_scalar(o_rows, bank(4)[:, 128:256], gate_rows[:, r, 0:1], None,
                                      ALU.mult).then_inc(s_or, 1)
                    keys(r, S)
                    for q in range(4):
                        dve.wait_ge(s_sp, SP0 * r + 1 + 12 + q + 1)
                        sl = scores[:, 512 * q:512 * q + 512]
                        link(dve.tensor_tensor(sl, bank(q), sl, ALU.add))
                    dve.wait_ge(s_sp, SP0 * r + 18)
                    link(dve.tensor_tensor(scores[:, PAST:], bank(4)[:, 256:288], bias_new[:, r], ALU.add))
                    maximum(k + 1, scores)
                    reciprocal(k + 1)
                    copy_probs(base + 1, [(5, probT[:, 0:4], four), (6, probT[:, 4:8], four), (5, probT[:, 8:12], four),
                                          (6, probT[:, 12:16], four), (7, probT[0:32, 16], lambda b: b[0:32, 0:128])])
                    link(dve.tensor_tensor(stats[:, 7:8], gate_rows[:, r, 1:2], stats[:, 6:7], ALU.mult))
                    dve.wait_ge(s_op, 4 * r + 2)
                    dve.wait_ge(s_or, 4 * r + 1)
                    dve.scalar_tensor_tensor(o_rows, bank(4)[:, 0:128], stats[:, 7:8], o_rows, ALU.mult,
                                             ALU.add).then_inc(s_or, 1)
                    dve.wait_ge(s_or, 4 * r + 2)
                    keys(r, W_)
                    dve.wait_ge(s_sp, SP0 * r + 18 + 5)
                    link(dve.tensor_tensor(scores[:, 0:512], bank(0), bias_win, ALU.add))
                    link(dve.tensor_tensor(scores[:, 512:544], bank(1)[:, 0:32], bias_new[:, r], ALU.add))
                    maximum(k + 2, scores[:, 0:544])
                    reciprocal(k + 2)
                    copy_probs(base + 6, [(2, probT[:, 0:4], four)])
                    dve.tensor_copy(probT[0:32, 16], bank(3)[0:32, 0:128]).then_inc(s_pe_, 1)
                    link(dve.tensor_tensor(stats[:, 11:12], gate_rows[:, r, 2:3], stats[:, 10:11], ALU.mult))
                    dve.wait_ge(s_op, 4 * r + 3)
                    dve.scalar_tensor_tensor(o_rows, bank(4)[:, 0:128], stats[:, 11:12], o_rows, ALU.mult,
                                             ALU.add).then_inc(s_or, 1)
                    keys(r, M)
                    dve.wait_ge(s_sp, SP0 * r + 27)
                    link(dve.tensor_copy(scores[:, 0:MEM], bank(1)[:, 256:512]))
                    maximum(k + 3, scores[:, 0:MEM])
                    reciprocal(k + 3)
                    dve.wait_ge(s_pt, base + 8)
                    dve.tensor_copy(probT[:, 0:2], bank(0)[:, 0:256].rearrange("p (a n) -> p a n", a=2)).then_inc(s_pe_, 1)
                    dve.wait_ge(s_op, 4 * r + 4)
                    dve.tensor_scalar(scores[:, 512:768], bank(2)[:, 0:256], stats[:, 14:15], None, ALU.mult).then_inc(s_or, 1)

            @block.tensor
            def _(pe):
                pe.wait_ge(s_sc, 16 * 12)
                pe.wait_ge(s_rr, 4)
                for q in range(4):
                    pe.matmul(bank(q), rel_rows, oh_slc[:, 512 * q:512 * q + 512], start=True, stop=True)
                pe.matmul(bank(4), rel_rows, oh_win, start=True, stop=True)
                pe.matmul(bank(5)[:, 0:NCMP_S], rel_rows, oh_cmp, start=True, stop=True)
                pe.matmul(bank(6)[:, 0:32], rel_rows, oh_new, start=True, stop=True).then_inc(s_bp, 1)
                pe.wait_ge(s_qr, 20)
                pe.wait_ge(s_be, 4)

                def keys_wait(n):
                    pe.wait_ge(s_ke_of[n % 2], n // 2 + 1)

                def transpose_keys(n):
                    r, b, s, q = GROUPS[n]
                    if b == S and q == 0:
                        pe.wait_ge(s_cs[s], 16 * (r + 1))
                    if n >= 2:
                        keys_wait(n - 2)
                    out = bank(5 + n % 2)
                    for a in range(4):
                        if b == S:
                            src = cache[:, s, (4 * q + a) * 256:(4 * q + a) * 256 + 128]
                        elif b == W_:
                            src = cache[:, s, a * 256:a * 256 + 128]
                        else:
                            mp, tok = a // 2, a % 2
                            src = cache[:, s, 1024 + 512 * tok + 128 * mp:1024 + 512 * tok + 128 * mp + 128]
                        mm = pe.transpose(out[:, 128 * a:128 * a + 128], src, ident)
                    mm.then_inc(s_tk, 1)

                def score(n):
                    r, b, s, q = GROUPS[n]
                    keys_wait(n)
                    seq = 4 * r + s
                    rows = slice(32 * s, 32 * s + 32)
                    if b == S:
                        pe.matmul(bank(q)[rows, :], q_rows[:, seq], keysT[:, 512 * q:512 * q + 512],
                                  start=True, stop=True, tile_position=(0, 32 * s)).then_inc(s_sp, 1)
                    elif b == W_:
                        pe.matmul(bank(0)[rows, :], q_rows[:, seq], keysT[:, 512 * s:512 * s + 512],
                                  start=True, stop=True, tile_position=(0, 32 * s)).then_inc(s_sp, 1)
                    else:
                        for mp in range(2):
                            mm = pe.matmul(bank(1)[rows, 256:512], qm_rows[:, mp, seq],
                                           keysT[:, 512 * s + 256 * mp:512 * s + 256 * mp + 256],
                                           start=(mp == 0), stop=(mp == 1), tile_position=(0, 32 * s))
                        mm.then_inc(s_sp, 1)

                def key_groups(r, b):
                    mine = [n for n, g in enumerate(GROUPS) if g[0] == r and g[1] == b]
                    transpose_keys(mine[0])
                    for n in mine[1:]:
                        transpose_keys(n)
                        score(n - 1)
                    score(mine[-1])

                for r in range(2):
                    q4 = q_rows[:, 4 * r:4 * r + 4].rearrange("p s q -> p (s q)")
                    if r:
                        pe.wait_ge(s_or, 4 * r)
                    for s in range(4):
                        mm = pe.matmul(bank(4)[32 * s:32 * s + 32, 0:NCMP_S], q_rows[:, 4 * r + s], kcT[:, 4 * r + s, 0:NCMP_S],
                                       start=True, stop=True, tile_position=(0, 32 * s))
                    mm.then_inc(s_sp, 1)
                    pe.wait_ge(s_pcn, r + 1)
                    if r:
                        pe.wait_ge(s_oe, 12)
                    pe.transpose(bank(7)[0:NCMP_S, 0:128], p_cmp[:, 0:NCMP_S], ident).then_inc(s_pt, 1)
                    pe.wait_ge(s_pe_, 9 * r + 1)
                    for s in range(4):
                        mm = pe.matmul(bank(4)[32 * s:32 * s + 32, 128:256], probT[0:NCMP_S, 0, 32 * s:32 * s + 32],
                                       v_cmp[0:NCMP_S, 4 * r + s], start=True, stop=True, tile_position=(0, 32 * s))
                    mm.then_inc(s_op, 1)
                    pe.wait_ge(s_px, 4 * r + 4)
                    pe.matmul(bank(7)[:, 128:161], p_exp[0:NCMP_S], covers[0:NCMP_S], start=True, stop=True).then_inc(s_im, 1)
                    pe.wait_ge(s_or, 4 * r + 1)
                    key_groups(r, S)
                    pe.matmul(bank(4)[:, 256:288], q4, ksT[:, NP_TOK:], start=True, stop=True).then_inc(s_sp, 1)
                    pe.wait_ge(s_ex, 4 * r + 2)
                    for q in range(4):
                        if q >= 2:
                            pe.wait_ge(s_pe_, 9 * r + q)
                        for a in range(4):
                            at = 128 * (4 * q + a)
                            mm = pe.transpose(bank(5 + q % 2)[:, 128 * a:128 * a + 128], scores[:, at:at + 128], ident)
                        mm.then_inc(s_pt, 1)
                    pe.transpose(bank(7)[0:32, 0:128], scores[:, PAST:], ident).then_inc(s_pt, 1)
                    pe.wait_ge(s_pe_, 9 * r + 6)
                    for s in range(4):
                        rows = slice(32 * s, 32 * s + 32)
                        pe.matmul(bank(4)[rows, 0:128], probT[0:32, 16, rows], v_slc[0:32, 4], start=True, stop=False,
                                  tile_position=(0, 32 * s))
                        for a in range(SUB):
                            mm = pe.matmul(bank(4)[rows, 0:128], probT[:, a, rows], cache[:, s, 256 * a + 128:256 * a + 256],
                                           start=False, stop=(a == SUB - 1), tile_position=(0, 32 * s))
                    mm.then_inc(s_op, 1)
                    pe.wait_ge(s_wl, 128 * (r + 1))
                    key_groups(r, W_)
                    pe.matmul(bank(1)[:, 0:32], q4, kwT[:, NP_TOK:], start=True, stop=True).then_inc(s_sp, 1)
                    pe.wait_ge(s_ex, 4 * r + 3)
                    for a in range(4):
                        pe.transpose(bank(2)[:, 128 * a:128 * a + 128], scores[:, 128 * a:128 * a + 128], ident)
                    pe.transpose(bank(3)[0:32, 0:128], scores[:, 512:544], ident).then_inc(s_pt, 1)
                    pe.wait_ge(s_pe_, 9 * r + 8)
                    pe.wait_ge(s_or, 4 * r + 2)
                    for s in range(4):
                        rows = slice(32 * s, 32 * s + 32)
                        pe.matmul(bank(4)[rows, 0:128], probT[0:32, 16, rows], v_win[0:32, 4], start=True, stop=False,
                                  tile_position=(0, 32 * s))
                        for a in range(4):
                            mm = pe.matmul(bank(4)[rows, 0:128], probT[:, a, rows], cache[:, s, 256 * a + 128:256 * a + 256],
                                           start=False, stop=(a == 3), tile_position=(0, 32 * s))
                    mm.then_inc(s_op, 1)
                    key_groups(r, M)
                    pe.wait_ge(s_ex, 4 * r + 4)
                    for a in range(2):
                        mm = pe.transpose(bank(0)[:, 128 * a:128 * a + 128], scores[:, 128 * a:128 * a + 128], ident)
                    mm.then_inc(s_pt, 1)
                    pe.wait_ge(s_pe_, 9 * r + 9)
                    for s in range(4):
                        rows = slice(32 * s, 32 * s + 32)
                        for a in range(2):
                            mm = pe.matmul(bank(2)[rows, 0:256], probT[:, a, rows],
                                           cache[:, s, 1024 + 512 * a + 256:1024 + 512 * a + 512],
                                           start=(a == 0), stop=(a == 1), tile_position=(0, 32 * s))
                    mm.then_inc(s_op, 1)
                    pe.wait_ge(s_or, 4 * r + 3)
                    pe.transpose(bank(7)[:, 0:128], o_rows, ident).then_inc(s_ot, 1)
                    pe.wait_ge(s_or, 4 * r + 4)
                    pe.wait_ge(s_oe, 12 * r + 8)
                    for mp in range(2):
                        mm = pe.transpose(bank(7)[:, 128 + 128 * mp:256 + 128 * mp], scores[:, 512 + 128 * mp:640 + 128 * mp], ident)
                    mm.then_inc(s_ot, 1)

        phase_over()
        cursor[0] = phase_base
        rel33 = take(8, 128)
        rel_sb = take(8)
        dist_desc = take(BIASL)
        dist_asc = take(CMPL)
        table = take(2, CMPL)
        table_c = take(2, CMPL)
        bias_q = take(8, NP_TOK)
        bias_b = take(8, NP_TOK)
        bias_c = take(4, 8, NCMP_P)
        sc_u = take(2, 512)
        pT_u = take(2, 512)
        stat_u = take(2, 2)
        sum_u = take(2, 16)
        coef = take(16)
        oa = take(8, HD)
        sc_f = take(8, HD)
        sc_c = take(8, NCMP_P)
        pT_c = take(8, 128)
        max_c, sum_c = take(8), take(8)
        p_m = take(4, MEM)
        pT_m = take(4, 2, 128)
        max_m, sum_m = take(4), take(4)
        om = take(4, HD)

        scr_desc = scratch("scr_desc", [8, 128 * BIASL])
        scr_asc = scratch("scr_asc", [8, NCMP_P * CMPL])

        s_bi = sem("s_bi")
        s_r3 = sem("s_r3")
        s_tb = sem("s_tb")
        s_te1 = sem("s_te1")
        s_te2 = sem("s_te2")
        s_ts = [sem(f"s_ts{n}") for n in range(2)]
        s_tl = sem("s_tl")
        s_bt = sem("s_bt")
        s_bc = sem("s_bc")
        u_sp, u_mx, u_ex, u_tp, u_pt, u_op = (sem(n) for n in ("u_sp", "u_mx", "u_ex", "u_tp", "u_pt", "u_op"))
        c_sp, c_mx, c_ex, c_pn, c_tp, c_pt, c_op, c_oa = (sem("c_" + n) for n in
                                                          ("sp", "mx", "ex", "pn", "tp", "pt", "op", "oa"))
        m_sp, m_mx, m_ex, m_tp, m_pt, m_op, m_nm, m_ot, m_oe = (sem("m_" + n) for n in
                                                                ("sp", "mx", "ex", "tp", "pt", "op", "nm", "ot", "oe"))
        f_oa, f_ot, f_oe = sem("f_oa"), sem("f_ot"), sem("f_oe")
        s_d4 = sem("s_d4")

        TILES = NP_TOK // 128
        UNITS = [(t, hh, b) for t in range(TILES) for hh in range(NH) for b in range(2)]
        PER = 2 * NH
        STEPS = len(UNITS) + 6

        def due(step, at, late=0):
            t = step // PER - late
            return t if step % PER == at and 0 <= t < TILES else None

        with nc.Block() as block:
            @block.sync
            def _(sp):
                sp.dma_start(rel_sb[0:32], i["rel_bias"]).then_inc(s_bi, 16)
                sp.dma_start(dist_desc[0:33], i["c_dist_desc"]).then_inc(s_bi, 16)
                sp.dma_start(dist_asc[0:33], i["c_dist_asc"]).then_inc(s_bi, 16)
                for h in range(NH):
                    sp.wait_ge(s_te1, h + 1)
                    sp.dma_start(scr_desc[h].rearrange("(p m) -> p m", p=128), table[:, h % 2, 0:BIASL]
                                 ).then_inc(s_ts[h % 2], 16)
                    sp.wait_ge(s_te2, h + 1)
                    sp.dma_start(scr_asc[h].rearrange("(p m) -> p m", p=NCMP_P), table_c[0:NCMP_P, h % 2]
                                 ).then_inc(s_ts[h % 2], 16)
                sp.wait_ge(s_ts[0], 128)
                sp.wait_ge(s_ts[1], 128)
                for h in range(NH):
                    sp.dma_start(bias_q[:, h], scr_desc[h][127:127 + 128 * (BIASL - 1)]
                                 .rearrange("(p m) -> p m", p=128)[:, 0:NP_TOK]).then_inc(s_tl, 16)
                    sp.dma_start(bias_b[0:NCMP_P, h], scr_asc[h][480:480 + NCMP_P * (CMPL - 16)]
                                 .rearrange("(p m) -> p m", p=NCMP_P)[:, 0:NP_TOK]).then_inc(s_tl, 16)

            @block.gpsimd
            def _(pool):
                pool.wait_ge(s_bi, 48)

            @block.scalar
            def _(act):
                copy = lambda a, b, **k: act.activation(a, b, ACT.Copy, **k)
                for h in range(NH):
                    act.wait_ge(s_tb, h + 1)
                    if h >= 2:
                        act.wait_ge(s_ts[h % 2], 32 * (h // 2))
                    copy(table[:, h % 2, 0:BIASL], psum[:, 2 * (h % 2):2 * (h % 2) + 2].rearrange("p b n -> p (b n)")[:, 0:BIASL]
                         ).then_inc(s_te1, 1)
                for t in range(TILES):
                    act.wait_ge(s_bt, t + 1)
                    copy(bias_c[:, t], bank(t)[:, 0:8 * NCMP_P].rearrange("p (h n) -> p h n", h=8)).then_inc(s_bc, 1)
                for step in range(STEPS):
                    u = step
                    if u < len(UNITS):
                        t, hh, b = UNITS[u]
                        w = 128 * (t + 1)
                        act.wait_ge(u_mx, u + 1)
                        if hh == 0 and b == 0 and t >= 2:
                            act.wait_ge(f_oa, t - 1)
                        act.activation(sc_u[:, u % 2, 0:w], sc_u[:, u % 2, 0:w], ACT.Exp, bias=stat_u[:, u % 2, 0:1],
                                       accum_out=sum_u[:, t % 2, 8 * b + hh:8 * b + hh + 1]).then_inc(u_ex, 1)
                    u = step - 1
                    if 0 <= u < len(UNITS):
                        w = 128 * (UNITS[u][0] + 1)
                        act.wait_ge(u_tp, u + 1)
                        if u >= 2:
                            act.wait_ge(u_op, u - 1)
                        copy(pT_u[:, u % 2, 0:w], bank(2 + u % 2)[:, 0:w]).then_inc(u_pt, 1)
                    if (t := due(step, 4, 1)) is not None:
                        act.wait_ge(f_ot, t + 1)
                        copy(oT_nsa[:, :, 128 * t:128 * t + 128], bank(6).rearrange("p (a n) -> p a n", a=4)).then_inc(f_oe, 1)
                    if (t := due(step, 6)) is not None:
                        act.wait_ge(c_mx, t + 1)
                        act.activation(sc_c, sc_c, ACT.Exp).then_inc(c_ex, 1)
                    if (t := due(step, 9)) is not None:
                        act.wait_ge(c_tp, t + 1)
                        if t:
                            act.wait_ge(c_op, t)
                        copy(pT_c[0:NCMP_P].rearrange("p (b a) n -> p b (a n)", b=2), psum[0:NCMP_P, 6:8]).then_inc(c_pt, 1)
                    if (t := due(step, 12)) is not None:
                        act.wait_ge(m_mx, t + 1)
                        if t:
                            act.wait_ge(m_tp, t)
                            act.wait_ge(m_nm, t)
                        for m in range(4):
                            act.activation(p_m[:, m], bank(6 + m // 2)[:, 256 * (m % 2):256 * (m % 2) + 256], ACT.Exp,
                                           bias=max_m[:, m:m + 1], accum_out=sum_m[:, m:m + 1]).then_inc(m_ex, 1)
                    if (t := due(step, 14)) is not None:
                        act.wait_ge(m_tp, t + 1)
                        if t:
                            act.wait_ge(m_op, t)
                        copy(pT_m.rearrange("p (b m) a n -> p b (m a n)", b=2), psum[:, 6:8]).then_inc(m_pt, 1)
                    if (t := due(step, 2, 1)) is not None:
                        act.wait_ge(m_ot, t + 1)
                        copy(oT_mem[:, :, 128 * t:128 * t + 128], bank(7)[:, 0:256].rearrange("p (a n) -> p a n", a=2)
                             ).then_inc(m_oe, 1)

            @block.vector
            def _(dve):
                link = linked(dve, s_d4, [0])
                dve.wait_ge(s_bi, 48)
                dve.tensor_copy(rel33[0:32], rel_sb[0:32].unsqueeze(2).to_broadcast([32, 8, 128])).then_inc(s_r3, 1)
                dve.memset(rel33[32:33], NEG).then_inc(s_r3, 1)
                for h in range(NH):
                    dve.wait_ge(s_tb, h + 1)
                    if h >= 2:
                        dve.wait_ge(s_ts[h % 2], 32 * (h // 2))
                    dve.tensor_copy(table_c[0:NCMP_P, h % 2].rearrange("p (b n) -> p b n", b=2),
                                    psum[0:NCMP_P, 4 + 2 * (h % 2):6 + 2 * (h % 2)]).then_inc(s_te2, 1)
                dve.wait_ge(s_tl, 16 * 16)
                dve.wait_ge(s_bc, TILES)
                for step in range(STEPS):
                    u = step
                    if u < len(UNITS):
                        t, hh, b = UNITS[u]
                        w = 128 * (t + 1)
                        dve.wait_ge(u_sp, u + 1)
                        if u >= 2:
                            dve.wait_ge(u_tp, u - 1)
                        link(dve.tensor_tensor(sc_u[:, u % 2, 0:w], bank(u % 2)[:, 0:w], bias_q[:, hh, 512 - w:512], ALU.add))
                        dve.tensor_reduce(stat_u[:, u % 2, 0:1], sc_u[:, u % 2, 0:w], AX, ALU.max, negate=True
                                          ).then_inc(u_mx, 1)
                    if (t := due(step, 2, 1)) is not None:
                        dve.wait_ge(u_ex, PER * (t + 1))
                        dve.wait_ge(u_op, PER * (t + 1))
                        dve.wait_ge(c_oa, t + 1)
                        link(dve.reciprocal(coef, sum_u[:, t % 2]))
                        g = gates[:, t].rearrange("p (h n) -> p n h", n=3)
                        link(dve.tensor_tensor(coef.rearrange("p (n h) -> p n h", n=2),
                                               coef.rearrange("p (n h) -> p n h", n=2), g[:, 1:3], ALU.mult))
                        for b in range(2):
                            o_b = sc_f
                            link(dve.tensor_tensor(o_b, bank(4 + b).rearrange("p (h d) -> p h d", h=8),
                                                   coef[:, 8 * b:8 * b + 8].unsqueeze(2).to_broadcast([128, 8, HD]), ALU.mult))
                            ins = dve.tensor_tensor(oa, oa, o_b, ALU.add)
                            if b == 0:
                                link(ins)
                            else:
                                ins.then_inc(f_oa, 1)
                    if (t := due(step, 5)) is not None:
                        dve.wait_ge(c_sp, t + 1)
                        if t:
                            dve.wait_ge(c_tp, t)
                        link(dve.tensor_tensor(sc_c.rearrange("p (b a) n -> p b (a n)", b=2), psum[:, 6:8, 0:4 * NCMP_P],
                                               bias_c[:, t].rearrange("p (b a) n -> p b (a n)", b=2), ALU.add))
                        link(dve.tensor_reduce(max_c, sc_c, AX, ALU.max))
                        link(dve.tensor_scalar(max_c, max_c, -1e20, None, ALU.max))
                        dve.tensor_tensor(sc_c, sc_c, max_c.unsqueeze(2).to_broadcast([128, 8, NCMP_P]),
                                          ALU.subtract).then_inc(c_mx, 1)
                    if (t := due(step, 7)) is not None:
                        dve.wait_ge(c_ex, t + 1)
                        link(dve.tensor_reduce(sum_c, sc_c, AX, ALU.add))
                        link(dve.tensor_scalar(sum_c, sum_c, 1e-30, None, ALU.max))
                        link(dve.reciprocal(sum_c, sum_c))
                        link(dve.tensor_tensor(sum_c.rearrange("p (g q) -> p g q", g=2), sum_c.rearrange("p (g q) -> p g q", g=2),
                                               gates[:, t].rearrange("p (q g n) -> p n g q", q=4, g=2)[:, 0], ALU.mult))
                        dve.tensor_tensor(sc_c, sc_c, sum_c.unsqueeze(2).to_broadcast([128, 8, NCMP_P]), ALU.mult
                                          ).then_inc(c_pn, 1)
                    if (t := due(step, 11)) is not None:
                        dve.wait_ge(c_op, t + 1)
                        if t:
                            dve.wait_ge(f_ot, t)
                        dve.tensor_copy(oa, bank(6).rearrange("p (h d) -> p h d", h=8)).then_inc(c_oa, 1)
                    if (t := due(step, 12)) is not None:
                        dve.wait_ge(m_sp, t + 1)
                        dve.tensor_reduce(max_m.rearrange("p (b m) -> p b m", b=2),
                                          psum[:, 6:8].rearrange("p b (m n) -> p b m n", m=2), AX, ALU.max,
                                          negate=True).then_inc(m_mx, 1)
                    if (t := due(step, 0, 1)) is not None:
                        dve.wait_ge(m_op, t + 1)
                        dve.wait_ge(m_ex, 4 * t + 4)
                        if t:
                            dve.wait_ge(m_ot, t)
                        link(dve.reciprocal(sum_m, sum_m))
                        dve.tensor_tensor(om.rearrange("p (a b) d -> p a b d", a=2),
                                          bank(6)[:, 0:256].rearrange("p (a b d) -> p a b d", a=2, b=2),
                                          sum_m.rearrange("p (b a) -> p a b", b=2).unsqueeze(3).to_broadcast([128, 2, 2, HD]),
                                          ALU.mult).then_inc(m_nm, 1)

            @block.tensor
            def _(pe):
                pe.wait_ge(s_bi, 48)
                pe.wait_ge(s_r3, 2)
                for h in range(NH):
                    if h >= 2:
                        pe.wait_ge(s_te1, h - 1)
                        pe.wait_ge(s_te2, h - 1)
                    b = 2 * (h % 2)
                    pe.matmul(bank(b), rel33[0:33, h], dist_desc[0:33, 0:512], start=True, stop=True)
                    pe.matmul(bank(b + 1)[:, 0:BIASL - 512], rel33[0:33, h], dist_desc[0:33, 512:], start=True, stop=True)
                    for half in range(2):
                        mm = pe.matmul(bank(4 + b + half)[0:NCMP_P], rel33[0:33, h, 0:NCMP_P],
                                       dist_asc[0:33, 512 * half:512 * half + 512], start=True, stop=True)
                    mm.then_inc(s_tb, 1)
                pe.wait_ge(s_te1, NH)
                pe.wait_ge(s_te2, NH)
                pe.wait_ge(s_tl, 256)
                for t in range(TILES):
                    for g in range(2):
                        for p in range(4):
                            mm = pe.transpose(bank(t)[:, (4 * g + p) * NCMP_P:(4 * g + p + 1) * NCMP_P],
                                              bias_b[0:NCMP_P, 2 * p + g, 128 * t:128 * t + 128], ident[0:NCMP_P, 0:NCMP_P])
                    mm.then_inc(s_bt, 1)
                pe.wait_ge(s_bc, TILES)
                for step in range(STEPS):
                    u = step
                    if u < len(UNITS):
                        t, hh, b = UNITS[u]
                        p, g = hh // 2, hh % 2
                        q = slice(64 * g, 64 * g + 64)
                        if u >= 2:
                            pe.wait_ge(u_mx, u - 1)
                        keys = (ksT, kwT)[b]
                        pe.matmul(bank(u % 2)[:, 0:128 * (t + 1)], qT[q, p, 128 * t:128 * t + 128], keys[q, 0:128 * (t + 1)],
                                  start=True, stop=True).then_inc(u_sp, 1)
                    u = step - 1
                    if 0 <= u < len(UNITS):
                        t = UNITS[u][0]
                        pe.wait_ge(u_ex, u + 1)
                        if u >= 2:
                            pe.wait_ge(u_pt, u - 1)
                        for a in range(t + 1):
                            mm = pe.transpose(bank(2 + u % 2)[:, 128 * a:128 * a + 128], sc_u[:, u % 2, 128 * a:128 * a + 128],
                                              ident)
                        mm.then_inc(u_tp, 1)
                    u = step - 2
                    if 0 <= u < len(UNITS):
                        t, hh, b = UNITS[u]
                        g = hh % 2
                        pe.wait_ge(u_pt, u + 1)
                        if hh == 0 and b == 0 and t:
                            pe.wait_ge(f_oa, t)
                        values = (v_slc, v_win)[b]
                        for a in range(t + 1):
                            mm = pe.matmul(bank(4 + b)[:, 64 * hh:64 * hh + 64], pT_u[:, u % 2, 128 * a:128 * a + 128],
                                           values[:, a, 64 * g:64 * g + 64], start=(a == 0), stop=(a == t))
                        mm.then_inc(u_op, 1)
                    if (t := due(step, 1, 1)) is not None:
                        pe.wait_ge(m_nm, t + 1)
                        for mp in range(2):
                            mm = pe.transpose(bank(7)[:, 128 * mp:128 * mp + 128],
                                              om.rearrange("p (a b) d -> p a (b d)", a=2)[:, mp], ident)
                        mm.then_inc(m_ot, 1)
                    if (t := due(step, 3, 1)) is not None:
                        pe.wait_ge(f_oa, t + 1)
                        for p in range(4):
                            mm = pe.transpose(bank(6)[:, 128 * p:128 * p + 128],
                                              oa.rearrange("p (a b) d -> p a (b d)", a=4)[:, p], ident)
                        mm.then_inc(f_ot, 1)
                    if (t := due(step, 5)) is not None:
                        if t:
                            pe.wait_ge(f_oe, t)
                            pe.wait_ge(m_oe, t)
                        for g in range(2):
                            q = slice(64 * g, 64 * g + 64)
                            for p in range(4):
                                mm = pe.matmul(bank(6 + g)[:, p * NCMP_P:(p + 1) * NCMP_P], qT[q, p, 128 * t:128 * t + 128],
                                               kcT[q, NS, 0:NCMP_P], start=True, stop=True)
                        mm.then_inc(c_sp, 1)
                    if (t := due(step, 8)) is not None:
                        pe.wait_ge(c_pn, t + 1)
                        for k in range(8):
                            mm = pe.transpose(bank(6 + k // 4)[0:NCMP_P, 128 * (k % 4):128 * (k % 4) + 128], sc_c[:, k], ident)
                        mm.then_inc(c_tp, 1)
                    if (t := due(step, 10)) is not None:
                        pe.wait_ge(c_pt, t + 1)
                        for g in range(2):
                            for p in range(4):
                                hh = 2 * p + g
                                mm = pe.matmul(bank(6)[:, 64 * hh:64 * hh + 64], pT_c[0:NCMP_P, 4 * g + p],
                                               v_cmp[0:NCMP_P, NS, 64 * g:64 * g + 64], start=True, stop=True)
                        mm.then_inc(c_op, 1)
                    if (t := due(step, 12)) is not None:
                        pe.wait_ge(c_oa, t + 1)
                        for m2 in range(2):
                            q = slice(64 * m2, 64 * m2 + 64)
                            for mp in range(2):
                                mm = pe.matmul(bank(6 + m2)[:, 256 * mp:256 * mp + 256], qmT[q, mp, 128 * t:128 * t + 128],
                                               kmT[q, mp], start=True, stop=True)
                        mm.then_inc(m_sp, 1)
                    if (t := due(step, 13)) is not None:
                        pe.wait_ge(m_ex, 4 * t + 4)
                        for m in range(4):
                            for a in range(2):
                                mm = pe.transpose(bank(6 + m // 2)[:, 128 * (2 * (m % 2) + a):128 * (2 * (m % 2) + a) + 128],
                                                  p_m[:, m, 128 * a:128 * a + 128], ident)
                        mm.then_inc(m_tp, 1)
                    if (t := due(step, 15)) is not None:
                        pe.wait_ge(m_pt, t + 1)
                        for m in range(4):
                            m2, mp = m // 2, m % 2
                            h = 2 * mp + m2
                            for a in range(2):
                                mm = pe.matmul(bank(6)[:, 64 * h:64 * h + 64], pT_m[:, m, a],
                                               zm[:, a, 256 + 64 * h:320 + 64 * h], start=(a == 0), stop=(a == 1))
                        mm.then_inc(m_op, 1)

        phase_over()
        cursor[0] = 50200
        g4 = take(NT, TOPK)
        slot_token = take(NBLK + 1, dt=U32)
        slot_row = take(NBLK + 1, dt=U32)
        e_row = take(NBLK, dt=I32)
        n_used = take(2, dt=I32)
        e_match = take(NBLK, dt=BF16)
        b_parts = take(2048, dt=BF16)
        keep_end = cursor[0]
        assert keep_end <= 53000
        cursor[0] = tail_base
        w_gb = take(6, KD, 128)
        w_up = take(KD, D)
        w_out = take(KD, D)
        mixT = take(KD, NTOK)
        sig = take(2, NTOK)
        prod = take(2, NTOK)
        top = cursor[0]
        cursor[0] = tail_base
        x2n = take(2, D)
        sq2 = take(D)
        hT2 = take(2, KD, 128)
        assert cursor[0] <= tail_base + 6 * KD * 128
        cursor[0] = top
        router_w = take(KD, NE)
        router_b = take(NE)
        before = take(128)
        iota128 = take(128)
        row_id = take(NT * TOPK)
        spare_row = take(1)
        is_pad = take(NBLK + 1)
        row_f = take(NBLK + 1)
        row_i = take(NBLK + 1, dt=I32)
        logit = take(NT, NE)
        best = take(2, 8)
        best_i = take(2, 8, dt=U32)
        best_f = take(2, 8)
        eg = take(2, 6)
        hot = take(NT, TOPK, NE)
        mask = take(NT, NE)
        gmat = take(NE)
        gmT = take(128)
        b_down = take(D)
        tmp = take(TOPK, NE)
        cnt, nblk, ends, base_ = take(NE), take(NE), take(NE), take(NE)
        comb = take(NT, NE)
        pos_f = take(NT, TOPK)
        slot_i, blk_i = take(NT, TOPK, dt=I32), take(NT, TOPK, dt=I32)
        slot_f, blk_f = take(NT, TOPK), take(NT, TOPK)
        hot_slot = take(128)
        hot_blk = take(NBLK + 1)
        eb = take(2)
        ebw = take(128)
        assert cursor[0] <= 50200, cursor[0]
        bg = w_out.rearrange("p k n -> p (k n)")[:, 0:2048]
        bf_r = w_out.rearrange("p k n -> p (k n)")[:, 2048:4096]

        scr_h = scratch("scr_h", [NTOK, D])
        scr_rows = scratch("scr_rows", [NTOK * TOPK + 128, D])

        g_w = [sem(f"g_w{n}") for n in range(6)]
        g_wu, g_wo, g_rc = sem("g_wu"), sem("g_wo"), sem("g_rc")
        g_pp, g_sg, g_mx = sem("g_pp"), sem("g_sg"), sem("g_mx")
        x_p, x_a, x_rt, x_n, x_tp, x_te, x_lg = (sem("x_" + n) for n in
                                                       ("p", "a", "rt", "n", "tp", "te", "lg"))
        r_mx, r_ex, r_gm, r_gt, r_ge, r_bd, r_be = (sem("r_" + n) for n in ("mx", "ex", "gm", "gt", "ge", "bd", "be"))
        r_cnt, r_rank, r_hs, r_hu, r_eb, r_ebp, r_bg = (sem("r_" + n) for n in
                                                                ("cnt", "rank", "hs", "hu", "eb", "ebp", "bg"))
        s_d5 = sem("s_d5")
        g_pr = sem("g_pr")
        x_st = [sem(f"x_st{n}") for n in range(2)]
        x_sq = sem("x_sq")
        x_le = sem("x_le")
        UPK = [(0, 2), (2, 6), (6, 8)]
        oT_of = lambda k: oT_pool[:, k] if k < 2 else oT_nsa[:, k - 2] if k < 6 else oT_mem[:, k - 6]
        two = lambda ap: ap.rearrange("p (h n) -> p h n", h=2)

        with nc.Block() as block:
            @block.sync
            def _(sp):
                for u in range(24):
                    if u >= 6:
                        sp.wait_ge(g_pp, u - 5)
                    sp.dma_start(w_gb[:, u % 6], i["w_gb"][u // 3, u % 3].rearrange("p (k n) -> p k n", k=KD)
                                 ).then_inc(g_w[u % 6], 16)
                    if u == 0:
                        sp.dma_start(w_up, i["w_up"].rearrange("(k p) n -> p k n", p=128)).then_inc(g_wu, 16)
                    if u == 5:
                        sp.dma_start(w_out, i["w_out"].rearrange("(k p) n -> p k n", p=128)).then_inc(g_wo, 16)
                        for dst, src in ((router_w, i["router_w"].rearrange("(k p) n -> p k n", p=128)),
                                         (router_b, i["router_b"].partition_broadcast(128).rearrange("p a n -> p (a n)")),
                                         (before, i["c_before"]), (iota128, i["c_iota128"]), (row_id, i["c_row_id"]), (spare_row, i["c_spare_row"]),
                                         (b_down[0:32], i["b_down"])):
                            sp.dma_start(dst, src).then_inc(g_rc, 16)
                for n in range(NT):
                    sp.wait_ge(x_n, n + 1)
                    sp.dma_start(scr_h[128 * n:128 * n + ROWS[n]], x2n[0:ROWS[n], n % 2]).then_inc(x_st[n % 2], 16)
                sp.wait_ge(x_p, 2 * NT)
                for part in range(3):
                    sp.dma_start(bg[32 * part:32 * part + 32], i["b_gu"]).then_inc(r_bg, 16)
                sp.wait_ge(x_st[0], 48)
                sp.wait_ge(x_st[1], 32)

            @block.gpsimd
            def _(pool):
                pool.wait_ge(g_rc, 112)

            @block.scalar
            def _(act):
                for u in range(24):
                    s = u % 2
                    act.wait_ge(g_pp, u + 1)
                    if u >= 2:
                        act.wait_ge(g_pr, u - 1)
                    act.activation(two(sig[:, s]), psum[:, 4 * s:4 * s + 2, 0:HALF], ACT.Sigmoid).then_inc(g_sg, 1)
                for n in range(NT):
                    r = ROWS[n]
                    act.wait_ge(x_a, 2 * n + 2)
                    if n:
                        act.wait_ge(x_rt, n)
                    act.activation(sq2[0:r], x[0:r, n], ACT.Square, accum_out=sumsq[0:r, n:n + 1]).then_inc(x_sq, 1)
                    act.wait_ge(x_sq, n + 1)
                    act.activation(root[0:r, n:n + 1], sumsq[0:r, n:n + 1], ACT.Sqrt, bias=eps[0:r], scale=1.0 / D
                                   ).then_inc(x_rt, 1)
                for n in range(NT):
                    r = ROWS[n]
                    act.wait_ge(r_mx, n + 1)
                    act.activation(eg[0:r, n % 2, 0:4], best[0:r, n % 2, 0:4], ACT.Exp, bias=eg[0:r, n % 2, 4:5],
                                   accum_out=eg[0:r, n % 2, 5:6]).then_inc(r_ex, 1)
                    act.wait_ge(r_gt, n + 1)
                    if n:
                        act.wait_ge(r_bd, 2 * n)
                    act.activation(gmT[0:32, 0:r], bank(7)[0:32, 0:r], ACT.Copy).then_inc(r_ge, 1)

            @block.vector
            def _(dve):
                link = linked(dve, s_d5, [0])
                for u in range(24):
                    c, b, s = u // 3, u % 3, u % 2
                    dve.wait_ge(g_sg, u + 1)
                    dst = mixT[:, c] if b == 0 else prod[:, s]
                    if b and u >= 2:
                        dve.wait_ge(g_mx, u - 1)
                    dve.tensor_tensor(two(dst), psum[:, 4 * s + 2:4 * s + 4, 0:HALF], two(sig[:, s]), ALU.mult).then_inc(g_pr, 1)
                    dve.wait_ge(g_pr, u + 1)
                    if b:
                        dve.wait_ge(g_mx, u)
                        dve.tensor_tensor(mixT[:, c], mixT[:, c], prod[:, s], ALU.add).then_inc(g_mx, 1)
                    else:
                        dve.sem_inc(g_mx, 1)

                def residual(n):
                    r = ROWS[n]
                    for h in range(2):
                        dve.wait_ge(x_p, 2 * n + h + 1)
                        sl = x[0:r, n, 512 * h:512 * h + 512]
                        dve.tensor_tensor(sl, bank(2 * (n % 2) + h)[0:r], sl, ALU.add).then_inc(x_a, 1)

                def norm2(n):
                    r = ROWS[n]
                    dve.wait_ge(x_rt, n + 1)
                    link(dve.reciprocal(rinv[0:r, n:n + 1], root[0:r, n:n + 1]))
                    if n >= 2:
                        dve.wait_ge(x_tp, 2 * n - 2)
                        dve.wait_ge(x_st[n % 2], 16 * (n // 2))
                    dve.tensor_scalar(x2n[0:r, n % 2], x[0:r, n], rinv[0:r, n:n + 1], None, ALU.mult).then_inc(x_n, 1)

                def to_hT2(n):
                    r = ROWS[n]
                    if n >= 2:
                        dve.wait_ge(x_lg, n - 1)
                    for h in range(2):
                        dve.wait_ge(x_tp, 2 * n + h + 1)
                        dve.tensor_tensor(hT2[:, n % 2, 4 * h:4 * h + 4, 0:r],
                                          bank(4 + h)[:, 0:4 * r].rearrange("p (a b) -> p a b", a=4),
                                          g2c[:, 4 * h:4 * h + 4].unsqueeze(2).to_broadcast([128, 4, r]), ALU.mult
                                          ).then_inc(x_te, 1)

                def route(n):
                    r, s = ROWS[n], n % 2
                    link(dve.max(best[0:r, s], logit[0:r, n]))
                    link(dve.max_index(best_i[0:r, s], best[0:r, s], logit[0:r, n]))
                    dve.tensor_scalar(eg[0:r, s, 4:5], best[0:r, s, 0:1], -1.0, None, ALU.mult).then_inc(r_mx, 1)
                    link(dve.tensor_copy(best_f[0:r, s], best_i[0:r, s]))
                    for k in range(TOPK):
                        ins = dve.tensor_scalar(hot[0:r, n, k], iota32[0:r], best_f[0:r, s, k:k + 1], None, ALU.is_equal)
                        link(ins)
                    link(dve.tensor_reduce(mask[0:r, n], hot[0:r, n].rearrange("p k e -> p e k"), AX, ALU.add))
                    dve.wait_ge(r_ex, n + 1)
                    link(dve.reciprocal(eg[0:r, s, 5:6], eg[0:r, s, 5:6]))
                    link(dve.tensor_scalar(g4[0:r, n], eg[0:r, s, 0:4], eg[0:r, s, 5:6], None, ALU.mult))
                    link(dve.tensor_tensor(tmp[0:r], hot[0:r, n], g4[0:r, n].unsqueeze(2).to_broadcast([r, TOPK, NE]), ALU.mult))
                    if n:
                        dve.wait_ge(r_gt, n)
                    dve.tensor_reduce(gmat[0:r], tmp[0:r].rearrange("p k e -> p e k"), AX, ALU.add).then_inc(r_gm, 1)
                    for h in range(2):
                        dve.wait_ge(r_bd, 2 * n + h + 1)
                        sl = x[0:r, n, 512 * h:512 * h + 512]
                        dve.tensor_tensor(sl, bank(h)[0:r], sl, ALU.add).then_inc(r_be, 1)

                dve.wait_ge(g_rc, 112)
                residual(0)
                residual(1)
                for n in range(NT):
                    norm2(n)
                    if n + 2 < NT:
                        residual(n + 2)
                    to_hT2(n)
                    dve.wait_ge(x_lg, n + 1)
                    dve.tensor_tensor(logit[0:ROWS[n], n], bank(6)[0:ROWS[n], 0:NE], router_b[0:ROWS[n]], ALU.add
                                      ).then_inc(x_le, 1)
                dve.wait_ge(x_n, NT)
                dve.wait_ge(x_le, NT)
                for n in range(NT):
                    route(n)
                dve.wait_ge(r_cnt, 1)
                link(dve.tensor_copy(cnt, bank(4)[:, 0:NE]))
                link(dve.tensor_scalar(nblk, cnt, 0.0, None, ALU.is_gt))
                for j in range(1, NT):
                    link(dve.tensor_scalar(base_, cnt, 128.0 * j, None, ALU.is_gt))
                    link(dve.tensor_tensor(nblk, nblk, base_, ALU.add))
                link(dve.tensor_tensor_scan(ends, ones[:, 0:NE], nblk, 0.0, ALU.mult, ALU.add))
                link(dve.tensor_tensor(base_, ends, nblk, ALU.subtract))
                link(dve.tensor_scalar(base_, base_, 128.0, None, ALU.mult))
                link(dve.tensor_copy(n_used[:, 0:1], ends[:, NE - 1:NE]))
                for n in range(NT):
                    r = ROWS[n]
                    dve.wait_ge(r_rank, 1)
                    link(dve.tensor_tensor(comb[0:r, n], bank(5)[0:r, 32 * n:32 * n + 32], base_[0:r], ALU.add))
                    link(dve.tensor_tensor(tmp[0:r], hot[0:r, n], comb[0:r, n].unsqueeze(1).to_broadcast([r, TOPK, NE]), ALU.mult))
                    link(dve.tensor_reduce(pos_f[0:r, n], tmp[0:r], AX, ALU.add))
                    link(dve.tensor_copy(slot_i[0:r, n], pos_f[0:r, n]))
                    link(dve.tensor_scalar(blk_i[0:r, n], slot_i[0:r, n], 7, None, ALU.arith_shift_right))
                    link(dve.tensor_scalar(slot_i[0:r, n], slot_i[0:r, n], 127, None, ALU.bitwise_and))
                    link(dve.tensor_copy(blk_f[0:r, n], blk_i[0:r, n]))
                    link(dve.tensor_copy(slot_f[0:r, n], slot_i[0:r, n]))
                    for k in range(TOPK):
                        m = TOPK * n + k
                        if m:
                            dve.wait_ge(r_hu, m)
                        link(dve.tensor_scalar(hot_slot[0:r], iota128[0:r], slot_f[0:r, n, k:k + 1], None, ALU.is_equal))
                        dve.tensor_scalar(hot_blk[0:r], iota128[0:r, 0:NBLK + 1], blk_f[0:r, n, k:k + 1], row_id[0:r, m:m + 1],
                                          ALU.is_equal, ALU.mult).then_inc(r_hs, 1)
                link(dve.tensor_scalar(ebw[0:NBLK, 0:NE], ends[0:NBLK], cols[0:NBLK, 0:1], None, ALU.is_le))
                link(dve.tensor_reduce(eb[0:NBLK, 0:1], ebw[0:NBLK, 0:NE], AX, ALU.add))
                link(dve.tensor_scalar(eb[0:NBLK, 0:1], eb[0:NBLK, 0:1], float(NE - 1), None, ALU.min))
                dve.tensor_copy(ebw[0:NBLK], eb[0:NBLK, 0:1].to_broadcast([NBLK, 128])).then_inc(r_eb, 1)
                dve.wait_ge(r_ebp, 1)
                link(dve.tensor_copy(e_row, bank(6)[:, 64:64 + NBLK]))
                link(dve.tensor_scalar(e_match, bank(6)[:, 64:64 + NBLK], cols[:, 2:3], None, ALU.is_equal))
                dve.wait_ge(r_hu, NT * TOPK)
                link(dve.tensor_scalar(is_pad, bank(7)[:, 128:129 + NBLK], 0.0, spare_row, ALU.is_equal, ALU.mult))
                link(dve.scalar_tensor_tensor(row_f, bank(7)[:, 128:129 + NBLK], -1.0, is_pad, ALU.add, ALU.add))
                link(dve.tensor_copy(slot_row, row_f))
                link(dve.tensor_scalar(row_f, bank(7)[:, 128:129 + NBLK], -1.0, 0.0, ALU.add, ALU.max))
                link(dve.tensor_copy(row_i, row_f))
                link(dve.tensor_scalar(row_i, row_i, int(math.log2(TOPK)), None, ALU.arith_shift_right))
                link(dve.tensor_copy(slot_token, row_i))
                dve.wait_ge(r_bg, 48)
                for part in range(3):
                    q = slice(32 * part, 32 * part + 32)
                    link(dve.tensor_copy(b_parts[q], bg[q]))
                    for _ in range(part):
                        link(dve.tensor_copy(bf_r[q], b_parts[q]))
                        link(dve.tensor_tensor(bg[q], bg[q], bf_r[q], ALU.subtract))
                        link(dve.tensor_copy(b_parts[q], bg[q]))

            @block.tensor
            def _(pe):
                for u in range(24):
                    c, b, s = u // 3, u % 3, u % 2
                    pe.wait_ge(g_w[u % 6], 16 * (u // 6 + 1))
                    if u >= 2:
                        pe.wait_ge(g_pr, u - 1)
                    if u == 0:
                        pe.wait_ge(g_wu, 16)
                    for h in range(2):
                        t = slice(h * HALF, (h + 1) * HALF)
                        for k in range(KD):
                            pe.matmul(bank(4 * s + h)[:, 0:HALF], w_gb[:, u % 6, k], hT[:, k, t], start=(k == 0),
                                      stop=(k == KD - 1))
                        k0, k1 = UPK[b]
                        for k in range(k0, k1):
                            mm = pe.matmul(bank(4 * s + 2 + h)[:, 0:HALF], w_up[:, k, 128 * c:128 * c + 128], oT_of(k)[:, t],
                                           start=(k == k0), stop=(k == k1 - 1))
                    mm.then_inc(g_pp, 1)
                pe.wait_ge(g_mx, 24)
                pe.wait_ge(g_wo, 16)
                pe.wait_ge(g_rc, 112)

                def mix_out(n):
                    r = ROWS[n]
                    for h in range(2):
                        if n >= 2:
                            pe.wait_ge(x_a, 2 * (n - 2) + h + 1)
                        for k in range(KD):
                            mm = pe.matmul(bank(2 * (n % 2) + h)[0:r], mixT[:, k, 128 * n:128 * n + r],
                                           w_out[:, k, 512 * h:512 * h + 512], start=(k == 0), stop=(k == KD - 1))
                        mm.then_inc(x_p, 1)

                def router(n):
                    r, s = ROWS[n], n % 2
                    pe.wait_ge(x_n, n + 1)
                    for h in range(2):
                        if n:
                            pe.wait_ge(x_te, 2 * n - 1 + h)
                        for k in range(4):
                            mm = pe.transpose(bank(4 + h)[:, k * r:(k + 1) * r], x2n[0:r, s, (4 * h + k) * 128:(4 * h + k + 1) * 128],
                                              ident[0:r, 0:r])
                        mm.then_inc(x_tp, 1)

                def logits(n):
                    r, s = ROWS[n], n % 2
                    pe.wait_ge(x_te, 2 * n + 2)
                    if n:
                        pe.wait_ge(x_le, n)
                    for k in range(KD):
                        mm = pe.matmul(bank(6)[0:r, 0:NE], hT2[:, s, k, 0:r], router_w[:, k], start=(k == 0),
                                       stop=(k == KD - 1))
                    mm.then_inc(x_lg, 1)

                mix_out(0)
                mix_out(1)
                for n in range(NT):
                    if n + 2 < NT:
                        mix_out(n + 2)
                    router(n)
                    logits(n)
                for n in range(NT):
                    r = ROWS[n]
                    pe.wait_ge(r_gm, n + 1)
                    if n:
                        pe.wait_ge(r_ge, n)
                        pe.wait_ge(r_be, 2 * n)
                    else:
                        pe.wait_ge(x_le, NT)
                        pe.wait_ge(x_a, 2 * NT)
                    pe.transpose(bank(7)[0:32, 0:r], gmat[0:r], ident[0:r, 0:r]).then_inc(r_gt, 1)
                    pe.wait_ge(r_ge, n + 1)
                    for h in range(2):
                        if n:
                            pe.wait_ge(r_be, 2 * n - 1 + h)
                        pe.matmul(bank(h)[0:r], gmT[0:32, 0:r], b_down[0:32, 512 * h:512 * h + 512], start=True, stop=True
                                  ).then_inc(r_bd, 1)
                for n in range(NT):
                    mm = pe.matmul(bank(4)[:, 0:NE], ones[0:ROWS[n], 0:128], mask[0:ROWS[n], n], start=(n == 0), stop=(n == NT - 1))
                mm.then_inc(r_cnt, 1)
                for n in range(NT):
                    r = ROWS[n]
                    for m in range(n + 1):
                        w = before[0:r, 0:r] if m == n else ones[:, 0:r]
                        mm = pe.matmul(bank(5)[0:r, 32 * n:32 * n + 32], w, mask[0:ROWS[m], m], start=(m == 0), stop=(m == n))
                mm.then_inc(r_rank, 1)
                for n in range(NT):
                    r = ROWS[n]
                    for k in range(TOPK):
                        m = TOPK * n + k
                        pe.wait_ge(r_hs, m + 1)
                        pe.matmul(bank(7)[:, 128:129 + NBLK], hot_slot[0:r], hot_blk[0:r], start=(m == 0),
                                  stop=(m == NT * TOPK - 1)).then_inc(r_hu, 1)
                pe.wait_ge(r_eb, 1)
                pe.matmul(bank(6)[:, 64:64 + NBLK], ebw[0:NBLK], ident[0:NBLK, 0:NBLK], start=True, stop=True).then_inc(r_ebp, 1)

        phase_over()
        cursor[0] = moe_base
        w_in_e = take(2, KD, 2, 512)
        w_down_e = take(KD, D)
        cur_token, cur_row = take(2, dt=U32), take(2, dt=U32)
        xg = take(D)
        xgT = take(KD, 128)
        bias_of = take(128, dt=BF16)
        gate_c = take(2, 512)
        up_c = take(2, 512)
        act_h = take(2, 512)
        actT = take(KD, 128)
        y_rows = take(D)
        assert cursor[0] <= 50200
        cursor[0] = moe_base
        picked = take(2, TOPK, D)

        e_in = [[sem(f"e_in{h}{k}") for k in range(KD)] for h in range(2)]
        e_dn = [sem(f"e_dn{k}") for k in range(KD // 2)]
        e_ix, e_g, e_gt, e_xT, e_bs, e_gu, e_c, e_sg, e_a, e_at, e_ae, e_y, e_yc, e_out = (
            sem("e_" + n) for n in ("ix", "g", "gt", "xT", "bs", "gu", "c", "sg", "a", "at", "ae", "y", "yc", "out"))
        e_use = sem("e_use")
        e_d = sem("e_d")
        e_ir, e_st, e_all = sem("e_ir"), sem("e_st"), sem("e_all")
        e_sent = sem("e_sent")
        p_g = [sem(f"p_g{n}") for n in range(2)]
        p_add, p_out = sem("p_add"), sem("p_out")

        def used(eng):
            return eng.value_load(n_used[0:1, 0:1], min_val=1, max_val=NBLK)

        w_gu_v = i["w_gu"].rearrange("e (k p) (g h n) -> e k p g h n", p=128, g=2, h=2)
        w_dn_v = i["w_down"].rearrange("e (k p) n -> e p k n", p=128)
        USES = 2 * (KD - 1) + KD // 2 - 1

        with nc.Block() as block:
            @block.sync
            def _(sp):
                blocks = used(sp)
                with sp.Fori(0, NBLK) as b:
                    e = sp.value_load(e_row[0:1, bass.ds(b, 1)], min_val=0, max_val=NE - 1)
                    with sp.If(b < blocks):
                        for h in range(2):
                            for k in range(KD):
                                sp.wait_ge(e_use, USES * b + h * (KD - 1) + k + 1)
                                sp.dma_start(w_in_e[:, h, k], w_gu_v[bass.ds(e, 1), k, :, :, h].rearrange("e p g n -> (e p) g n")
                                             ).then_inc(e_in[h][k], 16)
                        for k in range(KD // 2):
                            if k < KD // 2 - 1:
                                sp.wait_ge(e_use, USES * b + 2 * (KD - 1) + k + 1)
                            else:
                                sp.wait_ge(e_y, b + 1)
                            sp.dma_start(w_down_e[:, 2 * k:2 * k + 2],
                                         w_dn_v[bass.ds(e, 1), :, 2 * k:2 * k + 2].rearrange("e p k n -> (e p) k n")
                                         ).then_inc(e_dn[k], 16)
                        sp.nop()
                    with sp.Else():
                        sp.nop()
                sp.wait_ge(e_all, 1)
                for n in range(NT + 2):
                    if n < NT:
                        if n >= 2:
                            sp.wait_ge(p_add, TOPK * (n - 1))
                        t0 = 128 * n
                        sp.dma_start(picked[0:ROWS[n], n % 2], scr_rows[TOPK * t0:TOPK * (t0 + ROWS[n])].rearrange(
                            "(p k) n -> p k n", k=TOPK)).then_inc(p_g[n % 2], 16)
                    if n < 2:
                        continue
                    n -= 2
                    r = ROWS[n]
                    sp.wait_ge(p_add, TOPK * (n + 1))
                    dst = o["y_prompt"][0, 128 * n:128 * n + 128] if n < 4 else o["y_sample"].rearrange("s t d -> (s t) d")
                    sp.dma_start(dst, x[0:r, n]).then_inc(p_out, 16)
                sp.wait_ge(p_out, 16 * NT)

            @block.gpsimd
            def _(pool):
                def gather(b):
                    pool.tensor_copy(cur_token[:, 0:1], slot_token[:, bass.ds(b, 1)]).then_inc(e_ix, 1)
                    pool.wait_ge(e_ix, b + 1)
                    pool.sem_inc(e_sent, 1)
                    pool.indirect_dma_start(xg, None, scr_h, bass.IndirectOffsetOnAxis(cur_token[:, 0:1], 0)
                                            ).then_inc(e_g, 16)

                blocks = used(pool)
                pool.sem_inc(e_st, 1)
                gather(0)
                with pool.Fori(0, NBLK) as b:
                    with pool.If(b < blocks):
                        pool.wait_ge(e_gt, 2 * b + 2)
                        gather(b + 1)
                        pool.tensor_copy(cur_row[:, 0:1], slot_row[:, bass.ds(b, 1)]).then_inc(e_ir, 1)
                        pool.wait_ge(e_ir, b + 1)
                        pool.wait_ge(e_yc, b + 2)
                        pool.sem_inc(e_sent, 1)
                        pool.indirect_dma_start(scr_rows, bass.IndirectOffsetOnAxis(cur_row[:, 0:1], 0), y_rows, None
                                                ).then_inc(e_out, 16)
                        pool.wait_ge(e_out, 16 * b + 16)
                        pool.sem_inc(e_st, 1)
                    with pool.Else():
                        pool.nop()
                pool.wait_ge(e_g, blocks * 16 + 16)
                pool.nop().then_inc(e_all, 1)

            @block.scalar
            def _(act):
                act.sem_inc(e_ae, 2)
                act.sem_inc(e_yc, 1)
                blocks = used(act)
                with act.Fori(0, NBLK) as b:
                    with act.If(b < blocks):
                        for h in range(2):
                            act.wait_ge(e_c, 4 * b + 2 * h + 1)
                            act.activation(act_h[:, h], gate_c[:, h], ACT.Sigmoid, scale=ALPHA).then_inc(e_sg, 1)
                        for h in range(2):
                            act.wait_ge(e_at, 2 * b + h + 1)
                            act.activation(actT[:, 4 * h:4 * h + 4].rearrange("p k n -> p (k n)"), bank(6 + h), ACT.Copy
                                           ).then_inc(e_ae, 1)
                        act.wait_ge(e_y, b + 2)
                        act.wait_ge(e_st, b + 1)
                        act.activation(y_rows.rearrange("p (h n) -> p h n", h=2), bank(4, 2), ACT.Copy).then_inc(e_yc, 1)
                        act.nop()
                    with act.Else():
                        act.nop()

            @block.vector
            def _(dve):
                blocks = used(dve)
                with dve.Fori(0, NBLK) as b:
                    with dve.If(b < blocks):
                        dve.wait_ge(e_gu, 2 * b + 2)
                        dve.tensor_copy(bias_of[0:96], e_match[0:96, bass.ds(b, 1)].to_broadcast([96, 128])).then_inc(e_bs, 1)
                        for h in range(2):
                            dve.wait_ge(e_gt, 2 * b + h + 1)
                            dve.tensor_tensor(xgT[:, 4 * h:4 * h + 4], bank(6 + h).rearrange("p (a n) -> p a n", a=4),
                                              g2c[:, 4 * h:4 * h + 4].unsqueeze(2).to_broadcast([128, 4, 128]),
                                              ALU.mult).then_inc(e_xT, 1)
                        for h in range(2):
                            dve.wait_ge(e_gu, 2 * b + h + 3)
                            dve.tensor_scalar(gate_c[:, h], bank(2 * h), LIMIT, None, ALU.min).then_inc(e_c, 1)
                            dve.tensor_scalar(up_c[:, h], bank(2 * h + 1), LIMIT, -LIMIT, ALU.min, ALU.max).then_inc(e_c, 1)
                            dve.wait_ge(e_c, 4 * b + 2 * h + 2)
                            dve.scalar_tensor_tensor(up_c[:, h], up_c[:, h], 1.0, gate_c[:, h], ALU.add, ALU.mult
                                                     ).then_inc(e_d, 1)
                            dve.wait_ge(e_d, 2 * b + h + 1)
                            dve.wait_ge(e_sg, 2 * b + h + 1)
                            dve.tensor_tensor(act_h[:, h], act_h[:, h], up_c[:, h], ALU.mult).then_inc(e_a, 1)
                        dve.nop()
                    with dve.Else():
                        dve.nop()
                for n in range(NT):
                    for k in range(TOPK):
                        r = ROWS[n]
                        dve.wait_ge(p_g[n % 2], 16 * (n // 2 + 1))
                        if n or k:
                            dve.wait_ge(p_add, TOPK * n + k)
                        dve.scalar_tensor_tensor(x[0:r, n], picked[0:r, n % 2, k], g4[0:r, n, k:k + 1], x[0:r, n], ALU.mult, ALU.add
                                                 ).then_inc(p_add, 1)

            @block.tensor
            def _(pe):
                pe.sem_inc(e_use, USES)
                pe.sem_inc(e_gu, 2)
                pe.sem_inc(e_y, 1)
                blocks = used(pe)
                with pe.Fori(0, NBLK) as b:
                    with pe.If(b < blocks):
                        pe.wait_ge(e_g, 16 * b + 16)
                        pe.wait_ge(e_ae, 2 * b + 2)
                        for h in range(2):
                            for k in range(4):
                                mm = pe.transpose(bank(6 + h)[:, 128 * k:128 * k + 128],
                                                  xg[:, 128 * (4 * h + k):128 * (4 * h + k) + 128], ident)
                            mm.then_inc(e_gt, 1)
                        pe.wait_ge(e_bs, b + 1)
                        pe.wait_ge(e_xT, 2 * b + 2)
                        for h in range(2):
                            for g in range(2):
                                n0 = 1024 * g + 512 * h
                                pe.matmul(bank(2 * h + g), bias_of[0:96], b_parts[0:96, n0:n0 + 512], start=True, stop=False)
                            for k in range(KD):
                                pe.wait_ge(e_in[h][k], 16 * b + 16)
                                for g in range(2):
                                    mm = pe.matmul(bank(2 * h + g), xgT[:, k], w_in_e[:, h, k, g], start=False,
                                                   stop=(k == KD - 1))
                                if k < KD - 1:
                                    mm.then_inc(e_use, 1)
                                else:
                                    mm.then_inc(e_gu, 1)
                        for h in range(2):
                            pe.wait_ge(e_a, 2 * b + h + 1)
                            for k in range(4):
                                mm = pe.transpose(bank(6 + h)[:, 128 * k:128 * k + 128], act_h[:, h, 128 * k:128 * k + 128], ident)
                            mm.then_inc(e_at, 1)
                            pe.wait_ge(e_ae, 2 * b + h + 3)
                            if h == 0:
                                pe.wait_ge(e_yc, b + 1)
                            for kk in range(2):
                                k2 = 2 * h + kk
                                pe.wait_ge(e_dn[k2], 16 * b + 16)
                                for k in (2 * k2, 2 * k2 + 1):
                                    for n in range(2):
                                        mm = pe.matmul(bank(4 + n), actT[:, k], w_down_e[:, k, 512 * n:512 * n + 512],
                                                       start=(k == 0), stop=(k == KD - 1))
                                if k2 < 3:
                                    mm.then_inc(e_use, 1)
                                else:
                                    mm.then_inc(e_y, 1)
                        pe.nop()
                    with pe.Else():
                        pe.nop()


def kernel(**inputs):
    import concourse.bacc as bacc
    from concourse.bass_utils import run_bass_kernel_spmd

    arrays = lay_out({k: np.asarray(v) for k, v in inputs.items()})
    arrays.update(shape_constants())
    nc = bacc.Bacc("TRN2", target_bir_lowering=False, num_devices=1)
    ins = {k: nc.dram_tensor(f"in_{k}", v.shape, mybir.dt.from_np(v.dtype), kind="ExternalInput").ap()
           for k, v in arrays.items()}
    outs = {k: nc.dram_tensor(f"out_{k}", shape, F32, kind="ExternalOutput").ap() for k, shape in OUTPUTS.items()}
    build_program(nc, ins, outs)
    done = run_bass_kernel_spmd(nc, [{f"in_{k}": v for k, v in arrays.items()}], core_ids=[0])
    return tuple(done.results[0][f"out_{k}"] for k in OUTPUTS)
```

```python
import math
from contextlib import ExitStack

import numpy as np

import concourse.bass as bass
from concourse import mybir

F32 = mybir.dt.float32
BF16 = mybir.dt.bfloat16
I32 = mybir.dt.int32
U32 = mybir.dt.uint32
ALU = mybir.AluOpType
ACT = mybir.ActivationFunctionType
AX = mybir.AxisListType.X

D = 1024
NP_TOK = 512
NS = 8
TS = 4
NTOK = NP_TOK + NS * TS
NT = 5
ROWS = [128, 128, 128, 128, 32]
KD = D // 128
HD = 64
NH = 8
MH = 4
MEM = 256
EPS = 1e-6
NEG = -1e30
PAST = 2048
PAGE = 128
SUB = 16
NSUB = PAST // SUB
NCMP_S = NSUB - 1
NCMP_P = NP_TOK // SUB - 1
ROWF = SUB * 256
WTOK = 1560
NE = 32
BIASL = 640
CMPL = 1024
QSCALE = HD ** -0.5
HALF = NTOK // 2
TOPK = 4
NBLK = (NTOK * TOPK - NE) // 128 + NE
ALPHA = 1.702
LIMIT = 7.0


def shape_constants():
    def bucket(dist):
        n = np.maximum(dist, 0)
        nf = np.maximum(n, 1).astype(np.float32)
        large = 16 + (np.log(nf / np.float32(16)) / np.float32(math.log(8.0)) * np.float32(16)).astype(np.int32)
        return np.where(n < 16, n, np.minimum(large, 31))

    def onehot(dist, rows):
        out = np.zeros((rows,) + dist.shape, np.float32)
        b = bucket(dist)
        for r in range(32):
            out[r] = (b == r)
        if rows > 32:
            out[:32] *= (dist >= 0)
            out[32] = (dist < 0)
        return out

    c = {}
    c["c_ident"] = np.eye(128, dtype=np.float32)
    c["c_before"] = np.triu(np.ones((128, 128), np.float32), 1)
    for name, dist in (("c_dist_desc", 511 - np.arange(BIASL)), ("c_dist_asc", np.arange(CMPL) - 511)):
        o = onehot(dist, 33)
        c[name] = np.concatenate([o[:32], o[:32], o[:32], o[32:]], 0)
    t = np.arange(TS)[:, None]
    col = np.arange(PAST)
    slc_key = (col % 128) * SUB + col // 128
    win_key = (np.arange(512) % 128) * 4 + np.arange(512) // 128
    tables = {
        "c_oh_slc": PAST + t - slc_key[None],
        "c_oh_win": 512 + t - win_key[None],
        "c_oh_cmp": PAST + t - (np.arange(NCMP_S)[None] * 16 + 31),
    }
    for name, dist in tables.items():
        o = onehot(dist, 32)
        c[name] = np.ascontiguousarray(o.transpose(1, 0, 2).reshape(128, -1))
    c["c_mask_win"] = np.ascontiguousarray(np.tile(
        np.where(512 + t - win_key[None] < 512, 0.0, NEG).astype(np.float32), (32, 1)))
    new = np.zeros((TS, 32, 32), np.float32)
    cols_t = np.arange(32) % TS
    for tt in range(TS):
        new[tt] = onehot(np.maximum(tt - cols_t, 0), 32)
    c["c_oh_new"] = new.reshape(128, 32)
    mask = np.zeros((128, 2, 32), np.float32)
    for row in range(128):
        for r in range(2):
            for cc in range(32):
                ok = cc // TS == 4 * r + row // 32 and cc % TS <= row % TS
                mask[row, r, cc] = 0.0 if ok else NEG
    c["c_mask_new"] = mask.reshape(128, 64)
    covers = np.zeros((NCMP_S, 33), np.float32)
    for n in range(NCMP_S):
        for j in range(33):
            covers[n, j] = (n * 16 < j * 64 + 64) and (n * 16 + 31 >= j * 64)
    c["c_covers"] = covers
    force = np.zeros((128, 33), np.float32)
    force[:, [0, 31, 32]] = 1e30
    c["c_force"] = force
    inv = np.zeros((128, 2, NP_TOK), np.float32)
    for ch in range(256):
        w = (2, 4, 8, 16)[ch // 64]
        inv[ch % 128, ch // 128] = 1.0 / np.minimum(np.arange(NP_TOK) + 1, w)
    c["c_inv_count"] = inv.reshape(128, -1)
    p = np.arange(128)
    c["c_cols"] = np.stack([p, p % 8, p % 32, 1.0 * (p >= 64), 1.0 * (p < 64)], 1).astype(np.float32)
    c["c_iota32"] = np.tile(np.arange(32, dtype=np.float32), (128, 1))
    c["c_token1"] = (1 + np.arange(128)[:, None] + 128 * np.arange(NT)[None]).astype(np.float32)
    c["c_spare_row"] = (NTOK + 1 + np.arange(128)[:, None]).astype(np.float32)
    c["c_iota128"] = np.tile(np.arange(128, dtype=np.float32), (128, 1))
    return c


def lay_out(a):
    f = {}
    f["x_all"] = np.concatenate([a["x_prompt"][0], a["x_sample"].reshape(NS * TS, D)], 0)
    f["mem"] = a["mem_prompt"][0]
    w = a["w_in"][0]
    q0, qm0, c0, s0, w0, gn0, gb0 = 256, 768, 1024, 1280, 1536, 1792, 1816
    q = w[:, q0:qm0].reshape(D, 2, 4, HD).transpose(0, 2, 1, 3).reshape(D, 512)
    gn = w[:, gn0:gb0].reshape(D, 3, 2, 4).transpose(0, 3, 2, 1).reshape(D, 24)
    f["w_tok"] = np.concatenate([q, w[:, qm0:c0], w[:, s0:s0 + 128], w[:, w0:w0 + 128], w[:, c0:s0],
                                 w[:, s0 + 128:s0 + 256], w[:, w0 + 128:w0 + 256], gn], 1)
    f["w_u"] = w[:, :256]
    gb = w[:, gb0:].reshape(KD, 128, 3, KD, 128)
    f["w_gb"] = gb.transpose(3, 2, 1, 0, 4).reshape(KD, 3, 128, KD * 128)
    f["w_mem"] = a["w_mem_kv"][0]
    col = lambda v: v.reshape(KD, 128).T
    f["gain_cols"] = np.concatenate([col(a["norm1_g"][0]), col(a["mem_norm_g"][0]), col(a["norm2_g"][0]),
                                     a["pool_scale"][0].reshape(2, 128).T], 1)
    qk, mq = a["nsa_qk_norm"][0], a["mem_qk_norm"][0]
    f["gain_rows"] = np.concatenate([np.tile(qk[0], 8), np.tile(mq[0], 4), np.tile(qk[2], 2), np.tile(qk[3], 2),
                                     np.tile(mq[1], 4), np.tile(qk[1], 2)])[None]
    rb = a["rel_bias"].reshape(32, 2, 4).transpose(0, 2, 1).reshape(32, 8)
    f["rel_bias"] = rb
    cw = a["cmp_w"][0].reshape(2, 2, 8, 2, HD, HD)
    f["w_cmp"] = cw.transpose(3, 4, 0, 2, 1, 5).reshape(128, 2 * 8 * 128)
    pe = a["cmp_pe"][0].reshape(2, 2, 8, 2, HD)
    f["pe_cmp"] = pe.transpose(3, 4, 0, 2, 1).reshape(128, 32)
    pw = np.zeros((2, 128, 128), np.float32)
    for i in range(4):
        h = 64 * (i % 2)
        pw[i // 2, h:h + 64, h:h + 64] = a["pool_w"][0, i]
    f["w_pool"] = pw
    nsa = a["w_up_nsa"][0].reshape(2, 4, HD, D).transpose(1, 0, 2, 3).reshape(512, D)
    f["w_up"] = np.concatenate([a["w_up_pool"][0], nsa, a["w_up_mem"][0]], 0)
    f["w_out"] = a["w_out"][0]
    f["router_w"] = a["router_w"][0]
    f["router_b"] = a["router_b"]
    f["w_gu"] = a["w_gu"][0]
    f["b_gu"] = a["b_gu"][0]
    f["w_down"] = a["w_down"][0]
    f["b_down"] = a["b_down"][0]
    f["cache_cmp"] = a["cache_cmp_kv"][0].reshape(-1, ROWF)
    f["cache_slc"] = a["cache_slc_kv"][0].reshape(-1, ROWF)
    f["cache_win"] = a["cache_win_kv"][0].reshape(NS, 512, 256)
    f["cache_mem"] = a["cache_mem_kv"][0].reshape(NS, 256, 512)
    f["state_pool"] = a["state_pool"][0]
    f["pages"] = np.repeat(np.asarray(a["page_table"]).T, PAGE // SUB, axis=0)
    return {k: np.ascontiguousarray(v) for k, v in f.items()}


OUTPUTS = {
    "y_prompt": (1, 512, 1024), "y_sample": (8, 4, 1024), "new_cmp_p": (1, 1, 512, 2, 2, 64),
    "new_slc_p": (1, 1, 512, 2, 2, 64), "new_win_p": (1, 1, 512, 2, 2, 64), "new_mem_p": (1, 1, 256, 2, 4, 64),
    "new_pool_p": (1, 1, 15, 256), "new_cmp_s": (1, 8, 4, 2, 2, 64), "new_slc_s": (1, 8, 4, 2, 2, 64),
    "new_win_s": (1, 8, 512, 2, 2, 64), "new_pool_s": (1, 8, 15, 256),
}


def build_program(nc, i, o, stop_after=99):
    ctx = ExitStack()
    with ctx:
        of_phase = []

        def sem(name):
            of_phase.append(nc.alloc_semaphore(name=name))
            return of_phase[-1]

        def lasting(name):
            return nc.alloc_semaphore(name=name)

        def phase_over():
            nc.clear_and_free_semaphores(list(of_phase))
            nc.all_engine_barrier()
            of_phase.clear()

        def scratch(name, shape, dt=F32):
            return nc.dram_tensor(name, shape, dt, kind="Internal").ap()

        arena = ctx.enter_context(nc.sbuf_tensor("arena", [128, 53000], F32))
        psum = ctx.enter_context(nc.psum_tensor("psum", [128, 8, 512], F32))
        cursor = [0]

        def take(*dims, dt=F32):
            n = int(np.prod(dims))
            words = n if dt in (F32, I32, U32) else -(-n // 2)
            at = arena[:, cursor[0]:cursor[0] + words]
            cursor[0] += words + words % 2
            assert cursor[0] <= 53000, cursor[0]
            if dt != F32:
                at = at.bitcast(dt)[:, 0:n]
            if len(dims) == 1:
                return at
            names = "abcd"[:len(dims)]
            return at.rearrange(f"p ({' '.join(names)}) -> p {' '.join(names)}",
                                **{n_: d_ for n_, d_ in zip(names, dims)})

        def bank(b, n=1):
            return psum[:, b] if n == 1 else psum[:, b:b + n]

        ident = take(128)
        ones = take(128)
        x = take(NT, D)
        gain_cols = take(26)
        g1c, gmc, g2c, psc = (gain_cols[:, 8 * n:min(8 * n + 8, 26)] for n in range(4))
        cols = take(6)
        iota32 = take(32)
        sumsq, root, rinv = take(8), take(8), take(8)
        eps = take(1)
        rel_parts = take(8, dt=BF16)
        rel_rest, rel_part = take(8), take(8)
        moe_base = cursor[0]
        w_gb_at = 53000 - 6 * KD * 128
        hT = take(KD, NTOK)
        gates = take(NT, 24)
        oT_at = cursor[0]
        oT_nsa = take(4, NTOK)
        oT_mem = take(2, NTOK)
        oT_pool = take(2, NTOK)
        tail_base = cursor[0]
        qT = take(4, NTOK)
        qmT = take(2, NTOK)
        ksT = take(NTOK)
        kwT = take(NTOK)
        kmT = take(2, MEM)
        v_slc = take(NT, 128)
        v_win = take(NT, 128)
        zm = take(2, 512)
        kcT = take(NS + 1, 128)
        v_cmp = take(NS + 1, 128)
        phase_base = cursor[0]
        mT = take(KD, MEM)
        w_tok = take(KD, WTOK)
        w_mem = take(KD, 512)
        w_u_at = cursor[0]
        w_u = take(KD, 256)
        mem = take(2, D)
        xn = take(2, D)
        zt = arena[:, oT_at:oT_at + 2 * WTOK].rearrange("p (b n) -> p b n", b=2)
        zsq = take(D)
        gain_rows = take(1408)
        ss16, rt16, ri16 = take(16), take(16), take(16)
        cursor[0] = phase_base
        pages = take(NS, dt=I32)
        row_index = take(NS, dt=U32)
        u_prompt = take(2, 16 + NP_TOK)
        u_sample = take(2, NS, 16 + TS)
        sum_a = take(2, 16 + NP_TOK)
        sum_b = take(2, 16 + NP_TOK)
        ssum_a = take(2, NS, 16 + TS)
        ssum_b = take(2, NS, 16 + TS)
        dT = take(2, NTOK)
        inv_count = take(2, NP_TOK)
        w_pool = take(2, 128)
        hist = take(256)
        u_rows = take(2, 256)
        u_new = take(2, NS * TS)
        early_base = cursor[0]
        gain_kc = take(128)
        w_cmp = take(2, 8, 128)
        pe_cmp = take(2, 8, 2)
        sub_rows = take(2, ROWF)
        early_end = cursor[0]
        assert early_end <= w_u_at

        s_cw = lasting("s_cw")
        s_pg = sem("s_pg")
        s_ix = sem("s_ix")
        s_sub = [lasting(f"s_sub{n}") for n in range(2)]
        s_const = sem("s_const")
        s_gain = sem("s_gain")
        s_rel, s_rp = sem("s_rel"), sem("s_rp")
        s_ones = sem("s_ones")
        s_x = [sem(f"s_x{n}") for n in range(7)]
        s_wtok = [sem(f"s_wtok{c}") for c in range(4)]
        s_wmem = sem("s_wmem")
        s_act = sem("s_act")
        s_dve = sem("s_dve")
        s_pool = sem("s_pool")
        s_root = sem("s_root")
        s_xn = sem("s_xn")
        s_tp = sem("s_tp")
        s_hT = sem("s_hT")
        s_zp = sem("s_zp")
        s_ze = sem("s_ze")
        s_sq = sem("s_sq")
        s_ss = sem("s_ss")
        s_rt = sem("s_rt")
        s_zn = sem("s_zn")
        s_vc = sem("s_vc")
        s_gn = sem("s_gn")
        s_zo = [sem(f"s_zo{n}") for n in range(2)]
        s_mo = sem("s_mo")
        s_tq = sem("s_tq")
        s_te = sem("s_te")
        s_cp = sem("s_cp")
        s_up = sem("s_up")
        s_ue = sem("s_ue")
        s_pl = sem("s_pl")
        s_uz = sem("s_uz")
        s_ht = sem("s_ht")
        s_he = sem("s_he")
        s_uo = sem("s_uo")
        s_dT = sem("s_dT")
        s_pp = sem("s_pp")
        s_po = sem("s_po")

        rows_of = lambda n: ROWS[n] if n < NT else 128
        src = lambda n: x[0:rows_of(n), n, :] if n < NT else mem[:, n - NT, :]
        dstT = lambda n: hT[:, :, 128 * n:128 * n + rows_of(n)] if n < NT else mT[:, :, 128 * (n - NT):128 * (n - NT) + 128]
        CH = [(0, 512), (512, 1024), (1024, 1536), (1536, WTOK)]
        tok_rows = lambda ap, n: ap[128 * n:128 * n + ROWS[n]]

        def linked(eng, s, at):
            def link(ins):
                at[0] += 1
                ins.then_inc(s, 1)
                eng.wait_ge(s, at[0])
            return link

        out_cp = o["new_cmp_p"].rearrange("a b t c g d -> (a b t) (c g d)")
        out_sp = o["new_slc_p"].rearrange("a b t c g d -> (a b t) (c g d)")
        out_wp = o["new_win_p"].rearrange("a b t c g d -> (a b t) (c g d)")
        out_cs = o["new_cmp_s"].rearrange("a s t c g d -> (a s t) (c g d)")
        out_ss = o["new_slc_s"].rearrange("a s t c g d -> (a s t) (c g d)")
        out_ws = o["new_win_s"].rearrange("a s t c g d -> (a s) t (c g d)")
        out_mp = o["new_mem_p"].rearrange("a b t c h d -> (a b t) (c h d)")
        out_pp = o["new_pool_p"].rearrange("a b t c -> (a b t) c")
        out_ps = o["new_pool_s"].rearrange("a s t c -> (a s) t c")

        def bf16_parts(link, pool, parts, rest, part_f32):
            for part in range(3):
                q = slice(32 * part, 32 * part + 32)
                link(pool.tensor_copy(parts[q], rest[q]))
                for _ in range(part):
                    link(pool.tensor_copy(part_f32[q], parts[q]))
                    link(pool.tensor_tensor(rest[q], rest[q], part_f32[q], ALU.subtract))
                    link(pool.tensor_copy(parts[q], rest[q]))

        def gather_sub(pool, s):
            pool.indirect_dma_start(sub_rows[:, s % 2], None, i["cache_cmp"],
                                    bass.IndirectOffsetOnAxis(row_index[:, s:s + 1], 0)).then_inc(s_sub[s % 2], 16)

        with nc.Block() as block:

            @block.sync
            def _(sp):
                def load_x(n):
                    r = rows_of(n)
                    from_ = i["x_all"][128 * n:128 * n + r] if n < NT else i["mem"][128 * (n - NT):128 * (n - NT) + 128]
                    sp.dma_start(src(n), from_).then_inc(s_x[n], 16)

                load_x(0)
                for dst, name in ((ident, "c_ident"), (gain_cols, "gain_cols"), (cols[:, 0:5], "c_cols"),
                                  (iota32, "c_iota32")):
                    sp.dma_start(dst, i[name]).then_inc(s_const, 16)
                for part in range(3):
                    sp.dma_start(rel_rest[32 * part:32 * part + 32], i["rel_bias"]).then_inc(s_rel, 16)
                w = i["w_tok"].rearrange("(k p) n -> p k n", p=128)
                for c, (a, b) in enumerate(CH):
                    sp.dma_start(w_tok[:, :, a:b], w[:, :, a:b]).then_inc(s_wtok[c], 16)
                    if c == 0:
                        load_x(1)
                sp.dma_start(gain_rows, i["gain_rows"].partition_broadcast(128).rearrange("p a n -> p (a n)")
                             ).then_inc(s_gain, 16)
                for n in range(2, 7):
                    load_x(n)
                sp.dma_start(w_mem, i["w_mem"].rearrange("(k p) n -> p k n", p=128)).then_inc(s_wmem, 16)
                sp.dma_start(w_u, i["w_u"].rearrange("(k p) n -> p k n", p=128)).then_inc(s_wmem, 16)
                sp.dma_start(out_ws[:, 0:508], i["cache_win"][:, 4:512]).then_inc(s_cp, 16)
                sp.dma_start(out_ps[:, 0:11], i["state_pool"][:, 4:15]).then_inc(s_cp, 16)
                for n in range(NT):
                    r = ROWS[n]
                    z = zt[0:r, n % 2]
                    sp.wait_ge(s_zn, n + 1)
                    sp.wait_ge(s_ze, 4 * n + 4)
                    if n < 4:
                        oc, os_, ow = tok_rows(out_cp, n), tok_rows(out_sp, n), tok_rows(out_wp, n)
                        sp.dma_start(ow[:, 0:128], z[:, 896:1024]).then_inc(s_zo[n % 2], 16)
                        sp.dma_start(ow[:, 128:256], z[:, 1408:1536]).then_inc(s_zo[n % 2], 16)
                    else:
                        oc, os_ = out_cs, out_ss
                        sp.dma_start(out_ws[:, 508:512, 0:128], z[:, 896:1024]).then_inc(s_zo[n % 2], 16)
                        sp.dma_start(out_ws[:, 508:512, 128:256], z[:, 1408:1536]).then_inc(s_zo[n % 2], 16)
                    sp.dma_start(oc, z[:, 1024:1280]).then_inc(s_zo[n % 2], 16)
                    sp.dma_start(os_[:, 0:128], z[:, 768:896]).then_inc(s_zo[n % 2], 16)
                    sp.dma_start(os_[:, 128:256], z[:, 1280:1408]).then_inc(s_zo[n % 2], 16)
                sp.wait_ge(s_zn, NT + 2)
                sp.wait_ge(s_ze, 22)
                sp.dma_start(out_mp.rearrange("(m p) c -> p m c", p=128), zm).then_inc(s_mo, 16)
                sp.wait_ge(s_zp, 22)
                sp.dma_start(pages, i["pages"]).then_inc(s_pg, 16)
                sp.dma_start(inv_count, i["c_inv_count"].rearrange("p (k t) -> p k t", k=2)).then_inc(s_pl, 16)
                sp.dma_start(w_pool, i["w_pool"].rearrange("k p n -> p k n")).then_inc(s_pl, 16)
                sp.dma_start(hist[0:120], i["state_pool"].rearrange("s t c -> (s t) c")).then_inc(s_pl, 16)
                sp.dma_start(w_cmp, i["w_cmp"].rearrange("p (c j m) -> p c j m", c=2, j=8)).then_inc(s_cw, 16)
                sp.dma_start(pe_cmp, i["pe_cmp"].rearrange("p (c j r) -> p c j r", c=2, j=8)).then_inc(s_cw, 16)
                sp.dma_start(gain_kc, i["gain_rows"][:, 1280:1408].partition_broadcast(128)
                             .rearrange("p a n -> p (a n)")).then_inc(s_cw, 16)
                sp.wait_ge(s_he, 4)
                sp.dma_start(out_pp, u_rows[0:15, 0]).then_inc(s_uo, 16)
                sp.dma_start(out_ps[:, 11:15], u_rows[0:32, 1]).then_inc(s_uo, 16)
                sp.wait_ge(s_zo[0], 16 * 15)
                sp.wait_ge(s_zo[1], 16 * 10)
                sp.wait_ge(s_mo, 16)
                sp.wait_ge(s_cp, 32)
                sp.wait_ge(s_uo, 32)

            @block.scalar
            def _(act):
                link = linked(act, s_act, [0])
                act.wait_ge(s_ones, 2)
                act.wait_ge(s_const, 64)
                for n in range(7):
                    r = rows_of(n)
                    act.wait_ge(s_x[n], 16)
                    link(act.activation(zsq[0:r], src(n), ACT.Square, accum_out=sumsq[0:r, n:n + 1]))
                    act.activation(root[0:r, n:n + 1], sumsq[0:r, n:n + 1], ACT.Sqrt, bias=eps[0:r],
                                   scale=1.0 / D).then_inc(s_root, 1)

                def evacuate(n):
                    r = ROWS[n]
                    if n >= 2:
                        act.wait_ge(s_zo[n % 2], 80 * (n // 2))
                        act.wait_ge(s_tq, 2 * n - 2)
                        act.wait_ge(s_vc, n - 1)
                    for c, (a, b) in enumerate(CH):
                        act.wait_ge(s_zp, 4 * n + c + 1)
                        act.activation(zt[0:r, n % 2, a:b], bank(2 + c)[0:r, 0:b - a], ACT.Copy).then_inc(s_ze, 1)

                def evacuate_mem(m):
                    act.wait_ge(s_zp, 21 + m)
                    act.activation(zm[:, m], bank(2 + m), ACT.Copy).then_inc(s_ze, 1)

                def roots(n):
                    r = rows_of(n)
                    act.wait_ge(s_ss, n + 1)
                    act.activation(rt16[0:r], ss16[0:r], ACT.Sqrt, bias=eps[0:r], scale=1.0 / HD).then_inc(s_rt, 1)

                def heads_out(n):
                    r = ROWS[n]
                    t = slice(128 * n, 128 * n + r)
                    act.wait_ge(s_tq, 2 * n + 1)
                    act.activation(qT[:, :, t], bank(6)[:, 0:4 * r].rearrange("p (a b) -> p a b", a=4), ACT.Copy,
                                   scale=QSCALE).then_inc(s_te, 1)
                    act.wait_ge(s_tq, 2 * n + 2)
                    b7 = bank(7)[:, 0:4 * r].rearrange("p (a b) -> p a b", a=4)
                    act.activation(qmT[:, :, t], b7[:, 0:2], ACT.Copy, scale=QSCALE).then_inc(s_te, 1)
                    act.activation(ksT[:, t], b7[:, 2], ACT.Copy).then_inc(s_te, 1)
                    act.activation(kwT[:, t], b7[:, 3], ACT.Copy).then_inc(s_te, 1)

                def keys_out(m):
                    act.wait_ge(s_tq, 11 + m)
                    act.activation(kmT[:, :, 128 * m:128 * m + 128],
                                   bank(7)[:, 0:256].rearrange("p (a b) -> p a b", a=2), ACT.Copy).then_inc(s_te, 1)

                for n in range(NT):
                    evacuate(n)
                    roots(n)
                    act.wait_ge(s_ze, 4 * n + 4)
                    act.activation(gates[0:ROWS[n], n], zt[0:ROWS[n], n % 2, 1536:WTOK], ACT.Sigmoid).then_inc(s_gn, 1)
                    if n >= 2:
                        heads_out(n - 2)
                for m in range(2):
                    evacuate_mem(m)
                    roots(NT + m)
                    heads_out(NT - 2 + m)
                for m in range(2):
                    keys_out(m)
                act.wait_ge(s_uz, 1)
                for k in range(2):
                    act.wait_ge(s_up, 2 * k + 1)
                    act.activation(u_prompt[:, k, 16:16 + HALF], bank(2 + 2 * k)[:, 0:HALF], ACT.Copy).then_inc(s_ue, 1)
                    act.wait_ge(s_up, 2 * k + 2)
                    b = bank(3 + 2 * k)
                    act.activation(u_prompt[:, k, 16 + HALF:], b[:, 0:NP_TOK - HALF], ACT.Copy).then_inc(s_ue, 1)
                    act.activation(u_sample[:, k, :, 16:], b[:, NP_TOK - HALF:HALF].rearrange("p (s t) -> p s t", t=TS),
                                   ACT.Copy).then_inc(s_ue, 1)
                    act.activation(u_new[:, k], b[:, NP_TOK - HALF:HALF], ACT.Copy).then_inc(s_ue, 1)
                for k in range(2):
                    act.wait_ge(s_ht, k + 1)
                    act.activation(u_sample[:, k, :, 1:16], bank(6 + k)[:, 0:120].rearrange("p (s t) -> p s t", t=15),
                                   ACT.Copy).then_inc(s_he, 1)
                act.wait_ge(s_ht, 3)
                act.activation(u_rows[0:15, 0], bank(0)[0:15, 0:256], ACT.Copy).then_inc(s_he, 1)
                act.wait_ge(s_ht, 4)
                act.activation(u_rows[0:32, 1], bank(1)[0:32, 0:256], ACT.Copy).then_inc(s_he, 1)
                for k in range(2):
                    for h in range(2):
                        act.wait_ge(s_pp, 2 * k + h + 1)
                        act.activation(oT_pool[:, k, h * HALF:(h + 1) * HALF], bank(2 + 2 * k + h)[:, 0:HALF], ACT.Copy,
                                       scale=psc[:, k:k + 1]).then_inc(s_po, 1)

            @block.vector
            def _(dve):
                link = linked(dve, s_dve, [0])
                dve.memset(ones, 1.0).then_inc(s_ones, 1)
                dve.memset(eps, EPS).then_inc(s_ones, 1)
                dve.wait_ge(s_const, 64)

                def norm(n):
                    r = rows_of(n)
                    dve.wait_ge(s_root, n + 1)
                    link(dve.reciprocal(rinv[0:r, n:n + 1], root[0:r, n:n + 1]))
                    if n >= 2:
                        dve.wait_ge(s_tp, 2 * n - 2)
                    dve.tensor_scalar(xn[0:r, n % 2], src(n), rinv[0:r, n:n + 1], None, ALU.mult).then_inc(s_xn, 1)

                def to_hT(n):
                    r = rows_of(n)
                    g = g1c if n < NT else gmc
                    for h in range(2):
                        dve.wait_ge(s_tp, 2 * n + h + 1)
                        dve.tensor_tensor(dstT(n)[:, 4 * h:4 * h + 4], bank(h)[:, 0:4 * r].rearrange("p (a b) -> p a b", a=4),
                                          g[:, 4 * h:4 * h + 4].unsqueeze(2).to_broadcast([128, 4, r]),
                                          ALU.mult).then_inc(s_hT, 1)

                def head_norm(n):
                    r = rows_of(n)
                    heads = 16 if n < NT else 4
                    z = zt[0:r, n % 2, 0:D] if n < NT else zm[:, n - NT, 0:256]
                    g = gain_rows[0:r, 0:D] if n < NT else gain_rows[0:r, D:D + 256]
                    zh = z.rearrange("p (h d) -> p h d", d=HD)
                    dve.wait_ge(s_sq, n + 1)
                    dve.tensor_reduce(ss16[0:r, 0:heads], zsq[0:r, 0:heads * HD].rearrange("p (h d) -> p h d", d=HD),
                                      AX, ALU.add).then_inc(s_ss, 1)
                    dve.wait_ge(s_rt, n + 1)
                    link(dve.reciprocal(ri16[0:r, 0:heads], rt16[0:r, 0:heads]))
                    link(dve.tensor_tensor(zh, zh, ri16[0:r, 0:heads].unsqueeze(2).to_broadcast([r, heads, HD]), ALU.mult))
                    dve.tensor_tensor(z, z, g, ALU.mult).then_inc(s_zn, 1)

                norm(0)
                for n in range(1, 7):
                    norm(n)
                    to_hT(n - 1)
                    if n == 3:
                        dve.wait_ge(s_gain, 16)
                    if n >= 3:
                        head_norm(n - 3)
                to_hT(6)
                for n in range(4, 7):
                    head_norm(n)
                dve.wait_ge(s_zp, 22)
                dve.memset(u_prompt[:, :, 0:16], 0.0).then_inc(s_uz, 1)
                dve.wait_ge(s_pg, 16)
                dve.tensor_scalar(row_index, pages, float(PAGE // SUB), cols[:, 1:2], ALU.mult,
                                  ALU.add).then_inc(s_ix, 1)
                dve.wait_ge(s_ue, 8)
                dve.wait_ge(s_he, 2)
                dve.wait_ge(s_pl, 48)
                dve.wait_ge(s_uz, 1)
                u, a, b = u_prompt, sum_a, sum_b
                us, sa, sb_ = u_sample, ssum_a, ssum_b
                W = 16 + NP_TOK
                WS = 16 + TS
                link(dve.tensor_tensor(a[:, :, 1:W], u[:, :, 1:W], u[:, :, 0:W - 1], ALU.add))
                link(dve.tensor_tensor(b[:, :, 3:W], a[:, :, 3:W], a[:, :, 1:W - 2], ALU.add))
                link(dve.tensor_copy(a[64:128, 0, 16:W], b[64:128, 0, 16:W]))
                link(dve.tensor_tensor(a[:, 1, 7:W], b[:, 1, 7:W], b[:, 1, 3:W - 4], ALU.add))
                link(dve.tensor_tensor(b[:, 1, 15:W], a[:, 1, 15:W], a[:, 1, 7:W - 8], ALU.add))
                link(dve.tensor_copy(a[64:128, 1, 16:W], b[64:128, 1, 16:W]))
                link(dve.tensor_tensor(a[:, :, 16:W], a[:, :, 16:W], inv_count, ALU.mult))
                dve.tensor_tensor(dT[:, :, 0:NP_TOK], a[:, :, 16:W], u[:, :, 16:W], ALU.subtract).then_inc(s_dT, 1)
                for k in range(2):
                    x_, y_, z_ = us[:, k], sa[:, k], sb_[:, k]
                    link(dve.tensor_tensor(y_[:, :, 2:WS], x_[:, :, 2:WS], x_[:, :, 1:WS - 1], ALU.add))
                    link(dve.tensor_tensor(z_[:, :, 4:WS], y_[:, :, 4:WS], y_[:, :, 2:WS - 2], ALU.add))
                    if k == 0:
                        link(dve.tensor_copy(y_[64:128, :, 16:WS], z_[64:128, :, 16:WS]))
                    else:
                        link(dve.tensor_tensor(y_[:, :, 8:WS], z_[:, :, 8:WS], z_[:, :, 4:WS - 4], ALU.add))
                        link(dve.tensor_tensor(z_[64:128, :, 16:WS], y_[64:128, :, 16:WS], y_[64:128, :, 8:WS - 8], ALU.add))
                        link(dve.tensor_copy(y_[64:128, :, 16:WS], z_[64:128, :, 16:WS]))
                    for h in range(2):
                        q = slice(64 * h, 64 * h + 64)
                        link(dve.tensor_scalar(z_[q, :, 16:WS], y_[q, :, 16:WS], 1.0 / (2, 4, 8, 16)[2 * k + h], None, ALU.mult))
                    dve.tensor_tensor(dT[:, k, NP_TOK:].rearrange("p (s t) -> p s t", t=TS), z_[:, :, 16:WS],
                                      x_[:, :, 16:WS], ALU.subtract).then_inc(s_dT, 1)

            @block.gpsimd
            def _(pool):
                pool.wait_ge(s_rel, 48)
                bf16_parts(linked(pool, s_rp, [0]), pool, rel_parts, rel_rest, rel_part)
                for n in range(NT + 2):
                    r = rows_of(n)
                    if n:
                        pool.wait_ge(s_ss, n)
                    if n == 0:
                        pool.wait_ge(s_root, 7)
                    if n < NT:
                        pool.wait_ge(s_ze, 4 * n + 2)
                        z = zt[0:r, n % 2, 0:D]
                        pool.tensor_tensor(zsq[0:r], z, z, ALU.mult).then_inc(s_sq, 1)
                        pool.wait_ge(s_ze, 4 * n + 3)
                        pool.tensor_copy(v_slc[0:r, n], zt[0:r, n % 2, 1280:1408])
                        pool.tensor_copy(v_win[0:r, n], zt[0:r, n % 2, 1408:1536]).then_inc(s_vc, 1)
                    else:
                        pool.wait_ge(s_ze, 16 + n)
                        z = zm[:, n - NT, 0:256]
                        pool.tensor_tensor(zsq[:, 0:256], z, z, ALU.mult).then_inc(s_sq, 1)
                pool.wait_ge(s_zp, 22)
                pool.wait_ge(s_ix, 1)
                for s in range(2):
                    gather_sub(pool, s)

            @block.tensor
            def _(pe):
                pe.wait_ge(s_const, 64)

                def transposes(n):
                    r = rows_of(n)
                    pe.wait_ge(s_xn, n + 1)
                    for h in range(2):
                        if n:
                            pe.wait_ge(s_hT, 2 * n - 1 + h)
                        for k in range(4):
                            mm = pe.transpose(bank(h)[:, k * r:(k + 1) * r],
                                              xn[0:r, n % 2, (4 * h + k) * 128:(4 * h + k + 1) * 128], ident[0:r, 0:r])
                        mm.then_inc(s_tp, 1)

                def project(n):
                    r = rows_of(n)
                    pe.wait_ge(s_hT, 2 * n + 2)
                    if n < NT:
                        for c, (a, b) in enumerate(CH):
                            if n == 0:
                                pe.wait_ge(s_wtok[c], 16)
                            if n:
                                pe.wait_ge(s_ze, 4 * n - 3 + c)
                            for k in range(KD):
                                mm = pe.matmul(bank(2 + c)[0:r, 0:b - a], dstT(n)[:, k], w_tok[:, k, a:b],
                                               start=(k == 0), stop=(k == KD - 1))
                            mm.then_inc(s_zp, 1)
                    else:
                        if n == NT:
                            pe.wait_ge(s_wmem, 32)
                        pe.wait_ge(s_ze, 17 + n - NT)
                        for k in range(KD):
                            mm = pe.matmul(bank(2 + n - NT), dstT(n)[:, k], w_mem[:, k], start=(k == 0), stop=(k == KD - 1))
                        mm.then_inc(s_zp, 1)

                def heads(n):
                    pe.wait_ge(s_zn, n + 1)
                    if n < NT:
                        r = ROWS[n]
                        z = zt[0:r, n % 2]
                        if n:
                            pe.wait_ge(s_te, 4 * n - 3)
                        for p in range(4):
                            mm = pe.transpose(bank(6)[:, p * r:(p + 1) * r], z[:, p * 128:p * 128 + 128], ident[0:r, 0:r])
                        mm.then_inc(s_tq, 1)
                        if n:
                            pe.wait_ge(s_te, 4 * n)
                        for p in range(4):
                            mm = pe.transpose(bank(7)[:, p * r:(p + 1) * r], z[:, 512 + p * 128:640 + p * 128],
                                              ident[0:r, 0:r])
                        mm.then_inc(s_tq, 1)
                    else:
                        pe.wait_ge(s_te, 20 + n - NT)
                        for p in range(2):
                            mm = pe.transpose(bank(7)[:, p * 128:(p + 1) * 128], zm[:, n - NT, p * 128:p * 128 + 128], ident)
                        mm.then_inc(s_tq, 1)

                transposes(0)
                for n in range(1, 7):
                    transposes(n)
                    project(n - 1)
                    if n >= 3:
                        heads(n - 3)
                project(6)
                for n in range(4, 7):
                    heads(n)
                pe.wait_ge(s_ze, 22)
                for k in range(2):
                    for h in range(2):
                        for kk in range(KD):
                            mm = pe.matmul(bank(2 + 2 * k + h)[:, 0:HALF], w_u[:, kk, k * 128:k * 128 + 128],
                                           hT[:, kk, h * HALF:(h + 1) * HALF], start=(kk == 0), stop=(kk == KD - 1))
                        mm.then_inc(s_up, 1)
                pe.wait_ge(s_te, 22)
                pe.wait_ge(s_pl, 48)
                for k in range(2):
                    pe.transpose(bank(6 + k)[:, 0:120], hist[0:120, k * 128:k * 128 + 128], ident[0:120, 0:120]
                                 ).then_inc(s_ht, 1)
                pe.wait_ge(s_ue, 8)
                for k in range(2):
                    mm = pe.transpose(bank(0)[0:15, k * 128:k * 128 + 128], u_prompt[:, k, 16 + NP_TOK - 15:], ident)
                mm.then_inc(s_ht, 1)
                for k in range(2):
                    mm = pe.transpose(bank(1)[0:32, k * 128:k * 128 + 128], u_new[:, k], ident)
                mm.then_inc(s_ht, 1)
                pe.wait_ge(s_dT, 3)
                for k in range(2):
                    for h in range(2):
                        pe.matmul(bank(2 + 2 * k + h)[:, 0:HALF], w_pool[:, k], dT[:, k, h * HALF:(h + 1) * HALF],
                                  start=True, stop=True).then_inc(s_pp, 1)

        phase_over()
        cursor[0] = phase_base + 16
        pe_bias = take(2)
        kvT = take(2, 8, 2, 128)
        parts = take(2, 2, 128)
        both_halves = take(64)
        kc_sq = take(128)
        kn = take(128)
        kc_ss, kc_rt, kc_ri = take(2), take(2), take(2)
        assert cursor[0] <= early_base
        cursor[0] = phase_base + 16
        cache = take(4, ROWF)
        cursor[0] = max(cursor[0], early_end)
        rel_rows = take(128)
        rel4 = take(8)
        oh_cmp = take(NCMP_S)
        oh_new = take(32)
        mask_new = take(2, 32)
        covers = take(33)
        force = take(33)
        bias_cmp = take(128)
        bias_new = take(2, 32)
        bias_win = take(512)
        bias_slc = take(PAST)
        q_rows = take(NS, 32)
        qm_rows = take(2, NS, 32)
        gate_rows = take(2, 3)
        keysT = take(PAST)
        scores = take(PAST + 32)
        probT = take(17, 128)
        o_rows = take(128)
        p_cmp = take(128)
        p_sum = take(32)
        p_exp = take(128)
        pick = take(4, 33)
        top8 = take(8)
        top8b = take(8)
        stats = take(16)
        oh_slc = scores[:, 0:PAST]
        oh_win = keysT[:, 0:512]

        gate_scratch = scratch("gate_scratch", [NS * NH * TS, 3])

        s_sc = lasting("s_sc")
        s_gs = sem("s_gs")
        s_gl = lasting("s_gl")
        s_subp = sem("s_subp")
        s_ct = sem("s_ct")
        s_kv = sem("s_kv")
        s_cw_mm = sem("s_cw_mm")
        s_pa = sem("s_pa")
        s_bl = sem("s_bl")
        s_kq = sem("s_kq")
        s_ksum = sem("s_ksum")
        s_kr = sem("s_kr")
        s_kn = sem("s_kn")
        s_vcm = sem("s_vcm")
        s_kt = sem("s_kt")
        s_kc = sem("s_kc")
        s_pb = sem("s_pb")
        s_pbe = sem("s_pbe")
        s_d2 = sem("s_d2")
        s_bh = sem("s_bh")

        subs = lambda s: NSUB if s < NS else NP_TOK // SUB

        with nc.Block() as block:
            @block.sync
            def _(sp):
                for s in range(NS):
                    sp.dma_start(gate_scratch[32 * s:32 * s + 32].rearrange("(h t) n -> t h n", h=NH),
                                 gates[4 * s:4 * s + 4, 4].rearrange("t (h n) -> t h n", n=3)
                                 ).then_inc(s_gs, 16)
                for t in range(TS):
                    sp.dma_start(rel4[32 * t:32 * t + 32], i["rel_bias"]).then_inc(s_sc, 16)
                for dst, name in ((oh_cmp, "c_oh_cmp"), (oh_new, "c_oh_new"), (covers[0:NCMP_S], "c_covers"),
                                  (force, "c_force"), (oh_slc, "c_oh_slc"), (oh_win, "c_oh_win"),
                                  (bias_win, "c_mask_win")):
                    sp.dma_start(dst, i[name]).then_inc(s_sc, 16)
                sp.dma_start(mask_new, i["c_mask_new"].rearrange("p (r c) -> p r c", r=2)).then_inc(s_sc, 16)
                sp.wait_ge(s_gs, 16 * NS)
                sp.dma_start(gate_rows, gate_scratch.rearrange("(r p) n -> p r n", r=2)).then_inc(s_gl, 16)
                sp.wait_ge(s_ct, 8 * 7)
                sp.dma_start(sub_rows[0:32, 0], out_cp.rearrange("(n t) c -> n (t c)", t=SUB)).then_inc(s_subp, 16)

            @block.gpsimd
            def _(pool):
                for s in range(2, NS):
                    pool.wait_ge(s_ct, 8 * (s - 1))
                    gather_sub(pool, s)

            def copy_group(eng, copy, s, c, q):
                n = subs(s)
                eng.wait_ge(s_ct, 8 * s + 4 * c + q + 1)
                if s:
                    eng.wait_ge(s_cw_mm, 2 * s - 1 + c)
                b = bank(q)[:, 0:4 * n].rearrange("p (j a n) -> p j a n", j=2, a=2)
                for g in range(2):
                    for a in range(2):
                        copy(kvT[64 * a:64 * a + 64, c, 2 * q:2 * q + 2, g, 0:n],
                             b[64 * g:64 * g + 64, :, a]).then_inc(s_kv, 1)

            @block.scalar
            def _(act):
                act.wait_ge(s_pb, 1)
                for r in range(2):
                    q = slice(64 * r, 64 * r + 64)
                    act.activation(pe_bias[q, :], bank(7)[q, 0:4].rearrange("p (c r) -> p r c", r=2)[:, r],
                                   ACT.Copy).then_inc(s_pbe, 1)
                act.wait_ge(s_pbe, 2)
                cp = lambda a, b: act.activation(a, b, ACT.Copy)

                def after(s):
                    n = subs(s) - 1
                    act.wait_ge(s_bl, s + 1)
                    if s:
                        act.wait_ge(s_ksum, s)
                    act.activation(kc_sq[0:n], bank(6)[0:n, 0:128], ACT.Square).then_inc(s_kq, 1)
                    act.activation(v_cmp[0:n, s], bank(6)[0:n, 128:256], ACT.Copy).then_inc(s_vcm, 1)
                    act.wait_ge(s_ksum, s + 1)
                    act.activation(kc_rt[0:n], kc_ss[0:n], ACT.Sqrt, bias=eps[0:n], scale=1.0 / HD).then_inc(s_kr, 1)
                    act.wait_ge(s_kt, s + 1)
                    act.activation(kcT[:, s, 0:n], bank(7)[:, 0:n], ACT.Copy).then_inc(s_kc, 1)

                for s in range(NS + 1):
                    for c in range(2):
                        for q in (0, 2):
                            copy_group(act, cp, s, c, q)
                        if c == 0 and s:
                            after(s - 1)
                    for c in range(2):
                        act.wait_ge(s_cw_mm, 2 * s + c + 1)
                        if s:
                            act.wait_ge(s_bl, s)
                        n = subs(s)
                        sums = bank(4 + c)[:, 0:2 * n].rearrange("p (g n) -> p g n", g=2)
                        for r in range(2):
                            q = slice(64 * r, 64 * r + 64)
                            act.activation(parts[q, c, :, 0:n - 1], sums[q, :, r:r + n - 1], ACT.Identity,
                                           bias=pe_bias[q, c:c + 1]).then_inc(s_pa, 1)
                after(NS)

            @block.vector
            def _(dve):
                link = linked(dve, s_d2, [0])
                dve.tensor_tensor(both_halves, ident[:, 0:64], ident[:, 64:128], ALU.add).then_inc(s_bh, 1)
                dve.wait_ge(s_cw, 48)
                cp = dve.tensor_copy

                def after(s):
                    n = subs(s) - 1
                    heads = lambda ap: ap.rearrange("p (g d) -> p g d", g=2)
                    dve.wait_ge(s_kq, s + 1)
                    dve.tensor_reduce(kc_ss[0:n], heads(kc_sq[0:n]), AX, ALU.add).then_inc(s_ksum, 1)
                    dve.wait_ge(s_kr, s + 1)
                    link(dve.reciprocal(kc_ri[0:n], kc_rt[0:n]))
                    if s:
                        dve.wait_ge(s_kt, s)
                    link(dve.tensor_tensor(heads(kn[0:n]), heads(bank(6)[0:n, 0:128]),
                                           kc_ri[0:n].unsqueeze(2).to_broadcast([n, 2, HD]), ALU.mult))
                    dve.tensor_tensor(kn[0:n], kn[0:n], gain_kc[0:n], ALU.mult).then_inc(s_kn, 1)

                for s in range(NS + 1):
                    for c in range(2):
                        for q in (1, 3):
                            copy_group(dve, cp, s, c, q)
                        if c == 0 and s:
                            after(s - 1)
                after(NS)

            @block.tensor
            def _(pe):
                pe.wait_ge(s_bh, 1)
                pe.wait_ge(s_cw, 48)
                for c in range(2):
                    for j in range(8):
                        mm = pe.matmul(bank(7)[:, 2 * c:2 * c + 2], w_cmp[:, c, j], pe_cmp[:, c, j],
                                       start=(j == 0), stop=(j == 7))
                mm.then_inc(s_pb, 1)

                def tokens(s, c):
                    n = subs(s)
                    if c == 0:
                        pe.wait_ge(*((s_sub[s % 2], 16 * (s // 2 + 1)) if s < NS else (s_subp, 16)))
                    rows = sub_rows[0:n, s % 2].rearrange("p (t c f) -> p t c f", t=SUB, c=2)
                    for q in range(4):
                        group = 8 * s + 4 * c + q
                        if group >= 4:
                            pe.wait_ge(s_kv, 16 * (group // 4))
                        for t in range(4):
                            mm = pe.transpose(bank(q)[:, t * n:(t + 1) * n], rows[:, 4 * q + t, c], ident[0:n, 0:n])
                        mm.then_inc(s_ct, 1)

                def products(s, c):
                    n = subs(s)
                    pe.wait_ge(s_kv, 16 * (2 * s + c + 1))
                    if s:
                        pe.wait_ge(s_pa, 2 * (2 * s - 1 + c))
                    for j in range(8):
                        mm = pe.matmul(bank(4 + c)[:, 0:2 * n].rearrange("p (g n) -> p g n", g=2), w_cmp[:, c, j],
                                       kvT[:, c, j, :, 0:n], start=(j == 0), stop=(j == 7))
                    mm.then_inc(s_cw_mm, 1)

                def blocks(s):
                    n = subs(s) - 1
                    pe.wait_ge(s_pa, 4 * s + 4)
                    if s:
                        pe.wait_ge(s_kn, s)
                        pe.wait_ge(s_vcm, s)
                    for c in range(2):
                        for g in range(2):
                            out = bank(6)[0:n, 128 * c + 64 * g:128 * c + 64 * g + 64]
                            mm = pe.matmul(out, parts[:, c, g, 0:n], both_halves, start=True, stop=True)
                    mm.then_inc(s_bl, 1)

                def keys(s):
                    n = subs(s) - 1
                    pe.wait_ge(s_kn, s + 1)
                    if s:
                        pe.wait_ge(s_kc, s)
                    else:
                        pe.wait_ge(s_pbe, 2)
                    pe.transpose(bank(7)[:, 0:n], kn[0:n], ident[0:n, 0:n]).then_inc(s_kt, 1)

                for s in range(NS + 1):
                    tokens(s, 0)
                    if s:
                        blocks(s - 1)
                    tokens(s, 1)
                    if s:
                        keys(s - 1)
                    for c in range(2):
                        products(s, c)
                blocks(NS)
                keys(NS)

        phase_over()
        s_rr = sem("s_rr")
        s_bp = sem("s_bp")
        s_be = sem("s_be")
        s_qr = sem("s_qr")
        s_cs = [sem(f"s_cs{n}") for n in range(4)]
        s_wl = [sem(f"s_wl{n}") for n in range(4)]
        s_vu = sem("s_vu")
        s_tk = sem("s_tk")
        s_ke = sem("s_ke")
        s_sp = sem("s_sp")
        s_sr = sem("s_sr")
        s_mx = sem("s_mx")
        s_ex = sem("s_ex")
        s_pt = sem("s_pt")
        s_pe_ = sem("s_pe")
        s_op = sem("s_op")
        s_or = sem("s_or")
        s_im = sem("s_im")
        s_px = sem("s_px")
        s_ot = sem("s_ot")
        s_oe = sem("s_oe")
        s_d3 = sem("s_d3")
        s_pcn = sem("s_pcn")

        C, S, W_, M = range(4)

        with nc.Block() as block:
            @block.sync
            def _(sp):
                for r in range(2):
                    for s in range(4):
                        sp.wait_ge(s_vu, 4 * r + s + 1)
                        sp.dma_start(cache[:, s, 0:1024], i["cache_win"][4 * r + s].rearrange("(p a) c -> p (a c)", p=128)
                                     ).then_inc(s_wl[s], 16)
                        sp.dma_start(cache[:, s, 1024:2048],
                                     i["cache_mem"][4 * r + s].rearrange("(p a) c -> p (a c)", p=128)).then_inc(s_wl[s], 16)

            @block.gpsimd
            def _(pool):
                for r in range(2):
                    if r:
                        pool.wait_ge(s_op, 3)
                    for s in range(4):
                        pool.indirect_dma_start(cache[:, s], None, i["cache_slc"],
                                                bass.IndirectOffsetOnAxis(row_index[:, 4 * r + s:4 * r + s + 1], 0)
                                                ).then_inc(s_cs[s], 16)

            def groups():
                for r in range(2):
                    for b, per in ((S, 4), (W_, 1), (M, 1)):
                        for s in range(4):
                            for q in range(per):
                                yield r, b, s, q
            GROUPS = list(groups())

            def copies_keys(eng, copy, mine):
                def run(r, b):
                    for n, (r_, b_, s, q) in enumerate(GROUPS):
                        if (r_, b_) != (r, b):
                            continue
                        if n % 2 == mine:
                            eng.wait_ge(s_tk, n + 1)
                            if n >= 1:
                                eng.wait_ge(s_sp, score_count(n))
                            dst = keysT[:, 512 * q:512 * q + 512] if b == S else keysT[:, 512 * (s % 4):512 * (s % 4) + 512]
                            copy(dst, bank(5 + n % 2)).then_inc(s_ke_of[mine], 1)
                return run
            s_ke_of = [sem("s_ke_act"), sem("s_ke_dve")]

            def score_count(n):
                r, b, s, q = GROUPS[n]
                if b == S:
                    base = SP0 * r + 1
                    if s == 0:
                        return SP0 * r if r else 1
                    return base + 4 * (s - 1) + q + 1
                if b == W_:
                    return SP0 * r + 1 + 16 + 1
                return SP0 * r + 1 + 16 + 1 + s + 1
            SP0 = 27

            @block.scalar
            def _(act):
                copy = lambda a, b: act.activation(a, b, ACT.Copy)
                keys = copies_keys(act, copy, 0)

                def exponentials(k, cols, r):
                    act.wait_ge(s_mx, k + 1)
                    act.activation(scores[:, 0:cols], scores[:, 0:cols], ACT.Exp, bias=stats[:, 4 * (k % 4):4 * (k % 4) + 1],
                                   accum_out=stats[:, 4 * (k % 4) + 1:4 * (k % 4) + 2]).then_inc(s_ex, 1)

                for r in range(2):
                    k = 4 * r
                    act.wait_ge(s_mx, k + 1)
                    act.activation(p_cmp[:, 0:NCMP_S], p_cmp[:, 0:NCMP_S], ACT.Exp, bias=stats[:, 0:1],
                                   accum_out=stats[:, 1:2]).then_inc(s_ex, 1)
                    keys(r, S)
                    exponentials(k + 1, PAST + 32, r)
                    keys(r, W_)
                    exponentials(k + 2, 512 + 32, r)
                    keys(r, M)
                    exponentials(k + 3, MEM, r)
                    act.wait_ge(s_ot, 2 * r + 1)
                    for g in range(2):
                        q = slice(64 * g, 64 * g + 64)
                        rows = bank(7)[q, 0:128].rearrange("d (s p g t) -> d g p s t", s=4, p=4, g=2)[:, g]
                        for p in range(4):
                            act.activation(oT_nsa[q, p, NP_TOK + 16 * r:NP_TOK + 16 * r + 16].rearrange("d (s t) -> d s t", s=4),
                                           rows[:, p], ACT.Copy).then_inc(s_oe, 1)
                    act.wait_ge(s_ot, 2 * r + 2)
                    for mp in range(2):
                        for m2 in range(2):
                            q = slice(64 * m2, 64 * m2 + 64)
                            rows = bank(7)[q, 128 + 128 * mp:256 + 128 * mp].rearrange("d (s m t) -> d m s t", s=4, t=4)
                            act.activation(oT_mem[q, mp, NP_TOK + 16 * r:NP_TOK + 16 * r + 16].rearrange("d (s t) -> d s t", s=4),
                                           rows[:, 2 * mp + m2], ACT.Copy).then_inc(s_oe, 1)

            @block.vector
            def _(dve):
                link = linked(dve, s_d3, [0])
                copy = dve.tensor_copy
                keys = copies_keys(dve, copy, 1)
                dve.wait_ge(s_sc, 16 * 12)
                link(dve.memset(rel_rows, 0.0))
                for t in range(TS):
                    q = slice(32 * t, 32 * t + 32)
                    dst = rel_rows[q].rearrange("b (s h t) -> b t s h", s=4, t=TS)[:, t]
                    dve.tensor_copy(dst, rel4[q].unsqueeze(1).to_broadcast([32, 4, 8])).then_inc(s_rr, 1)
                link(dve.memset(q_rows, 0.0))
                link(dve.memset(qm_rows, 0.0))
                for g in range(2):
                    q = slice(64 * g, 64 * g + 64)
                    for s in range(NS):
                        src = qT[q, :, NP_TOK + 4 * s:NP_TOK + 4 * s + 4]
                        dst = q_rows[q, s].rearrange("d (p g t) -> d g p t", p=4, g=2)[:, g]
                        dve.tensor_copy(dst, src).then_inc(s_qr, 1)
                for mp in range(2):
                    for m2 in range(2):
                        q = slice(64 * m2, 64 * m2 + 64)
                        m = 2 * mp + m2
                        dve.tensor_copy(qm_rows[q, mp, :, 4 * m:4 * m + 4],
                                        qmT[q, mp, NP_TOK:].rearrange("d (s t) -> d s t", t=4)).then_inc(s_qr, 1)
                dve.wait_ge(s_bp, 1)
                dve.tensor_copy(bias_slc.rearrange("p (b n) -> p b n", b=4), bank(0, 4)).then_inc(s_be, 1)
                dve.tensor_tensor(bias_win, bias_win, bank(4), ALU.add).then_inc(s_be, 1)
                dve.tensor_copy(bias_cmp[:, 0:NCMP_S], bank(5)[:, 0:NCMP_S]).then_inc(s_be, 1)
                dve.tensor_tensor(bias_new, mask_new, bank(6)[:, 0:32].unsqueeze(1).to_broadcast([128, 2, 32]),
                                  ALU.add).then_inc(s_be, 1)
                dve.wait_ge(s_be, 4)
                dve.wait_ge(s_gl, 16)

                def maximum(k, ap):
                    at = stats[:, 4 * (k % 4):4 * (k % 4) + 1]
                    dve.tensor_reduce(at, ap, AX, ALU.max, negate=True).then_inc(s_mx, 1)

                def reciprocal(k):
                    at = 4 * (k % 4)
                    dve.wait_ge(s_ex, k + 1)
                    link(dve.reciprocal(stats[:, at + 2:at + 3], stats[:, at + 1:at + 2]))

                def copy_probs(base, banks):
                    for n, (b, dst, width) in enumerate(banks):
                        dve.wait_ge(s_pt, base + n + 1)
                        dve.tensor_copy(dst, width(bank(b))).then_inc(s_pe_, 1)

                PT0 = 8
                four = lambda b: b.rearrange("p (a n) -> p a n", a=4)
                for r in range(2):
                    k = 4 * r
                    base = PT0 * r
                    dve.wait_ge(s_sp, SP0 * r + 1)
                    link(dve.tensor_tensor(p_cmp[:, 0:NCMP_S], bank(4)[:, 0:NCMP_S], bias_cmp[:, 0:NCMP_S], ALU.add))
                    maximum(k, p_cmp[:, 0:NCMP_S])
                    reciprocal(k)
                    dve.tensor_scalar(p_cmp[:, 0:NCMP_S], p_cmp[:, 0:NCMP_S], stats[:, 2:3], None, ALU.mult).then_inc(s_pcn, 1)
                    dve.wait_ge(s_pt, base + 1)
                    dve.tensor_copy(probT[0:NCMP_S, 0], bank(7)[0:NCMP_S, 0:128]).then_inc(s_pe_, 1)
                    dve.wait_ge(s_pe_, 9 * r + 1)
                    rows = probT[0:NCMP_S, 0].rearrange("n (s p q) -> n s q p", s=4, p=4)
                    link(dve.tensor_reduce(p_sum[0:NCMP_S].rearrange("n (s q) -> n s q", s=4), rows, AX, ALU.add))
                    for p in range(4):
                        ins = dve.tensor_copy(p_exp[0:NCMP_S].rearrange("n (s p q) -> n p s q", s=4, p=4)[:, p],
                                              p_sum[0:NCMP_S].rearrange("n (s q) -> n s q", s=4))
                        ins.then_inc(s_px, 1)
                    dve.wait_ge(s_im, r + 1)
                    link(dve.tensor_tensor(pick[:, 0], bank(7)[:, 128:161], force, ALU.add))
                    link(dve.max(top8, pick[:, 0]))
                    link(dve.match_replace(pick[:, 1], top8, pick[:, 0], -1.0))
                    link(dve.max(top8b, pick[:, 1]))
                    link(dve.match_replace(pick[:, 2], top8b, pick[:, 1], -1.0))
                    link(dve.tensor_tensor(pick[:, 3], pick[:, 0], pick[:, 2], ALU.is_equal))
                    link(dve.tensor_scalar(pick[:, 3], pick[:, 3], NEG, None, ALU.mult))
                    if r == 0:
                        dve.wait_ge(s_bp, 1)
                    else:
                        dve.wait_ge(s_ot, 2 * r)
                    blocks_of = lambda ap: ap.rearrange("p (a j k) -> p a j k", a=SUB, k=4)
                    link(dve.tensor_tensor(blocks_of(scores[:, 0:PAST]), blocks_of(bias_slc),
                                           pick[:, 3, 0:32].unsqueeze(1).unsqueeze(3).to_broadcast([128, SUB, 32, 4]),
                                           ALU.add))
                    dve.wait_ge(s_op, 3 * r + 1)
                    dve.tensor_scalar(o_rows, bank(4)[:, 128:256], gate_rows[:, r, 0:1], None,
                                      ALU.mult).then_inc(s_or, 1)
                    keys(r, S)
                    for q in range(4):
                        dve.wait_ge(s_sp, SP0 * r + 1 + 12 + q + 1)
                        sl = scores[:, 512 * q:512 * q + 512]
                        link(dve.tensor_tensor(sl, bank(q), sl, ALU.add))
                    dve.wait_ge(s_sp, SP0 * r + 18)
                    link(dve.tensor_tensor(scores[:, PAST:], bank(4)[:, 256:288], bias_new[:, r], ALU.add))
                    maximum(k + 1, scores)
                    reciprocal(k + 1)
                    copy_probs(base + 1, [(5, probT[:, 0:4], four), (6, probT[:, 4:8], four), (5, probT[:, 8:12], four),
                                          (6, probT[:, 12:16], four), (7, probT[0:32, 16], lambda b: b[0:32, 0:128])])
                    link(dve.tensor_tensor(stats[:, 7:8], gate_rows[:, r, 1:2], stats[:, 6:7], ALU.mult))
                    dve.wait_ge(s_vu, 4 * r + 4)
                    dve.wait_ge(s_or, 4 * r + 1)
                    dve.scalar_tensor_tensor(o_rows, bank(4)[:, 0:128], stats[:, 7:8], o_rows, ALU.mult,
                                             ALU.add).then_inc(s_or, 1)
                    dve.wait_ge(s_or, 4 * r + 2)
                    keys(r, W_)
                    dve.wait_ge(s_sp, SP0 * r + 18 + 5)
                    link(dve.tensor_tensor(scores[:, 0:512], bank(0), bias_win, ALU.add))
                    link(dve.tensor_tensor(scores[:, 512:544], bank(1)[:, 0:32], bias_new[:, r], ALU.add))
                    maximum(k + 2, scores[:, 0:544])
                    reciprocal(k + 2)
                    copy_probs(base + 6, [(2, probT[:, 0:4], four)])
                    dve.tensor_copy(probT[0:32, 16], bank(3)[0:32, 0:128]).then_inc(s_pe_, 1)
                    link(dve.tensor_tensor(stats[:, 11:12], gate_rows[:, r, 2:3], stats[:, 10:11], ALU.mult))
                    dve.wait_ge(s_op, 3 * r + 2)
                    dve.scalar_tensor_tensor(o_rows, bank(4)[:, 0:128], stats[:, 11:12], o_rows, ALU.mult,
                                             ALU.add).then_inc(s_or, 1)
                    keys(r, M)
                    dve.wait_ge(s_sp, SP0 * r + 27)
                    link(dve.tensor_copy(scores[:, 0:MEM], bank(1)[:, 256:512]))
                    maximum(k + 3, scores[:, 0:MEM])
                    reciprocal(k + 3)
                    dve.wait_ge(s_pt, base + 8)
                    dve.tensor_copy(probT[:, 0:2], bank(0)[:, 0:256].rearrange("p (a n) -> p a n", a=2)).then_inc(s_pe_, 1)
                    dve.wait_ge(s_op, 3 * r + 3)
                    dve.tensor_scalar(scores[:, 512:768], bank(2)[:, 0:256], stats[:, 14:15], None, ALU.mult).then_inc(s_or, 1)

            @block.tensor
            def _(pe):
                pe.wait_ge(s_sc, 16 * 12)
                pe.wait_ge(s_rr, 4)
                for q in range(4):
                    pe.matmul(bank(q), rel_rows, oh_slc[:, 512 * q:512 * q + 512], start=True, stop=True)
                pe.matmul(bank(4), rel_rows, oh_win, start=True, stop=True)
                pe.matmul(bank(5)[:, 0:NCMP_S], rel_rows, oh_cmp, start=True, stop=True)
                pe.matmul(bank(6)[:, 0:32], rel_rows, oh_new, start=True, stop=True).then_inc(s_bp, 1)
                pe.wait_ge(s_qr, 20)
                pe.wait_ge(s_be, 4)

                def keys_wait(n):
                    pe.wait_ge(s_ke_of[n % 2], n // 2 + 1)

                def transpose_keys(n):
                    r, b, s, q = GROUPS[n]
                    if b == S and q == 0:
                        pe.wait_ge(s_cs[s], 16 * (r + 1))
                    if b == W_:
                        pe.wait_ge(s_wl[s], 32 * (r + 1))
                    if n >= 2:
                        keys_wait(n - 2)
                    out = bank(5 + n % 2)
                    for a in range(4):
                        if b == S:
                            src = cache[:, s, (4 * q + a) * 256:(4 * q + a) * 256 + 128]
                        elif b == W_:
                            src = cache[:, s, a * 256:a * 256 + 128]
                        else:
                            mp, tok = a // 2, a % 2
                            src = cache[:, s, 1024 + 512 * tok + 128 * mp:1024 + 512 * tok + 128 * mp + 128]
                        mm = pe.transpose(out[:, 128 * a:128 * a + 128], src, ident)
                    mm.then_inc(s_tk, 1)

                def score(n):
                    r, b, s, q = GROUPS[n]
                    keys_wait(n)
                    seq = 4 * r + s
                    rows = slice(32 * s, 32 * s + 32)
                    if b == S:
                        pe.matmul(bank(q)[rows, :], q_rows[:, seq], keysT[:, 512 * q:512 * q + 512],
                                  start=True, stop=True, tile_position=(0, 32 * s)).then_inc(s_sp, 1)
                    elif b == W_:
                        pe.matmul(bank(0)[rows, :], q_rows[:, seq], keysT[:, 512 * s:512 * s + 512],
                                  start=True, stop=True, tile_position=(0, 32 * s)).then_inc(s_sp, 1)
                    else:
                        for mp in range(2):
                            mm = pe.matmul(bank(1)[rows, 256:512], qm_rows[:, mp, seq],
                                           keysT[:, 512 * s + 256 * mp:512 * s + 256 * mp + 256],
                                           start=(mp == 0), stop=(mp == 1), tile_position=(0, 32 * s))
                        mm.then_inc(s_sp, 1)

                def key_groups(r, b):
                    mine = [n for n, g in enumerate(GROUPS) if g[0] == r and g[1] == b]
                    transpose_keys(mine[0])
                    for n in mine[1:]:
                        transpose_keys(n)
                        score(n - 1)
                    score(mine[-1])

                for r in range(2):
                    q4 = q_rows[:, 4 * r:4 * r + 4].rearrange("p s q -> p (s q)")
                    if r:
                        pe.wait_ge(s_or, 4 * r)
                    for s in range(4):
                        mm = pe.matmul(bank(4)[32 * s:32 * s + 32, 0:NCMP_S], q_rows[:, 4 * r + s], kcT[:, 4 * r + s, 0:NCMP_S],
                                       start=True, stop=True, tile_position=(0, 32 * s))
                    mm.then_inc(s_sp, 1)
                    pe.wait_ge(s_pcn, r + 1)
                    if r:
                        pe.wait_ge(s_oe, 12)
                    pe.transpose(bank(7)[0:NCMP_S, 0:128], p_cmp[:, 0:NCMP_S], ident).then_inc(s_pt, 1)
                    pe.wait_ge(s_pe_, 9 * r + 1)
                    for s in range(4):
                        mm = pe.matmul(bank(4)[32 * s:32 * s + 32, 128:256], probT[0:NCMP_S, 0, 32 * s:32 * s + 32],
                                       v_cmp[0:NCMP_S, 4 * r + s], start=True, stop=True, tile_position=(0, 32 * s))
                    mm.then_inc(s_op, 1)
                    pe.wait_ge(s_px, 4 * r + 4)
                    pe.matmul(bank(7)[:, 128:161], p_exp[0:NCMP_S], covers[0:NCMP_S], start=True, stop=True).then_inc(s_im, 1)
                    pe.wait_ge(s_or, 4 * r + 1)
                    key_groups(r, S)
                    pe.matmul(bank(4)[:, 256:288], q4, ksT[:, NP_TOK:], start=True, stop=True).then_inc(s_sp, 1)
                    pe.wait_ge(s_ex, 4 * r + 2)
                    for q in range(4):
                        if q >= 2:
                            pe.wait_ge(s_pe_, 9 * r + q)
                        for a in range(4):
                            at = 128 * (4 * q + a)
                            mm = pe.transpose(bank(5 + q % 2)[:, 128 * a:128 * a + 128], scores[:, at:at + 128], ident)
                        mm.then_inc(s_pt, 1)
                    pe.transpose(bank(7)[0:32, 0:128], scores[:, PAST:], ident).then_inc(s_pt, 1)
                    pe.wait_ge(s_pe_, 9 * r + 6)
                    for s in range(4):
                        rows = slice(32 * s, 32 * s + 32)
                        pe.matmul(bank(4)[rows, 0:128], probT[0:32, 16, rows], v_slc[0:32, 4], start=True, stop=False,
                                  tile_position=(0, 32 * s))
                        for a in range(SUB):
                            mm = pe.matmul(bank(4)[rows, 0:128], probT[:, a, rows], cache[:, s, 256 * a + 128:256 * a + 256],
                                           start=False, stop=(a == SUB - 1), tile_position=(0, 32 * s))
                        mm.then_inc(s_vu, 1)
                    key_groups(r, W_)
                    pe.matmul(bank(1)[:, 0:32], q4, kwT[:, NP_TOK:], start=True, stop=True).then_inc(s_sp, 1)
                    pe.wait_ge(s_ex, 4 * r + 3)
                    for a in range(4):
                        pe.transpose(bank(2)[:, 128 * a:128 * a + 128], scores[:, 128 * a:128 * a + 128], ident)
                    pe.transpose(bank(3)[0:32, 0:128], scores[:, 512:544], ident).then_inc(s_pt, 1)
                    pe.wait_ge(s_pe_, 9 * r + 8)
                    pe.wait_ge(s_or, 4 * r + 2)
                    for s in range(4):
                        rows = slice(32 * s, 32 * s + 32)
                        pe.matmul(bank(4)[rows, 0:128], probT[0:32, 16, rows], v_win[0:32, 4], start=True, stop=False,
                                  tile_position=(0, 32 * s))
                        for a in range(4):
                            mm = pe.matmul(bank(4)[rows, 0:128], probT[:, a, rows], cache[:, s, 256 * a + 128:256 * a + 256],
                                           start=False, stop=(a == 3), tile_position=(0, 32 * s))
                    mm.then_inc(s_op, 1)
                    key_groups(r, M)
                    pe.wait_ge(s_ex, 4 * r + 4)
                    for a in range(2):
                        mm = pe.transpose(bank(0)[:, 128 * a:128 * a + 128], scores[:, 128 * a:128 * a + 128], ident)
                    mm.then_inc(s_pt, 1)
                    pe.wait_ge(s_pe_, 9 * r + 9)
                    for s in range(4):
                        rows = slice(32 * s, 32 * s + 32)
                        for a in range(2):
                            mm = pe.matmul(bank(2)[rows, 0:256], probT[:, a, rows],
                                           cache[:, s, 1024 + 512 * a + 256:1024 + 512 * a + 512],
                                           start=(a == 0), stop=(a == 1), tile_position=(0, 32 * s))
                    mm.then_inc(s_op, 1)
                    pe.wait_ge(s_or, 4 * r + 3)
                    pe.transpose(bank(7)[:, 0:128], o_rows, ident).then_inc(s_ot, 1)
                    pe.wait_ge(s_or, 4 * r + 4)
                    pe.wait_ge(s_oe, 12 * r + 8)
                    for mp in range(2):
                        mm = pe.transpose(bank(7)[:, 128 + 128 * mp:256 + 128 * mp], scores[:, 512 + 128 * mp:640 + 128 * mp], ident)
                    mm.then_inc(s_ot, 1)

        phase_over()
        cursor[0] = phase_base
        RING = 4
        rel97 = take(8, 128, dt=BF16)
        desc_b = take(BIASL, dt=BF16)
        asc_b = take(CMPL, dt=BF16)
        dist_desc = take(BIASL)
        dist_asc = take(CMPL)
        table = take(2, CMPL)
        table_c = take(2, CMPL)
        top = cursor[0]
        cursor[0] = phase_base
        sc_u = take(RING, 512)
        pT_u = take(RING, 512)
        assert cursor[0] <= top
        cursor[0] = top
        bias_q = take(8, NP_TOK)
        bias_b = take(8, NP_TOK)
        bias_c = take(4, 8, NCMP_P)
        stat_u = take(RING, 2)
        sum_u = take(2, 16)
        coef = take(16)
        oa = take(8, HD)
        sc_f = take(8, HD)
        sc_c = take(8, NCMP_P)
        pT_c = take(8, 128)
        max_c, sum_c = take(8), take(8)
        p_m = take(4, MEM)
        pT_m = take(4, 2, 128)
        max_m, sum_m = take(4), take(4)
        om = take(4, HD)

        assert cursor[0] <= w_gb_at
        cursor[0] = w_gb_at
        w_gb = take(6, KD, 128)
        g_w = [lasting(f"g_w{n}") for n in range(6)]

        scr_desc = scratch("scr_desc", [8, 128 * BIASL])
        scr_asc = scratch("scr_asc", [8, NCMP_P * CMPL])

        s_bi = sem("s_bi")
        s_r3 = sem("s_r3")
        s_tb = sem("s_tb")
        s_te1 = sem("s_te1")
        s_te2 = sem("s_te2")
        s_ts = [sem(f"s_ts{n}") for n in range(2)]
        s_tl = sem("s_tl")
        s_bt = sem("s_bt")
        s_bc = sem("s_bc")
        u_sp, u_mx, u_ex, u_tp, u_pt, u_op = (sem(n) for n in ("u_sp", "u_mx", "u_ex", "u_tp", "u_pt", "u_op"))
        c_sp, c_mx, c_ex, c_pn, c_tp, c_pt, c_op, c_oa = (sem("c_" + n) for n in
                                                          ("sp", "mx", "ex", "pn", "tp", "pt", "op", "oa"))
        m_sp, m_mx, m_ex, m_tp, m_pt, m_op, m_nm, m_ot, m_oe = (sem("m_" + n) for n in
                                                                ("sp", "mx", "ex", "tp", "pt", "op", "nm", "ot", "oe"))
        f_oa, f_ot, f_oe = sem("f_oa"), sem("f_ot"), sem("f_oe")
        s_d4 = sem("s_d4")

        TILES = NP_TOK // 128
        UNITS = [(t, hh, b) for t in range(TILES) for hh in range(NH) for b in range(2)]
        PER = 2 * NH
        TURN, VALUES = 2, 4
        STEPS = len(UNITS) + 4 + VALUES

        def due(step, at, late=0):
            step -= VALUES - 2
            t = step // PER - late
            return t if step % PER == at and 0 <= t < TILES else None

        with nc.Block() as block:
            @block.sync
            def _(sp):
                sp.dma_start(dist_desc[0:97], i["c_dist_desc"]).then_inc(s_bi, 16)
                sp.dma_start(dist_asc[0:97], i["c_dist_asc"]).then_inc(s_bi, 16)
                for h in range(NH):
                    sp.wait_ge(s_te1, h + 1)
                    sp.dma_start(scr_desc[h].rearrange("(p m) -> p m", p=128), table[:, h % 2, 0:BIASL]
                                 ).then_inc(s_ts[h % 2], 16)
                    sp.wait_ge(s_te2, h + 1)
                    sp.dma_start(scr_asc[h].rearrange("(p m) -> p m", p=NCMP_P), table_c[0:NCMP_P, h % 2]
                                 ).then_inc(s_ts[h % 2], 16)
                sp.wait_ge(s_ts[0], 128)
                sp.wait_ge(s_ts[1], 128)
                for u in range(6):
                    sp.dma_start(w_gb[:, u], i["w_gb"][u // 3, u % 3].rearrange("p (k n) -> p k n", k=KD)
                                 ).then_inc(g_w[u], 16)

            @block.gpsimd
            def _(pool):
                for h in range(NH):
                    pool.wait_ge(s_ts[h % 2], 32 * (h // 2 + 1))
                    pool.dma_start(bias_q[:, h], scr_desc[h][127:127 + 128 * (BIASL - 1)]
                                   .rearrange("(p m) -> p m", p=128)[:, 0:NP_TOK]).then_inc(s_tl, 16)
                    pool.dma_start(bias_b[0:NCMP_P, h], scr_asc[h][480:480 + NCMP_P * (CMPL - 16)]
                                   .rearrange("(p m) -> p m", p=NCMP_P)[:, 0:NP_TOK]).then_inc(s_tl, 16)

            @block.scalar
            def _(act):
                copy = lambda a, b, **k: act.activation(a, b, ACT.Copy, **k)
                act.wait_ge(s_bi, 32)
                copy(asc_b[0:97], dist_asc[0:97]).then_inc(s_r3, 1)
                for h in range(NH):
                    act.wait_ge(s_tb, h + 1)
                    if h >= 2:
                        act.wait_ge(s_ts[h % 2], 32 * (h // 2))
                    copy(table[:, h % 2, 0:BIASL], psum[:, 2 * (h % 2):2 * (h % 2) + 2].rearrange("p b n -> p (b n)")[:, 0:BIASL]
                         ).then_inc(s_te1, 1)
                for t in range(TILES):
                    act.wait_ge(s_bt, t + 1)
                    copy(bias_c[:, t], bank(t)[:, 0:8 * NCMP_P].rearrange("p (h n) -> p h n", h=8)).then_inc(s_bc, 1)
                for step in range(STEPS):
                    u = step
                    if u < len(UNITS):
                        t, hh, b = UNITS[u]
                        w = 128 * (t + 1)
                        act.wait_ge(u_mx, u + 1)
                        if hh == 0 and b == 0 and t >= 2:
                            act.wait_ge(f_oa, t - 1)
                        act.activation(sc_u[:, u % RING, 0:w], sc_u[:, u % RING, 0:w], ACT.Exp, bias=stat_u[:, u % RING, 0:1],
                                       accum_out=sum_u[:, t % 2, 8 * b + hh:8 * b + hh + 1]).then_inc(u_ex, 1)
                    u = step - TURN
                    if 0 <= u < len(UNITS):
                        w = 128 * (UNITS[u][0] + 1)
                        act.wait_ge(u_tp, u + 1)
                        if u >= RING:
                            act.wait_ge(u_op, u - RING + 1)
                        copy(pT_u[:, u % RING, 0:w], bank(2 + u % 2)[:, 0:w]).then_inc(u_pt, 1)
                    if (t := due(step, 4, 1)) is not None:
                        act.wait_ge(f_ot, t + 1)
                        copy(oT_nsa[:, :, 128 * t:128 * t + 128], bank(6).rearrange("p (a n) -> p a n", a=4)).then_inc(f_oe, 1)
                    if (t := due(step, 6)) is not None:
                        act.wait_ge(c_mx, t + 1)
                        act.activation(sc_c, sc_c, ACT.Exp).then_inc(c_ex, 1)
                    if (t := due(step, 9)) is not None:
                        act.wait_ge(c_tp, t + 1)
                        if t:
                            act.wait_ge(c_op, t)
                        copy(pT_c[0:NCMP_P].rearrange("p (b a) n -> p b (a n)", b=2), psum[0:NCMP_P, 6:8]).then_inc(c_pt, 1)
                    if (t := due(step, 12)) is not None:
                        act.wait_ge(m_mx, t + 1)
                        if t:
                            act.wait_ge(m_tp, t)
                            act.wait_ge(m_nm, t)
                        for m in range(4):
                            act.activation(p_m[:, m], bank(6 + m // 2)[:, 256 * (m % 2):256 * (m % 2) + 256], ACT.Exp,
                                           bias=max_m[:, m:m + 1], accum_out=sum_m[:, m:m + 1]).then_inc(m_ex, 1)
                    if (t := due(step, 14)) is not None:
                        act.wait_ge(m_tp, t + 1)
                        if t:
                            act.wait_ge(m_op, t)
                        copy(pT_m.rearrange("p (b m) a n -> p b (m a n)", b=2), psum[:, 6:8]).then_inc(m_pt, 1)
                    if (t := due(step, 2, 1)) is not None:
                        act.wait_ge(m_ot, t + 1)
                        copy(oT_mem[:, :, 128 * t:128 * t + 128], bank(7)[:, 0:256].rearrange("p (a n) -> p a n", a=2)
                             ).then_inc(m_oe, 1)

            @block.vector
            def _(dve):
                link = linked(dve, s_d4, [0])
                dve.tensor_copy(rel97[0:96], rel_parts[0:96].unsqueeze(2).to_broadcast([96, 8, 128])).then_inc(s_r3, 1)
                dve.memset(rel97[96:97], NEG).then_inc(s_r3, 1)
                dve.wait_ge(s_bi, 32)
                dve.tensor_copy(desc_b[0:97], dist_desc[0:97]).then_inc(s_r3, 1)
                for h in range(NH):
                    dve.wait_ge(s_tb, h + 1)
                    if h >= 2:
                        dve.wait_ge(s_ts[h % 2], 32 * (h // 2))
                    dve.tensor_copy(table_c[0:NCMP_P, h % 2].rearrange("p (b n) -> p b n", b=2),
                                    psum[0:NCMP_P, 4 + 2 * (h % 2):6 + 2 * (h % 2)]).then_inc(s_te2, 1)
                dve.wait_ge(s_tl, 16 * 16)
                dve.wait_ge(s_bc, TILES)
                for step in range(STEPS):
                    u = step
                    if u < len(UNITS):
                        t, hh, b = UNITS[u]
                        w = 128 * (t + 1)
                        dve.wait_ge(u_sp, u + 1)
                        if u >= RING:
                            dve.wait_ge(u_tp, u - RING + 1)
                        link(dve.tensor_tensor(sc_u[:, u % RING, 0:w], bank(u % 2)[:, 0:w], bias_q[:, hh, 512 - w:512], ALU.add))
                        dve.tensor_reduce(stat_u[:, u % RING, 0:1], sc_u[:, u % RING, 0:w], AX, ALU.max, negate=True
                                          ).then_inc(u_mx, 1)
                    if (t := due(step, 2, 1)) is not None:
                        dve.wait_ge(u_ex, PER * (t + 1))
                        dve.wait_ge(u_op, PER * (t + 1))
                        dve.wait_ge(c_oa, t + 1)
                        link(dve.reciprocal(coef, sum_u[:, t % 2]))
                        g = gates[:, t].rearrange("p (h n) -> p n h", n=3)
                        link(dve.tensor_tensor(coef.rearrange("p (n h) -> p n h", n=2),
                                               coef.rearrange("p (n h) -> p n h", n=2), g[:, 1:3], ALU.mult))
                        for b in range(2):
                            o_b = sc_f
                            link(dve.tensor_tensor(o_b, bank(4 + b).rearrange("p (h d) -> p h d", h=8),
                                                   coef[:, 8 * b:8 * b + 8].unsqueeze(2).to_broadcast([128, 8, HD]), ALU.mult))
                            ins = dve.tensor_tensor(oa, oa, o_b, ALU.add)
                            if b == 0:
                                link(ins)
                            else:
                                ins.then_inc(f_oa, 1)
                    if (t := due(step, 5)) is not None:
                        dve.wait_ge(c_sp, t + 1)
                        if t:
                            dve.wait_ge(c_tp, t)
                        link(dve.tensor_tensor(sc_c.rearrange("p (b a) n -> p b (a n)", b=2), psum[:, 6:8, 0:4 * NCMP_P],
                                               bias_c[:, t].rearrange("p (b a) n -> p b (a n)", b=2), ALU.add))
                        link(dve.tensor_reduce(max_c, sc_c, AX, ALU.max))
                        link(dve.tensor_scalar(max_c, max_c, -1e20, None, ALU.max))
                        dve.tensor_tensor(sc_c, sc_c, max_c.unsqueeze(2).to_broadcast([128, 8, NCMP_P]),
                                          ALU.subtract).then_inc(c_mx, 1)
                    if (t := due(step, 7)) is not None:
                        dve.wait_ge(c_ex, t + 1)
                        link(dve.tensor_reduce(sum_c, sc_c, AX, ALU.add))
                        link(dve.tensor_scalar(sum_c, sum_c, 1e-30, None, ALU.max))
                        link(dve.reciprocal(sum_c, sum_c))
                        link(dve.tensor_tensor(sum_c.rearrange("p (g q) -> p g q", g=2), sum_c.rearrange("p (g q) -> p g q", g=2),
                                               gates[:, t].rearrange("p (q g n) -> p n g q", q=4, g=2)[:, 0], ALU.mult))
                        dve.tensor_tensor(sc_c, sc_c, sum_c.unsqueeze(2).to_broadcast([128, 8, NCMP_P]), ALU.mult
                                          ).then_inc(c_pn, 1)
                    if (t := due(step, 11)) is not None:
                        dve.wait_ge(c_op, t + 1)
                        if t:
                            dve.wait_ge(f_ot, t)
                        dve.tensor_copy(oa, bank(6).rearrange("p (h d) -> p h d", h=8)).then_inc(c_oa, 1)
                    if (t := due(step, 12)) is not None:
                        dve.wait_ge(m_sp, t + 1)
                        dve.tensor_reduce(max_m.rearrange("p (b m) -> p b m", b=2),
                                          psum[:, 6:8].rearrange("p b (m n) -> p b m n", m=2), AX, ALU.max,
                                          negate=True).then_inc(m_mx, 1)
                    if (t := due(step, 0, 1)) is not None:
                        dve.wait_ge(m_op, t + 1)
                        dve.wait_ge(m_ex, 4 * t + 4)
                        if t:
                            dve.wait_ge(m_ot, t)
                        link(dve.reciprocal(sum_m, sum_m))
                        dve.tensor_tensor(om.rearrange("p (a b) d -> p a b d", a=2),
                                          bank(6)[:, 0:256].rearrange("p (a b d) -> p a b d", a=2, b=2),
                                          sum_m.rearrange("p (b a) -> p a b", b=2).unsqueeze(3).to_broadcast([128, 2, 2, HD]),
                                          ALU.mult).then_inc(m_nm, 1)

            @block.tensor
            def _(pe):
                pe.wait_ge(s_r3, 4)
                for h in range(NH):
                    if h >= 2:
                        pe.wait_ge(s_te1, h - 1)
                        pe.wait_ge(s_te2, h - 1)
                    b = 2 * (h % 2)
                    pe.matmul(bank(b), rel97[0:97, h], desc_b[0:97, 0:512], start=True, stop=True)
                    pe.matmul(bank(b + 1)[:, 0:BIASL - 512], rel97[0:97, h], desc_b[0:97, 512:], start=True, stop=True)
                    for half in range(2):
                        mm = pe.matmul(bank(4 + b + half)[0:NCMP_P], rel97[0:97, h, 0:NCMP_P],
                                       asc_b[0:97, 512 * half:512 * half + 512], start=True, stop=True)
                    mm.then_inc(s_tb, 1)
                pe.wait_ge(s_te1, NH)
                pe.wait_ge(s_te2, NH)
                pe.wait_ge(s_tl, 256)
                for t in range(TILES):
                    for g in range(2):
                        for p in range(4):
                            mm = pe.transpose(bank(t)[:, (4 * g + p) * NCMP_P:(4 * g + p + 1) * NCMP_P],
                                              bias_b[0:NCMP_P, 2 * p + g, 128 * t:128 * t + 128], ident[0:NCMP_P, 0:NCMP_P])
                    mm.then_inc(s_bt, 1)
                pe.wait_ge(s_bc, TILES)
                for step in range(STEPS):
                    u = step
                    if u < len(UNITS):
                        t, hh, b = UNITS[u]
                        p, g = hh // 2, hh % 2
                        q = slice(64 * g, 64 * g + 64)
                        if u >= 2:
                            pe.wait_ge(u_mx, u - 1)
                        keys = (ksT, kwT)[b]
                        pe.matmul(bank(u % 2)[:, 0:128 * (t + 1)], qT[q, p, 128 * t:128 * t + 128], keys[q, 0:128 * (t + 1)],
                                  start=True, stop=True).then_inc(u_sp, 1)
                    u = step - TURN
                    if 0 <= u < len(UNITS):
                        t = UNITS[u][0]
                        pe.wait_ge(u_ex, u + 1)
                        if u >= 2:
                            pe.wait_ge(u_pt, u - 1)
                        for a in range(t + 1):
                            mm = pe.transpose(bank(2 + u % 2)[:, 128 * a:128 * a + 128], sc_u[:, u % RING, 128 * a:128 * a + 128],
                                              ident)
                        mm.then_inc(u_tp, 1)
                    u = step - VALUES
                    if 0 <= u < len(UNITS):
                        t, hh, b = UNITS[u]
                        g = hh % 2
                        pe.wait_ge(u_pt, u + 1)
                        if hh == 0 and b == 0 and t:
                            pe.wait_ge(f_oa, t)
                        values = (v_slc, v_win)[b]
                        for a in range(t + 1):
                            mm = pe.matmul(bank(4 + b)[:, 64 * hh:64 * hh + 64], pT_u[:, u % RING, 128 * a:128 * a + 128],
                                           values[:, a, 64 * g:64 * g + 64], start=(a == 0), stop=(a == t))
                        mm.then_inc(u_op, 1)
                    if (t := due(step, 1, 1)) is not None:
                        pe.wait_ge(m_nm, t + 1)
                        for mp in range(2):
                            mm = pe.transpose(bank(7)[:, 128 * mp:128 * mp + 128],
                                              om.rearrange("p (a b) d -> p a (b d)", a=2)[:, mp], ident)
                        mm.then_inc(m_ot, 1)
                    if (t := due(step, 3, 1)) is not None:
                        pe.wait_ge(f_oa, t + 1)
                        for p in range(4):
                            mm = pe.transpose(bank(6)[:, 128 * p:128 * p + 128],
                                              oa.rearrange("p (a b) d -> p a (b d)", a=4)[:, p], ident)
                        mm.then_inc(f_ot, 1)
                    if (t := due(step, 5)) is not None:
                        if t:
                            pe.wait_ge(f_oe, t)
                            pe.wait_ge(m_oe, t)
                        for g in range(2):
                            q = slice(64 * g, 64 * g + 64)
                            for p in range(4):
                                mm = pe.matmul(bank(6 + g)[:, p * NCMP_P:(p + 1) * NCMP_P], qT[q, p, 128 * t:128 * t + 128],
                                               kcT[q, NS, 0:NCMP_P], start=True, stop=True)
                        mm.then_inc(c_sp, 1)
                    if (t := due(step, 8)) is not None:
                        pe.wait_ge(c_pn, t + 1)
                        for k in range(8):
                            mm = pe.transpose(bank(6 + k // 4)[0:NCMP_P, 128 * (k % 4):128 * (k % 4) + 128], sc_c[:, k], ident)
                        mm.then_inc(c_tp, 1)
                    if (t := due(step, 10)) is not None:
                        pe.wait_ge(c_pt, t + 1)
                        for g in range(2):
                            for p in range(4):
                                hh = 2 * p + g
                                mm = pe.matmul(bank(6)[:, 64 * hh:64 * hh + 64], pT_c[0:NCMP_P, 4 * g + p],
                                               v_cmp[0:NCMP_P, NS, 64 * g:64 * g + 64], start=True, stop=True)
                        mm.then_inc(c_op, 1)
                    if (t := due(step, 12)) is not None:
                        pe.wait_ge(c_oa, t + 1)
                        for m2 in range(2):
                            q = slice(64 * m2, 64 * m2 + 64)
                            for mp in range(2):
                                mm = pe.matmul(bank(6 + m2)[:, 256 * mp:256 * mp + 256], qmT[q, mp, 128 * t:128 * t + 128],
                                               kmT[q, mp], start=True, stop=True)
                        mm.then_inc(m_sp, 1)
                    if (t := due(step, 13)) is not None:
                        pe.wait_ge(m_ex, 4 * t + 4)
                        for m in range(4):
                            for a in range(2):
                                mm = pe.transpose(bank(6 + m // 2)[:, 128 * (2 * (m % 2) + a):128 * (2 * (m % 2) + a) + 128],
                                                  p_m[:, m, 128 * a:128 * a + 128], ident)
                        mm.then_inc(m_tp, 1)
                    if (t := due(step, 15)) is not None:
                        pe.wait_ge(m_pt, t + 1)
                        for m in range(4):
                            m2, mp = m // 2, m % 2
                            h = 2 * mp + m2
                            for a in range(2):
                                mm = pe.matmul(bank(6)[:, 64 * h:64 * h + 64], pT_m[:, m, a],
                                               zm[:, a, 256 + 64 * h:320 + 64 * h], start=(a == 0), stop=(a == 1))
                        mm.then_inc(m_op, 1)

        phase_over()
        cursor[0] = 50200
        g4 = take(NT, TOPK)
        slot_token = take(NBLK + 1, dt=U32)
        slot_row = take(NBLK + 1, dt=U32)
        slot_gate = take(NBLK + 1)
        e_row = take(NBLK, dt=I32)
        n_used = take(2, dt=I32)
        e_match = take(NBLK + 1, dt=BF16)
        b_parts = take(2048, dt=BF16)
        assert cursor[0] <= 53000
        cursor[0] = tail_base
        w_up = take(KD, D)
        w_out = take(KD, D)
        mixT = take(KD, NTOK)
        sig = take(2, NTOK)
        prod = take(2, NTOK)
        top = cursor[0]
        cursor[0] = tail_base
        x2n = take(2, D)
        sq2 = take(D)
        hT2 = take(2, KD, 128)
        bg = take(2048)
        assert cursor[0] <= tail_base + KD * D
        cursor[0] = top
        router_w = take(KD, NE)
        router_b = take(NE)
        before = take(128)
        before_b, ones_b = take(128, dt=BF16), take(128, dt=BF16)
        iota128 = take(128)
        token1 = take(NT)
        spare_row = take(1)
        logit = take(NT, NE)
        best = take(NT, 8)
        best_i = take(NT, 8, dt=U32)
        best_f = take(NT, TOPK)
        eg = take(NT, TOPK)
        eg_sum = take(NT)
        mask = take(NT, NE, dt=BF16)
        cnt_i = take(NE, dt=I32)
        nblk, ends, base_ = take(NE), take(NE), take(NE)
        comb = take(NT, NE)
        pos_f = take(NT * TOPK)
        slot_i, blk_i = take(NT * TOPK, dt=I32), take(NT * TOPK, dt=I32)
        slot_f, blk_f = take(NT, TOPK), take(NT, TOPK)
        hot_slot = take(2, TOPK, 128)
        hot_blk = take(2, TOPK, 2, NBLK + 1)
        is_pad, row_f = take(NBLK + 1), take(NBLK + 1)
        eb = take(2)
        ebw = take(128)
        bf_r = take(2048)
        routing_base = cursor[0]
        hot = take(NT, TOPK, NE)
        hot_any = take(NT, TOPK, NE)
        gmat = take(NT, NE)
        gmT = take(NTOK)
        b_down = take(D)
        assert cursor[0] <= w_gb_at, cursor[0]
        scr_h = scratch("scr_h", [NTOK, D])
        y_sum = scratch("y_sum", [NTOK + 128, D])

        g_wu, g_wo, g_rc = sem("g_wu"), sem("g_wo"), sem("g_rc")
        g_pp, g_sg, g_mx = sem("g_pp"), sem("g_sg"), sem("g_mx")
        x_p, x_a, x_rt, x_n, x_tp, x_te, x_lg = (sem("x_" + n) for n in
                                                       ("p", "a", "rt", "n", "tp", "te", "lg"))
        r_mx, r_ex, r_mk, r_cnt, r_rank, r_hs, r_hu, r_eb, r_ebp, r_bg, r_bp = (
            sem("r_" + n) for n in ("mx", "ex", "mk", "cnt", "rank", "hs", "hu", "eb", "ebp", "bg", "bp"))
        s_d5 = sem("s_d5")
        g_pr = sem("g_pr")
        x_st = [sem(f"x_st{n}") for n in range(2)]
        x_sq = sem("x_sq")
        x_le = sem("x_le")
        UPK = [(0, 2), (2, 6), (6, 8)]
        oT_of = lambda k: oT_pool[:, k] if k < 2 else oT_nsa[:, k - 2] if k < 6 else oT_mem[:, k - 6]
        two = lambda ap: ap.rearrange("p (h n) -> p h n", h=2)

        with nc.Block() as block:
            @block.sync
            def _(sp):
                sp.dma_start(w_up, i["w_up"].rearrange("(k p) n -> p k n", p=128)).then_inc(g_wu, 16)
                for u in range(6, 24):
                    sp.wait_ge(g_pp, u - 5)
                    sp.dma_start(w_gb[:, u % 6], i["w_gb"][u // 3, u % 3].rearrange("p (k n) -> p k n", k=KD)
                                 ).then_inc(g_w[u % 6], 16)
                    if u == 6:
                        sp.dma_start(w_out, i["w_out"].rearrange("(k p) n -> p k n", p=128)).then_inc(g_wo, 16)
                        for dst, src in ((router_w, i["router_w"].rearrange("(k p) n -> p k n", p=128)),
                                         (router_b, i["router_b"].partition_broadcast(128).rearrange("p a n -> p (a n)")),
                                         (before, i["c_before"]), (iota128, i["c_iota128"]), (token1, i["c_token1"]),
                                         (spare_row, i["c_spare_row"]), (b_down[0:32], i["b_down"])):
                            sp.dma_start(dst, src).then_inc(g_rc, 16)
                sp.wait_ge(g_pp, 24)
                for part in range(3):
                    sp.dma_start(bg[32 * part:32 * part + 32], i["b_gu"]).then_inc(r_bg, 16)
                for n in range(NT):
                    sp.wait_ge(x_n, n + 1)
                    sp.dma_start(scr_h[128 * n:128 * n + ROWS[n]], x2n[0:ROWS[n], n % 2]).then_inc(x_st[n % 2], 16)
                sp.wait_ge(x_st[0], 48)
                sp.wait_ge(x_st[1], 32)

            @block.gpsimd
            def _(pool):
                pool.wait_ge(r_bg, 48)
                bf16_parts(linked(pool, r_bp, [0]), pool, b_parts, bg, bf_r)

            @block.scalar
            def _(act):
                for u in range(24):
                    s = u % 2
                    act.wait_ge(g_pp, u + 1)
                    if u >= 2:
                        act.wait_ge(g_pr, u - 1)
                    act.activation(two(sig[:, s]), psum[:, 4 * s:4 * s + 2, 0:HALF], ACT.Sigmoid).then_inc(g_sg, 1)
                for n in range(NT):
                    r = ROWS[n]
                    act.wait_ge(x_a, 2 * n + 2)
                    if n:
                        act.wait_ge(x_rt, n)
                    act.activation(sq2[0:r], x[0:r, n], ACT.Square, accum_out=sumsq[0:r, n:n + 1]).then_inc(x_sq, 1)
                    act.wait_ge(x_sq, n + 1)
                    act.activation(root[0:r, n:n + 1], sumsq[0:r, n:n + 1], ACT.Sqrt, bias=eps[0:r], scale=1.0 / D
                                   ).then_inc(x_rt, 1)
                act.wait_ge(r_mx, 1)
                act.activation(eg, eg, ACT.Exp).then_inc(r_ex, 1)

            @block.vector
            def _(dve):
                link = linked(dve, s_d5, [0])
                for u in range(24):
                    c, b, s = u // 3, u % 3, u % 2
                    dve.wait_ge(g_sg, u + 1)
                    dst = mixT[:, c] if b == 0 else prod[:, s]
                    if b and u >= 2:
                        dve.wait_ge(g_mx, u - 1)
                    dve.tensor_tensor(two(dst), psum[:, 4 * s + 2:4 * s + 4, 0:HALF], two(sig[:, s]), ALU.mult).then_inc(g_pr, 1)
                    dve.wait_ge(g_pr, u + 1)
                    if b:
                        dve.wait_ge(g_mx, u)
                        dve.tensor_tensor(mixT[:, c], mixT[:, c], prod[:, s], ALU.add).then_inc(g_mx, 1)
                    else:
                        dve.sem_inc(g_mx, 1)

                def residual(n):
                    r = ROWS[n]
                    for h in range(2):
                        dve.wait_ge(x_p, 2 * n + h + 1)
                        sl = x[0:r, n, 512 * h:512 * h + 512]
                        dve.tensor_tensor(sl, bank(2 * (n % 2) + h)[0:r], sl, ALU.add).then_inc(x_a, 1)

                def norm2(n):
                    r = ROWS[n]
                    dve.wait_ge(x_rt, n + 1)
                    link(dve.reciprocal(rinv[0:r, n:n + 1], root[0:r, n:n + 1]))
                    if n >= 2:
                        dve.wait_ge(x_tp, 2 * n - 2)
                        dve.wait_ge(x_st[n % 2], 16 * (n // 2))
                    dve.tensor_scalar(x2n[0:r, n % 2], x[0:r, n], rinv[0:r, n:n + 1], None, ALU.mult).then_inc(x_n, 1)

                def to_hT2(n):
                    r = ROWS[n]
                    if n >= 2:
                        dve.wait_ge(x_lg, n - 1)
                    for h in range(2):
                        dve.wait_ge(x_tp, 2 * n + h + 1)
                        dve.tensor_tensor(hT2[:, n % 2, 4 * h:4 * h + 4, 0:r],
                                          bank(4 + h)[:, 0:4 * r].rearrange("p (a b) -> p a b", a=4),
                                          g2c[:, 4 * h:4 * h + 4].unsqueeze(2).to_broadcast([128, 4, r]), ALU.mult
                                          ).then_inc(x_te, 1)

                dve.wait_ge(g_rc, 112)
                link(dve.memset(logit[:, NT - 1], 0.0))
                dve.memset(ones_b, 1.0)
                dve.tensor_copy(before_b, before)
                residual(0)
                residual(1)
                for n in range(NT):
                    norm2(n)
                    if n + 2 < NT:
                        residual(n + 2)
                    to_hT2(n)
                    dve.wait_ge(x_lg, n + 1)
                    dve.tensor_tensor(logit[0:ROWS[n], n], bank(6)[0:ROWS[n], 0:NE], router_b[0:ROWS[n]], ALU.add
                                      ).then_inc(x_le, 1)
                dve.wait_ge(x_n, NT)
                dve.wait_ge(x_le, NT)
                for n in range(NT):
                    ins = dve.max(best[:, n], logit[:, n])
                link(ins)
                for n in range(NT):
                    ins = dve.max_index(best_i[:, n], best[:, n], logit[:, n])
                dve.tensor_tensor(eg, best[:, :, 0:TOPK], best[:, :, 0:1].to_broadcast([128, NT, TOPK]), ALU.subtract
                                  ).then_inc(r_mx, 1)
                dve.wait_ge(r_mx, 1)
                link(dve.tensor_copy(best_f, best_i[:, :, 0:TOPK]))
                flat = lambda ap: ap.rearrange("p n k -> p (n k)")
                flat3 = lambda ap: ap.rearrange("p n k e -> p (n k) e")
                link(dve.tensor_tensor(flat3(hot), iota32.unsqueeze(1).to_broadcast([128, NT * TOPK, NE]),
                                       flat(best_f).unsqueeze(2).to_broadcast([128, NT * TOPK, NE]), ALU.is_equal))
                dve.tensor_reduce(mask, hot.rearrange("p n k e -> p n e k"), AX, ALU.max).then_inc(r_mk, 1)
                dve.wait_ge(r_ex, 1)
                link(dve.tensor_reduce(eg_sum, eg, AX, ALU.add))
                link(dve.reciprocal(eg_sum, eg_sum))
                link(dve.tensor_tensor(g4, eg, eg_sum.unsqueeze(2).to_broadcast([128, NT, TOPK]), ALU.mult))
                dve.wait_ge(r_cnt, 1)
                link(dve.tensor_scalar(nblk, bank(4)[:, 0:NE], 127.0, None, ALU.add))
                link(dve.tensor_copy(cnt_i, nblk))
                link(dve.tensor_scalar(cnt_i, cnt_i, 7, None, ALU.arith_shift_right))
                link(dve.tensor_copy(nblk, cnt_i))
                link(dve.tensor_tensor_scan(ends, ones[:, 0:NE], nblk, 0.0, ALU.mult, ALU.add))
                link(dve.tensor_tensor(base_, ends, nblk, ALU.subtract))
                link(dve.tensor_scalar(base_, base_, 128.0, None, ALU.mult))
                link(dve.tensor_scalar(ebw[0:NBLK + 1, 0:NE], ends[0:NBLK + 1], cols[0:NBLK + 1, 0:1], None, ALU.is_le))
                link(dve.tensor_reduce(eb[0:NBLK + 1, 0:1], ebw[0:NBLK + 1, 0:NE], AX, ALU.add))
                link(dve.tensor_scalar(eb[0:NBLK + 1, 0:1], eb[0:NBLK + 1, 0:1], float(NE - 1), None, ALU.min))
                dve.tensor_copy(ebw[0:NBLK + 1], eb[0:NBLK + 1, 0:1].to_broadcast([NBLK + 1, 128])).then_inc(r_eb, 1)
                dve.tensor_copy(n_used[:, 0:1], ends[:, NE - 1:NE])
                dve.wait_ge(r_rank, 1)
                link(dve.tensor_tensor(comb, bank(5)[:, 0:NT * NE].rearrange("p (n e) -> p n e", n=NT),
                                       base_.unsqueeze(1).to_broadcast([128, NT, NE]), ALU.add))
                for n in range(NT):
                    ins = dve.tensor_tensor(hot_any[:, n], hot[:, n], comb[:, n].unsqueeze(1).to_broadcast([128, TOPK, NE]),
                                            ALU.mult)
                link(ins)
                link(dve.tensor_reduce(pos_f, flat3(hot_any), AX, ALU.add))
                link(dve.tensor_copy(slot_i, pos_f))
                link(dve.tensor_scalar(blk_i, slot_i, 7, None, ALU.arith_shift_right))
                link(dve.tensor_scalar(slot_i, slot_i, 127, None, ALU.bitwise_and))
                dve.tensor_copy(flat(blk_f), blk_i)
                link(dve.tensor_copy(flat(slot_f), slot_i))
                for n in range(NT):
                    r, s = ROWS[n], n % 2
                    if n >= 2:
                        dve.wait_ge(r_hu, n - 1)
                    wide = lambda ap, w: ap.unsqueeze(2).to_broadcast([r, TOPK, w])
                    link(dve.tensor_tensor(hot_blk[0:r, s, :, 1], iota128[0:r, 0:NBLK + 1].unsqueeze(1).to_broadcast([r, TOPK, NBLK + 1]),
                                           wide(blk_f[0:r, n], NBLK + 1), ALU.is_equal))
                    dve.tensor_tensor(hot_slot[0:r, s], iota128[0:r].unsqueeze(1).to_broadcast([r, TOPK, 128]),
                                      wide(slot_f[0:r, n], 128), ALU.is_equal)
                    link(dve.tensor_scalar(hot_blk[0:r, s, :, 0], hot_blk[0:r, s, :, 1], token1[0:r, n:n + 1], None, ALU.mult))
                    dve.tensor_tensor(hot_blk[0:r, s, :, 1], hot_blk[0:r, s, :, 1], wide(g4[0:r, n], NBLK + 1), ALU.mult
                                      ).then_inc(r_hs, 1)
                dve.wait_ge(r_ebp, 1)
                link(dve.tensor_copy(e_row, bank(6)[:, 64:64 + NBLK]))
                link(dve.tensor_scalar(e_match, bank(6)[:, 64:65 + NBLK], cols[:, 2:3], None, ALU.is_equal))
                dve.wait_ge(r_hu, NT)
                slots = bank(7)[:, 128:129 + NBLK]
                link(dve.tensor_scalar(is_pad, slots, 0.0, spare_row, ALU.is_equal, ALU.mult))
                dve.tensor_copy(slot_gate, bank(7)[:, 129 + NBLK:130 + 2 * NBLK])
                dve.tensor_scalar(slot_token, slots, -1.0, 0.0, ALU.add, ALU.max)
                link(dve.scalar_tensor_tensor(slot_row, slots, -1.0, is_pad, ALU.add, ALU.add))

            @block.tensor
            def _(pe):
                for u in range(24):
                    c, b, s = u // 3, u % 3, u % 2
                    pe.wait_ge(g_w[u % 6], 16 * (u // 6 + 1))
                    if u >= 2:
                        pe.wait_ge(g_pr, u - 1)
                    halves = [slice(h * HALF, (h + 1) * HALF) for h in range(2)]
                    for h, t in enumerate(halves):
                        for k in range(KD):
                            pe.matmul(bank(4 * s + h)[:, 0:HALF], w_gb[:, u % 6, k], hT[:, k, t], start=(k == 0),
                                      stop=(k == KD - 1))
                    if u == 0:
                        pe.wait_ge(g_wu, 16)
                    k0, k1 = UPK[b]
                    for h, t in enumerate(halves):
                        for k in range(k0, k1):
                            mm = pe.matmul(bank(4 * s + 2 + h)[:, 0:HALF], w_up[:, k, 128 * c:128 * c + 128], oT_of(k)[:, t],
                                           start=(k == k0), stop=(k == k1 - 1))
                    mm.then_inc(g_pp, 1)
                pe.wait_ge(g_mx, 24)
                pe.wait_ge(g_wo, 16)
                pe.wait_ge(g_rc, 112)

                def mix_out(n):
                    r = ROWS[n]
                    for h in range(2):
                        if n >= 2:
                            pe.wait_ge(x_a, 2 * (n - 2) + h + 1)
                        for k in range(KD):
                            mm = pe.matmul(bank(2 * (n % 2) + h)[0:r], mixT[:, k, 128 * n:128 * n + r],
                                           w_out[:, k, 512 * h:512 * h + 512], start=(k == 0), stop=(k == KD - 1))
                        mm.then_inc(x_p, 1)

                def router(n):
                    r, s = ROWS[n], n % 2
                    pe.wait_ge(x_n, n + 1)
                    for h in range(2):
                        if n:
                            pe.wait_ge(x_te, 2 * n - 1 + h)
                        for k in range(4):
                            mm = pe.transpose(bank(4 + h)[:, k * r:(k + 1) * r], x2n[0:r, s, (4 * h + k) * 128:(4 * h + k + 1) * 128],
                                              ident[0:r, 0:r])
                        mm.then_inc(x_tp, 1)

                def logits(n):
                    r, s = ROWS[n], n % 2
                    pe.wait_ge(x_te, 2 * n + 2)
                    if n:
                        pe.wait_ge(x_le, n)
                    for k in range(KD):
                        mm = pe.matmul(bank(6)[0:r, 0:NE], hT2[:, s, k, 0:r], router_w[:, k], start=(k == 0),
                                       stop=(k == KD - 1))
                    mm.then_inc(x_lg, 1)

                mix_out(0)
                mix_out(1)
                for n in range(NT):
                    if n + 2 < NT:
                        mix_out(n + 2)
                    router(n)
                    logits(n)
                pe.wait_ge(r_mk, 1)
                pe.wait_ge(x_a, 2 * NT)
                for n in range(NT):
                    mm = pe.matmul(bank(4)[:, 0:NE], ones_b[0:ROWS[n]], mask[0:ROWS[n], n], start=(n == 0), stop=(n == NT - 1))
                mm.then_inc(r_cnt, 1)
                for n in range(NT):
                    for m in range(n + 1):
                        w = before_b[0:ROWS[m]] if m == n else ones_b
                        mm = pe.matmul(bank(5)[:, 32 * n:32 * n + 32], w, mask[0:ROWS[m], m], start=(m == 0), stop=(m == n))
                mm.then_inc(r_rank, 1)
                pe.wait_ge(r_eb, 1)
                pe.matmul(bank(6)[:, 64:65 + NBLK], ebw[0:NBLK + 1], ident[0:NBLK + 1, 0:NBLK + 1], start=True, stop=True
                          ).then_inc(r_ebp, 1)
                for n in range(NT):
                    r = ROWS[n]
                    pe.wait_ge(r_hs, n + 1)
                    for k in range(TOPK):
                        mm = pe.matmul(bank(7)[:, 128:130 + 2 * NBLK], hot_slot[0:r, n % 2, k],
                                       hot_blk[0:r, n % 2, k].rearrange("p v b -> p (v b)"),
                                       start=(n == k == 0), stop=(n == NT - 1 and k == TOPK - 1))
                    mm.then_inc(r_hu, 1)

        phase_over()
        cursor[0] = moe_base
        w_in_e = take(2, KD, 2, 512)
        w_down_e = take(KD, D)
        cur_token, cur_row = take(2, dt=U32), take(2, dt=U32)
        xg = take(D)
        xgT = take(KD, 128)
        bias_of = take(128, dt=BF16)
        gate_c = take(2, 512)
        up_c = take(2, 512)
        act_h = take(2, 512)
        actT = take(KD, 128)
        y_rows = take(D)
        cur_gate = take(2)
        assert cursor[0] <= routing_base

        e_in = [[sem(f"e_in{h}{k}") for k in range(KD)] for h in range(2)]
        e_dn = [sem(f"e_dn{k}") for k in range(KD // 2)]
        e_ix, e_g, e_gt, e_xT, e_bs, e_gu, e_c, e_sg, e_a, e_at, e_ae, e_y, e_yc, e_out = (
            sem("e_" + n) for n in ("ix", "g", "gt", "xT", "bs", "gu", "c", "sg", "a", "at", "ae", "y", "yc", "out"))
        e_use = sem("e_use")
        e_d = sem("e_d")
        e_ir, e_st, e_all = sem("e_ir"), sem("e_st"), sem("e_all")
        e_sent = sem("e_sent")
        p_x, p_out = sem("p_x"), sem("p_out")
        p_gm, p_gt, p_ge, p_bd, p_be = (sem("p_" + n) for n in ("gm", "gt", "ge", "bd", "be"))

        def used(eng):
            return eng.value_load(n_used[0:1, 0:1], min_val=1, max_val=NBLK)

        w_gu_v = i["w_gu"].rearrange("e (k p) (g h n) -> e k p g h n", p=128, g=2, h=2)
        w_dn_v = i["w_down"].rearrange("e (k p) n -> e p k n", p=128)
        USES = 2 * (KD - 1) + KD // 2 - 1

        with nc.Block() as block:
            @block.sync
            def _(sp):
                blocks = used(sp)
                with sp.Fori(0, NBLK) as b:
                    e = sp.value_load(e_row[0:1, bass.ds(b, 1)], min_val=0, max_val=NE - 1)
                    with sp.If(b < blocks):
                        for h in range(2):
                            for k in range(KD):
                                sp.wait_ge(e_use, USES * b + h * (KD - 1) + k + 1)
                                sp.dma_start(w_in_e[:, h, k], w_gu_v[bass.ds(e, 1), k, :, :, h].rearrange("e p g n -> (e p) g n")
                                             ).then_inc(e_in[h][k], 16)
                        for k in range(KD // 2):
                            if k < KD // 2 - 1:
                                sp.wait_ge(e_use, USES * b + 2 * (KD - 1) + k + 1)
                            else:
                                sp.wait_ge(e_y, b + 1)
                            sp.dma_start(w_down_e[:, 2 * k:2 * k + 2],
                                         w_dn_v[bass.ds(e, 1), :, 2 * k:2 * k + 2].rearrange("e p k n -> (e p) k n")
                                         ).then_inc(e_dn[k], 16)
                        sp.nop()
                    with sp.Else():
                        sp.nop()
                sp.wait_ge(e_all, 1)
                for n in range(4):
                    sp.dma_start(o["y_prompt"][0, 128 * n:128 * n + 128], y_sum[128 * n:128 * n + 128]).then_inc(p_out, 16)
                sp.dma_start(o["y_sample"].rearrange("s t d -> (s t) d"), y_sum[NP_TOK:NTOK]).then_inc(p_out, 16)
                sp.wait_ge(p_out, 16 * 5)

            @block.gpsimd
            def _(pool):
                def gather(b):
                    pool.tensor_copy(cur_token[:, 0:1], slot_token[:, bass.ds(b, 1)]).then_inc(e_ix, 1)
                    pool.wait_ge(e_ix, b + 1)
                    pool.sem_inc(e_sent, 1)
                    pool.indirect_dma_start(xg, None, scr_h, bass.IndirectOffsetOnAxis(cur_token[:, 0:1], 0)
                                            ).then_inc(e_g, 16)

                blocks = used(pool)
                pool.sem_inc(e_st, 1)
                gather(0)
                pool.wait_ge(p_x, 16 * (NT + 1))
                with pool.Fori(0, NBLK) as b:
                    with pool.If(b < blocks):
                        pool.wait_ge(e_gt, 2 * b + 2)
                        gather(b + 1)
                        pool.tensor_copy(cur_gate[:, 0:1], slot_gate[:, bass.ds(b, 1)]).then_inc(e_ir, 1)
                        pool.tensor_copy(cur_row[:, 0:1], slot_row[:, bass.ds(b, 1)]).then_inc(e_ir, 1)
                        pool.wait_ge(e_ir, 2 * b + 2)
                        pool.wait_ge(e_yc, b + 2)
                        pool.sem_inc(e_sent, 1)
                        pool.indirect_dma_start(y_sum, bass.IndirectOffsetOnAxis(cur_row[:, 0:1], 0), y_rows, None,
                                                compute_op=ALU.add).then_inc(e_out, 16)
                        pool.wait_ge(e_out, 16 * b + 16)
                        pool.sem_inc(e_st, 1)
                    with pool.Else():
                        pool.nop()
                pool.wait_ge(e_g, blocks * 16 + 16)
                pool.nop().then_inc(e_all, 1)

            @block.scalar
            def _(act):
                act.sem_inc(e_yc, 1)
                for n, (cols_n, b) in enumerate(((512, 7), (NTOK - 512, 6))):
                    act.wait_ge(p_gt, n + 1)
                    act.activation(gmT[0:32, 512 * n:512 * n + cols_n], bank(b)[0:32, 0:cols_n], ACT.Copy).then_inc(p_ge, 1)
                for n in range(NT):
                    act.wait_ge(p_be, 2 * n + 2)
                    act.dma_start(y_sum[128 * n:128 * n + ROWS[n]], x[0:ROWS[n], n]).then_inc(p_x, 16)
                act.dma_start(y_sum[NTOK:], x[:, 0]).then_inc(p_x, 16)
                blocks = used(act)
                with act.Fori(0, NBLK) as b:
                    with act.If(b < blocks):
                        for h in range(2):
                            act.wait_ge(e_c, 4 * b + 2 * h + 1)
                            act.activation(act_h[:, h], gate_c[:, h], ACT.Sigmoid, scale=ALPHA).then_inc(e_sg, 1)
                        for h in range(2):
                            act.wait_ge(e_at, 2 * b + h + 1)
                            act.activation(actT[:, 4 * h:4 * h + 4].rearrange("p k n -> p (k n)"), bank(6 + h), ACT.Copy
                                           ).then_inc(e_ae, 1)
                        act.wait_ge(e_y, b + 2)
                        act.wait_ge(e_st, b + 1)
                        act.wait_ge(e_ir, 2 * b + 2)
                        act.activation(y_rows.rearrange("p (h n) -> p h n", h=2), bank(4, 2), ACT.Copy,
                                       scale=cur_gate[:, 0:1]).then_inc(e_yc, 1)
                        act.nop()
                    with act.Else():
                        act.nop()

            @block.vector
            def _(dve):
                def to_xgT(b):
                    for h in range(2):
                        dve.wait_ge(e_gt, 2 * b + h + 1)
                        dve.tensor_tensor(xgT[:, 4 * h:4 * h + 4], bank(h).rearrange("p (a n) -> p a n", a=4),
                                          g2c[:, 4 * h:4 * h + 4].unsqueeze(2).to_broadcast([128, 4, 128]),
                                          ALU.mult).then_inc(e_xT, 1)
                    dve.tensor_copy(bias_of[0:96], e_match[0:96, bass.ds(b, 1)].to_broadcast([96, 128])).then_inc(e_bs, 1)

                dve.tensor_tensor(hot_any.rearrange("p n k e -> p (n k) e"), hot.rearrange("p n k e -> p (n k) e"),
                                  g4.rearrange("p n k -> p (n k)").unsqueeze(2).to_broadcast([128, NT * TOPK, NE]),
                                  ALU.mult).then_inc(p_gm, 1)
                dve.wait_ge(p_gm, 1)
                dve.tensor_reduce(gmat, hot_any.rearrange("p n k e -> p n e k"), AX, ALU.add).then_inc(p_gm, 1)
                to_xgT(0)
                for n in range(NT):
                    for h in range(2):
                        r = ROWS[n]
                        dve.wait_ge(p_bd, 2 * n + h + 1)
                        sl = x[0:r, n, 512 * h:512 * h + 512]
                        dve.tensor_tensor(sl, bank(2 + (2 * n + h) % 4)[0:r], sl, ALU.add).then_inc(p_be, 1)
                blocks = used(dve)
                with dve.Fori(0, NBLK) as b:
                    with dve.If(b < blocks):
                        for h in range(2):
                            dve.wait_ge(e_gu, 2 * b + h + 1)
                            dve.tensor_scalar(gate_c[:, h], bank(2 * h), LIMIT, None, ALU.min).then_inc(e_c, 1)
                            dve.tensor_scalar(up_c[:, h], bank(2 * h + 1), LIMIT, -LIMIT, ALU.min, ALU.max).then_inc(e_c, 1)
                            dve.wait_ge(e_c, 4 * b + 2 * h + 2)
                            dve.scalar_tensor_tensor(up_c[:, h], up_c[:, h], 1.0, gate_c[:, h], ALU.add, ALU.mult
                                                     ).then_inc(e_d, 1)
                            dve.wait_ge(e_d, 2 * b + h + 1)
                            dve.wait_ge(e_sg, 2 * b + h + 1)
                            dve.tensor_tensor(act_h[:, h], act_h[:, h], up_c[:, h], ALU.mult).then_inc(e_a, 1)
                        to_xgT(b + 1)
                        dve.nop()
                    with dve.Else():
                        dve.nop()

            @block.tensor
            def _(pe):
                def turn_tokens(b):
                    pe.wait_ge(e_g, 16 * b + 16)
                    for h in range(2):
                        for k in range(4):
                            mm = pe.transpose(bank(h)[:, 128 * k:128 * k + 128],
                                              xg[:, 128 * (4 * h + k):128 * (4 * h + k) + 128], ident)
                        mm.then_inc(e_gt, 1)

                def turn_act(b, h):
                    pe.wait_ge(e_a, 2 * b + h + 1)
                    for k in range(4):
                        mm = pe.transpose(bank(6 + h)[:, 128 * k:128 * k + 128], act_h[:, h, 128 * k:128 * k + 128], ident)
                    mm.then_inc(e_at, 1)

                def down(b, k2):
                    pe.wait_ge(e_dn[k2], 16 * b + 16)
                    for k in (2 * k2, 2 * k2 + 1):
                        for n in range(2):
                            mm = pe.matmul(bank(4 + n), actT[:, k], w_down_e[:, k, 512 * n:512 * n + 512],
                                           start=(k == 0), stop=(k == KD - 1))
                    mm.then_inc(e_use if k2 < 3 else e_y, 1)

                pe.sem_inc(e_use, USES)
                pe.sem_inc(e_y, 1)
                blocks = used(pe)
                pe.wait_ge(p_gm, 2)
                for n in range(NT):
                    r = ROWS[n]
                    out = bank(7)[0:32, 128 * n:128 * n + r] if n < 4 else bank(6)[0:32, 0:r]
                    mm = pe.transpose(out, gmat[0:r, n], ident[0:r, 0:r])
                    if n >= 3:
                        mm.then_inc(p_gt, 1)
                turn_tokens(0)
                pe.wait_ge(p_ge, 2)
                for n in range(NT):
                    for h in range(2):
                        if 2 * n + h >= 4:
                            pe.wait_ge(p_be, 2 * n + h - 3)
                        r = ROWS[n]
                        pe.matmul(bank(2 + (2 * n + h) % 4)[0:r], gmT[0:32, 128 * n:128 * n + r],
                                  b_down[0:32, 512 * h:512 * h + 512], start=True, stop=True).then_inc(p_bd, 1)
                pe.wait_ge(p_be, 2 * NT)
                with pe.Fori(0, NBLK) as b:
                    with pe.If(b < blocks):
                        for h in range(2):
                            if h == 0:
                                pe.wait_ge(e_xT, 2 * b + 2)
                                pe.wait_ge(e_bs, b + 1)
                            for g in range(2):
                                n0 = 1024 * g + 512 * h
                                pe.matmul(bank(2 * h + g), bias_of[0:96], b_parts[0:96, n0:n0 + 512], start=True, stop=False)
                            for k in range(KD):
                                pe.wait_ge(e_in[h][k], 16 * b + 16)
                                for g in range(2):
                                    mm = pe.matmul(bank(2 * h + g), xgT[:, k], w_in_e[:, h, k, g], start=False,
                                                   stop=(k == KD - 1))
                                mm.then_inc(e_use if k < KD - 1 else e_gu, 1)
                        turn_act(b, 0)
                        turn_tokens(b + 1)
                        pe.wait_ge(e_ae, 2 * b + 1)
                        pe.wait_ge(e_yc, b + 1)
                        down(b, 0)
                        turn_act(b, 1)
                        down(b, 1)
                        pe.wait_ge(e_ae, 2 * b + 2)
                        down(b, 2)
                        down(b, 3)
                        pe.nop()
                    with pe.Else():
                        pe.nop()


def kernel(**inputs):
    import concourse.bacc as bacc
    from concourse.bass_utils import run_bass_kernel_spmd

    arrays = lay_out({k: np.asarray(v) for k, v in inputs.items()})
    arrays.update(shape_constants())
    nc = bacc.Bacc("TRN2", target_bir_lowering=False, num_devices=1)
    ins = {k: nc.dram_tensor(f"in_{k}", v.shape, mybir.dt.from_np(v.dtype), kind="ExternalInput").ap()
           for k, v in arrays.items()}
    outs = {k: nc.dram_tensor(f"out_{k}", shape, F32, kind="ExternalOutput").ap() for k, shape in OUTPUTS.items()}
    build_program(nc, ins, outs)
    done = run_bass_kernel_spmd(nc, [{f"in_{k}": v for k, v in arrays.items()}], core_ids=[0])
    return tuple(done.results[0][f"out_{k}"] for k in OUTPUTS)
```
